# Optimizing a Trainium2 kernel written in Bass

```python
import math
import jax
import jax.numpy as jnp
from jax import lax
import numpy as np
import jax, jax.numpy as jnp

D_MODEL = 1024
BATCH = 1
SEQ = 512
DEPTH = 1

N_META = 16
BLOCK = 128
PAD = BLOCK - N_META
WINDOW = 128
A_HEADS = 8
A_KV_HEADS = 2
A_HEAD_DIM = 64
B_HEADS = 8
B_HEAD_DIM = 64
B_Q_RANK = 256
B_KV_RANK = 128
IDX_HEADS = 4
IDX_DIM = 64
TOPK_MAX = 256
N_BUCKETS = 32
MAX_DISTANCE = 128
TOTAL_HEADS = A_HEADS + B_HEADS
D_FF = -(-8 * D_MODEL // (3 * 256)) * 256
EPS = 1e-6
NEG = -1e30

IN_WIDTHS = (A_HEADS * A_HEAD_DIM, A_KV_HEADS * A_HEAD_DIM, A_KV_HEADS * A_HEAD_DIM,
             B_Q_RANK, B_KV_RANK, IDX_HEADS * IDX_DIM, IDX_DIM, IDX_HEADS, 2 * D_MODEL)
IN_SPLITS = tuple(sum(IN_WIDTHS[:i + 1]) for i in range(len(IN_WIDTHS) - 1))
D_IN = sum(IN_WIDTHS)


def rms_norm(x, g):
    xf = x.astype(jnp.float32)
    y = xf * lax.rsqrt(jnp.mean(xf * xf, axis=-1, keepdims=True) + EPS)
    return (y * g.astype(jnp.float32)).astype(x.dtype)

def layer_norm(x, g, b):
    xf = x.astype(jnp.float32)
    mu = jnp.mean(xf, axis=-1, keepdims=True)
    xc = xf - mu
    var = jnp.mean(xc * xc, axis=-1, keepdims=True)
    return (xc * lax.rsqrt(var + EPS) * g.astype(jnp.float32) + b.astype(jnp.float32)).astype(x.dtype)

def t5_bucket(dist):
    max_exact = N_BUCKETS // 2
    d = jnp.maximum(dist, 1).astype(jnp.float32)
    large = max_exact + (jnp.log(d / max_exact) / math.log(MAX_DISTANCE / max_exact)
                         * (N_BUCKETS - max_exact)).astype(jnp.int32)
    large = jnp.minimum(large, N_BUCKETS - 1)
    return jnp.where(dist < max_exact, dist, large)

def sliding_window_sink_attention(q, k, v, sinks, bias_table):
    b, p, _ = q.shape
    nb = p // BLOCK
    grp = A_HEADS // A_KV_HEADS
    qb = q.reshape(b, nb, BLOCK, A_KV_HEADS, grp, A_HEAD_DIM)
    kb = k.reshape(b, nb, BLOCK, A_KV_HEADS, A_HEAD_DIM)
    vb = v.reshape(b, nb, BLOCK, A_KV_HEADS, A_HEAD_DIM)

    def with_prev(t):
        prev = jnp.concatenate([jnp.zeros_like(t[:, :1]), t[:, :-1]], axis=1)
        return jnp.concatenate([prev, t], axis=2)

    kw, vw = with_prev(kb), with_prev(vb)
    s = jnp.einsum('bnqhgd,bnkhd->bnhgqk', qb, kw).astype(jnp.float32) * (A_HEAD_DIM ** -0.5)
    blk = jnp.arange(nb)[:, None] * BLOCK
    qpos = blk + jnp.arange(BLOCK)[None]
    kpos = blk - BLOCK + jnp.arange(2 * BLOCK)[None]
    dist = qpos[:, :, None] - kpos[:, None, :]
    allowed = (dist >= 0) & (dist < WINDOW) & (kpos[:, None, :] >= PAD)
    bias = bias_table[t5_bucket(jnp.maximum(dist, 0))]
    bias = bias.reshape(nb, BLOCK, 2 * BLOCK, A_KV_HEADS, grp).transpose(0, 3, 4, 1, 2)
    s = jnp.where(allowed[None, :, None, None], s + bias.astype(jnp.float32)[None], NEG)
    sink = sinks.astype(jnp.float32).reshape(A_KV_HEADS, grp)[None, None, :, :, None]
    m = jnp.maximum(s.max(axis=-1), sink)
    e = jnp.exp(s - m[..., None])
    pr = e / (e.sum(axis=-1, keepdims=True) + jnp.exp(sink - m)[..., None])
    o = jnp.einsum('bnhgqk,bnkhd->bnqhgd', pr.astype(v.dtype), vw)
    return o.reshape(b, p, A_HEADS * A_HEAD_DIM)

def indexed_sparse_mla(q_abs, c_kv, iq, ik, iw, w_uv, bias_table):
    b, p, _, _ = q_abs.shape
    nb = p // BLOCK
    topk = min(TOPK_MAX, (p - BLOCK) // 4)
    kpos = jnp.arange(p)
    gather = jax.vmap(lambda rows, idx: rows[idx])
    scale = B_HEAD_DIM ** -0.5

    def one_block(i):
        start = i * BLOCK
        qa = lax.dynamic_slice_in_dim(q_abs, start, BLOCK, axis=1)
        qi = lax.dynamic_slice_in_dim(iq, start, BLOCK, axis=1)
        wi = lax.dynamic_slice_in_dim(iw, start, BLOCK, axis=1)
        qpos = start + jnp.arange(BLOCK)
        logits = jnp.einsum('bqhd,bsd->bqhs', qi, ik)
        score = jnp.einsum('bqhs,bqh->bqs', jax.nn.relu(logits).astype(jnp.float32),
                           wi.astype(jnp.float32))
        admissible = (kpos[None, :] <= qpos[:, None]) & (kpos[None, :] >= PAD)
        score = jnp.where(admissible[None], score, -jnp.inf)
        _, sel = lax.top_k(score, topk)
        valid = (sel <= qpos[None, :, None]) & (sel >= PAD)
        c_sel = gather(c_kv, sel)
        s = jnp.einsum('bqhc,bqkc->bqhk', qa, c_sel).astype(jnp.float32) * scale
        bias = bias_table[t5_bucket(jnp.maximum(qpos[None, :, None] - sel, 0))]
        s = jnp.where(valid[:, :, None, :], s + jnp.moveaxis(bias, -1, 2).astype(jnp.float32), NEG)
        pr = jax.nn.softmax(s, axis=-1)
        return jnp.einsum('bqhk,bqkc->bqhc', pr.astype(c_kv.dtype), c_sel)

    lat = lax.map(one_block, jnp.arange(nb))
    lat = lat.transpose(1, 0, 2, 3, 4).reshape(b, p, B_HEADS, B_KV_RANK)
    o = jnp.einsum('bphc,chd->bphd', lat, w_uv)
    return o.reshape(b, p, B_HEADS * B_HEAD_DIM)

def first_inputs(seed: int = 0) -> dict:
    key = jax.random.key(seed)
    ks = jax.random.split(key, 24)
    f32 = jnp.float32

    def dense(k, shape, fan_in):
        return jax.random.normal(k, shape, f32) * (fan_in ** -0.5)

    def gain(k, shape):
        return 1.0 + 0.05 * jax.random.normal(k, shape, f32)

    return {
        "x": jax.random.normal(ks[0], (BATCH, SEQ, D_MODEL), f32),
        "meta_tokens": jax.random.normal(ks[1], (N_META, D_MODEL), f32),
        "attn_norm_g": gain(ks[2], (DEPTH, D_MODEL)),
        "w_in": dense(ks[3], (DEPTH, D_MODEL, D_IN), D_MODEL),
        "b_gates": 0.02 * jax.random.normal(ks[4], (DEPTH, 2 * D_MODEL), f32),
        "q_norm_g": gain(ks[5], (DEPTH, B_Q_RANK)),
        "kv_norm_g": gain(ks[6], (DEPTH, B_KV_RANK)),
        "w_uq": dense(ks[7], (DEPTH, B_Q_RANK, B_HEADS * B_HEAD_DIM), B_Q_RANK),
        "w_uk": dense(ks[8], (DEPTH, B_KV_RANK, B_HEADS, B_HEAD_DIM), B_KV_RANK),
        "w_uv": dense(ks[9], (DEPTH, B_KV_RANK, B_HEADS, B_HEAD_DIM), B_KV_RANK),
        "idx_k_ln_g": gain(ks[10], (DEPTH, IDX_DIM)),
        "idx_k_ln_b": 0.02 * jax.random.normal(ks[11], (DEPTH, IDX_DIM), f32),
        "sinks": 0.5 * jax.random.normal(ks[12], (DEPTH, A_HEADS), f32),
        "rel_bias": 0.2 * jax.random.normal(ks[13], (N_BUCKETS, TOTAL_HEADS), f32),
        "w_branch_a": dense(ks[14], (DEPTH, A_HEADS * A_HEAD_DIM, D_MODEL), A_HEADS * A_HEAD_DIM),
        "w_branch_b": dense(ks[15], (DEPTH, B_HEADS * B_HEAD_DIM, D_MODEL), B_HEADS * B_HEAD_DIM),
        "w_out": dense(ks[16], (DEPTH, D_MODEL, D_MODEL), D_MODEL),
        "ffn_norm_g": gain(ks[17], (DEPTH, D_MODEL)),
        "w_ffn_gate": dense(ks[18], (DEPTH, D_MODEL, D_FF), D_MODEL),
        "w_ffn_up": dense(ks[19], (DEPTH, D_MODEL, D_FF), D_MODEL),
        "w_ffn_down": dense(ks[20], (DEPTH, D_FF, D_MODEL), D_FF),
        "final_norm_g": gain(ks[21], (D_MODEL,)),
    }

def first_block(x, meta_tokens, attn_norm_g, w_in, b_gates, q_norm_g, kv_norm_g, w_uq, w_uk, w_uv,
              idx_k_ln_g, idx_k_ln_b, sinks, rel_bias, w_branch_a, w_branch_b, w_out,
              ffn_norm_g, w_ffn_gate, w_ffn_up, w_ffn_down, final_norm_g):
    b, seq, d = x.shape
    meta = jnp.broadcast_to(meta_tokens.astype(x.dtype)[None], (b, N_META, d))
    h = jnp.concatenate([jnp.zeros((b, PAD, d), x.dtype), meta, x], axis=1)
    p = h.shape[1]
    bias_a = rel_bias[:, :A_HEADS]
    bias_b = rel_bias[:, A_HEADS:]
    for l in range(DEPTH):
        hn = rms_norm(h, attn_norm_g[l])
        proj = hn @ w_in[l]
        aq, ak, av, bq, bkv, iq, ik, iw, gates = jnp.split(proj, IN_SPLITS, axis=-1)
        gates = jax.nn.sigmoid((gates + b_gates[l]).astype(jnp.float32)).astype(h.dtype)
        gate_a, gate_b = jnp.split(gates, 2, axis=-1)
        o_a = sliding_window_sink_attention(aq, ak, av, sinks[l], bias_a)
        q = (rms_norm(bq, q_norm_g[l]) @ w_uq[l]).reshape(b, p, B_HEADS, B_HEAD_DIM)
        c_kv = rms_norm(bkv, kv_norm_g[l])
        q_abs = jnp.einsum('bphd,chd->bphc', q, w_uk[l])
        iq = iq.reshape(b, p, IDX_HEADS, IDX_DIM)
        ik = layer_norm(ik, idx_k_ln_g[l], idx_k_ln_b[l])
        iw = iw * ((IDX_HEADS * IDX_DIM) ** -0.5)
        o_b = indexed_sparse_mla(q_abs, c_kv, iq, ik, iw, w_uv[l], bias_b)
        mixed = gate_a * (o_a @ w_branch_a[l]) + gate_b * (o_b @ w_branch_b[l])
        h = h + mixed @ w_out[l]
        hn = rms_norm(h, ffn_norm_g[l])
        h = h + (jax.nn.silu(hn @ w_ffn_gate[l]) * (hn @ w_ffn_up[l])) @ w_ffn_down[l]
    y = rms_norm(h, final_norm_g)
    return y[:, PAD + N_META:]


HEAD_DIM = 64
A_HEADS_2 = D_MODEL // 256
A_V_DIM = 2 * HEAD_DIM
A_WIDTH = A_HEADS_2 * A_V_DIM
B_HEADS_2 = D_MODEL // 128
B_KV_HEADS = max(1, B_HEADS_2 // 4)
B_GROUP = B_HEADS_2 // B_KV_HEADS
B_WIDTH = B_HEADS_2 * HEAD_DIM
D_FF_2 = -(-8 * D_MODEL // (3 * 256)) * 256
QA_W = A_HEADS_2 * 2 * HEAD_DIM
KA_W = A_HEADS_2 * 2 * HEAD_DIM
VA_W = A_WIDTH
QB_W = B_WIDTH
KB_W = B_KV_HEADS * HEAD_DIM
VB_W = B_KV_HEADS * HEAD_DIM
GATE_W = D_MODEL
PROJ_W = QA_W + KA_W + VA_W + QB_W + KB_W + VB_W + 2 * GATE_W


def rms_norm_2(x, g):
    xf = x.astype(jnp.float32)
    y = xf * lax.rsqrt(jnp.mean(xf * xf, axis=-1, keepdims=True) + EPS)
    return (y * g.astype(jnp.float32)).astype(x.dtype)

def alibi_slopes(n):
    return jnp.asarray(2.0 ** (-8.0 * np.arange(1, n + 1) / n), dtype=jnp.float32)

def lambda_init_for(layer):
    return 0.8 - 0.6 * math.exp(-0.3 * layer)

def diff_attn_rows(q1, q2, k1, k2, v, qpos, kpos, key_real, slopes, lam):
    scale = HEAD_DIM ** -0.5
    dist = jnp.abs(qpos[:, None] - kpos[None, :]).astype(jnp.float32) * key_real[None, :]
    bias = -slopes[:, None, None] * dist[None]
    s1 = jnp.einsum('bqhd,bkhd->bhqk', q1, k1).astype(jnp.float32) * scale + bias
    s2 = jnp.einsum('bqhd,bkhd->bhqk', q2, k2).astype(jnp.float32) * scale + bias
    attn = jax.nn.softmax(s1, axis=-1) - lam * jax.nn.softmax(s2, axis=-1)
    return jnp.einsum('bhqk,bkhe->bqhe', attn.astype(v.dtype), v)

def differential_attention(q, k, v, lam_q1, lam_k1, lam_q2, lam_k2, subln_g, lambda_init):
    Bn, L = q.shape[0], q.shape[1]
    S = L - N_META
    nb = S // BLOCK
    pos = jnp.arange(L)
    key_real = (pos >= N_META).astype(jnp.float32)
    slopes = alibi_slopes(A_HEADS_2)
    lam = (jnp.exp(jnp.sum(lam_q1.astype(jnp.float32) * lam_k1.astype(jnp.float32)))
           - jnp.exp(jnp.sum(lam_q2.astype(jnp.float32) * lam_k2.astype(jnp.float32)))
           + lambda_init)
    q1, q2 = q[..., 0, :], q[..., 1, :]
    k1, k2 = k[..., 0, :], k[..., 1, :]

    def attend(a, b, p):
        return diff_attn_rows(a, b, k1, k2, v, p, pos, key_real, slopes, lam)

    y_meta = attend(q1[:, :N_META], q2[:, :N_META], pos[:N_META])

    def to_blocks(t):
        return t[:, N_META:].reshape(Bn, nb, BLOCK, *t.shape[2:]).swapaxes(0, 1)

    y_real = lax.map(lambda a: attend(*a),
                     (to_blocks(q1), to_blocks(q2), pos[N_META:].reshape(nb, BLOCK)))
    y_real = y_real.swapaxes(0, 1).reshape(Bn, S, A_HEADS_2, A_V_DIM)
    y = jnp.concatenate([y_meta, y_real], axis=1)
    y = rms_norm_2(y, subln_g) * (1.0 - lambda_init)
    return y.reshape(Bn, L, A_WIDTH)

def window_attn_blocks(q, k, v, qpos, kpos, kvalid, kreal, slopes, sink):
    scale = HEAD_DIM ** -0.5
    dt = jnp.abs(qpos[:, :, None] - kpos[:, None, :])
    visible = kvalid[:, None, :] & ((~kreal[:, None, :]) | (dt <= WINDOW))
    dist = jnp.where(kreal[:, None, :], dt, 0).astype(jnp.float32)
    bias = -slopes[None, :, :, None, None] * dist[:, None, None]
    s = jnp.einsum('bnqgrd,bnkgd->bngrqk', q, k).astype(jnp.float32) * scale + bias
    s = jnp.where(visible[None, :, None, None], s, -jnp.inf)
    sink_b = sink.astype(jnp.float32)[None, None, :, :, None, None]
    m = jnp.maximum(jnp.max(s, axis=-1, keepdims=True), sink_b)
    p = jnp.exp(s - m)
    denom = jnp.sum(p, axis=-1, keepdims=True) + jnp.exp(sink_b - m)
    return jnp.einsum('bngrqk,bnkgd->bnqgrd', (p / denom).astype(v.dtype), v)

def windowed_gqa(q, k, v, sink):
    Bn, L = q.shape[0], q.shape[1]
    S = L - N_META
    nb = S // BLOCK
    G, d = B_KV_HEADS, HEAD_DIM
    slopes = alibi_slopes(B_HEADS_2).reshape(B_KV_HEADS, B_GROUP)

    def band(t):
        tp = jnp.pad(t[:, N_META:], ((0, 0), (BLOCK, BLOCK), (0, 0), (0, 0)))
        tp = tp.reshape(Bn, nb + 2, BLOCK, G, d)
        win = jnp.concatenate([tp[:, j:j + nb] for j in range(3)], axis=2)
        meta = jnp.broadcast_to(t[:, None, :N_META], (Bn, nb, N_META, G, d))
        return jnp.concatenate([meta, win], axis=2)

    blk = jnp.arange(nb)[:, None]
    win_idx = (blk - 1) * BLOCK + jnp.arange(3 * BLOCK)[None, :]
    meta_pos = jnp.broadcast_to(jnp.arange(N_META)[None, :], (nb, N_META))
    kpos = jnp.concatenate([meta_pos, N_META + win_idx], axis=1)
    kvalid = jnp.concatenate([jnp.ones((nb, N_META), bool),
                              (win_idx >= 0) & (win_idx < S)], axis=1)
    kreal = jnp.concatenate([jnp.zeros((nb, N_META), bool),
                             jnp.ones((nb, 3 * BLOCK), bool)], axis=1)
    qpos = N_META + jnp.arange(S).reshape(nb, BLOCK)
    q_real = q[:, N_META:].reshape(Bn, nb, BLOCK, G, B_GROUP, d)
    y_real = window_attn_blocks(q_real, band(k), band(v), qpos, kpos, kvalid, kreal, slopes, sink)
    y_real = y_real.reshape(Bn, S, B_WIDTH)

    tk = N_META + BLOCK
    kpos_m = jnp.arange(tk)[None, :]
    y_meta = window_attn_blocks(q[:, None, :N_META], k[:, None, :tk], v[:, None, :tk],
                                jnp.arange(N_META)[None, :], kpos_m,
                                jnp.ones((1, tk), bool), kpos_m >= N_META, slopes, sink)
    y_meta = y_meta.reshape(Bn, N_META, B_WIDTH)
    return jnp.concatenate([y_meta, y_real], axis=1)

def mixer_block(h, w_in, lq1, lk1, lq2, lk2, subln_g, sink, w_ba, w_bb, w_o, lambda_init):
    Bn, L = h.shape[0], h.shape[1]
    proj = h @ w_in
    o = 0
    qa = proj[..., o:o + QA_W]; o += QA_W
    ka = proj[..., o:o + KA_W]; o += KA_W
    va = proj[..., o:o + VA_W]; o += VA_W
    qb = proj[..., o:o + QB_W]; o += QB_W
    kb = proj[..., o:o + KB_W]; o += KB_W
    vb = proj[..., o:o + VB_W]; o += VB_W
    ga = proj[..., o:o + GATE_W]; o += GATE_W
    gb = proj[..., o:o + GATE_W]
    y_a = differential_attention(qa.reshape(Bn, L, A_HEADS_2, 2, HEAD_DIM),
                                 ka.reshape(Bn, L, A_HEADS_2, 2, HEAD_DIM),
                                 va.reshape(Bn, L, A_HEADS_2, A_V_DIM),
                                 lq1, lk1, lq2, lk2, subln_g, lambda_init)
    y_b = windowed_gqa(qb.reshape(Bn, L, B_KV_HEADS, B_GROUP, HEAD_DIM),
                       kb.reshape(Bn, L, B_KV_HEADS, HEAD_DIM),
                       vb.reshape(Bn, L, B_KV_HEADS, HEAD_DIM),
                       sink.reshape(B_KV_HEADS, B_GROUP))
    merged = jax.nn.sigmoid(ga) * (y_a @ w_ba) + jax.nn.sigmoid(gb) * (y_b @ w_bb)
    return merged @ w_o

def swiglu(h, w_gate, w_up, w_down):
    return (jax.nn.silu(h @ w_gate) * (h @ w_up)) @ w_down

def second_inputs(seed: int = 0) -> dict:
    key = jax.random.key(seed)
    ks = jax.random.split(key, 20)

    def w(k, shape, fan_in):
        return jax.random.normal(k, shape, jnp.float32) * (fan_in ** -0.5)

    def gain(k, shape):
        return 1.0 + 0.02 * jax.random.normal(k, shape, jnp.float32)

    return {
        "x": jax.random.normal(ks[0], (BATCH, SEQ, D_MODEL), jnp.float32),
        "meta_tokens": jax.random.normal(ks[1], (N_META, D_MODEL), jnp.float32),
        "norm_mix": gain(ks[2], (DEPTH, D_MODEL)),
        "w_in": w(ks[3], (DEPTH, D_MODEL, PROJ_W), D_MODEL),
        "lambda_q1": 0.1 * jax.random.normal(ks[4], (DEPTH, HEAD_DIM), jnp.float32),
        "lambda_k1": 0.1 * jax.random.normal(ks[5], (DEPTH, HEAD_DIM), jnp.float32),
        "lambda_q2": 0.1 * jax.random.normal(ks[6], (DEPTH, HEAD_DIM), jnp.float32),
        "lambda_k2": 0.1 * jax.random.normal(ks[7], (DEPTH, HEAD_DIM), jnp.float32),
        "subln_gain": gain(ks[8], (DEPTH, A_V_DIM)),
        "sink_logits": 0.5 * jax.random.normal(ks[9], (DEPTH, B_HEADS_2), jnp.float32),
        "w_branch_a": w(ks[10], (DEPTH, A_WIDTH, D_MODEL), A_WIDTH),
        "w_branch_b": w(ks[11], (DEPTH, B_WIDTH, D_MODEL), B_WIDTH),
        "w_out": w(ks[12], (DEPTH, D_MODEL, D_MODEL), D_MODEL),
        "norm_ffn": gain(ks[13], (DEPTH, D_MODEL)),
        "w_ff_gate": w(ks[14], (DEPTH, D_MODEL, D_FF_2), D_MODEL),
        "w_ff_up": w(ks[15], (DEPTH, D_MODEL, D_FF_2), D_MODEL),
        "w_ff_down": w(ks[16], (DEPTH, D_FF_2, D_MODEL), D_FF_2),
        "norm_final": gain(ks[17], (D_MODEL,)),
    }

def second_block(x, meta_tokens, norm_mix, w_in, lambda_q1, lambda_k1, lambda_q2, lambda_k2,
              subln_gain, sink_logits, w_branch_a, w_branch_b, w_out, norm_ffn,
              w_ff_gate, w_ff_up, w_ff_down, norm_final):
    Bn = x.shape[0]
    meta = jnp.broadcast_to(meta_tokens.astype(x.dtype)[None], (Bn, N_META, x.shape[-1]))
    h = jnp.concatenate([meta, x], axis=1)
    for layer in range(DEPTH):
        h = h + mixer_block(rms_norm_2(h, norm_mix[layer]), w_in[layer],
                            lambda_q1[layer], lambda_k1[layer], lambda_q2[layer], lambda_k2[layer],
                            subln_gain[layer], sink_logits[layer],
                            w_branch_a[layer], w_branch_b[layer], w_out[layer],
                            lambda_init_for(layer))
        h = h + swiglu(rms_norm_2(h, norm_ffn[layer]), w_ff_gate[layer], w_ff_up[layer], w_ff_down[layer])
    return rms_norm_2(h, norm_final)[:, N_META:]


def setup_inputs(seed=0):
    out = dict(first_inputs(seed))
    for name, value in second_inputs(seed + 1).items():
        if name != "x":
            out[name + "_2"] = value
    return out


def reference(
    x, meta_tokens, attn_norm_g, w_in, b_gates, q_norm_g, kv_norm_g, w_uq, w_uk, w_uv,
    idx_k_ln_g, idx_k_ln_b, sinks, rel_bias, w_branch_a, w_branch_b, w_out, ffn_norm_g,
    w_ffn_gate, w_ffn_up, w_ffn_down, final_norm_g, meta_tokens_2, norm_mix_2, w_in_2,
    lambda_q1_2, lambda_k1_2, lambda_q2_2, lambda_k2_2, subln_gain_2, sink_logits_2,
    w_branch_a_2, w_branch_b_2, w_out_2, norm_ffn_2, w_ff_gate_2, w_ff_up_2, w_ff_down_2,
    norm_final_2,
):
    x = first_block(
        x, meta_tokens, attn_norm_g, w_in, b_gates, q_norm_g, kv_norm_g, w_uq, w_uk, w_uv,
        idx_k_ln_g, idx_k_ln_b, sinks, rel_bias, w_branch_a, w_branch_b, w_out, ffn_norm_g,
        w_ffn_gate, w_ffn_up, w_ffn_down, final_norm_g,
    )
    return second_block(
        x, meta_tokens_2, norm_mix_2, w_in_2, lambda_q1_2, lambda_k1_2, lambda_q2_2,
        lambda_k2_2, subln_gain_2, sink_logits_2, w_branch_a_2, w_branch_b_2, w_out_2,
        norm_ffn_2, w_ff_gate_2, w_ff_up_2, w_ff_down_2, norm_final_2,
    )


_drawn_inputs = setup_inputs


def setup_inputs(seed=0):
    import zlib

    import numpy as np

    out = dict(_drawn_inputs(seed))
    spreads = {}
    factors = {'b_gates': 8.0,
     'q_norm_g': 8.0,
     'kv_norm_g': 4.826,
     'idx_k_ln_g': 3.27,
     'idx_k_ln_b': 5.704,
     'sinks': 8.0,
     'norm_mix_2': 3.536,
     'lambda_q1_2': 8.0,
     'lambda_k1_2': 3.091,
     'subln_gain_2': 6.679,
     'sink_logits_2': 64.0,
     'norm_ffn_2': 4.061,
     'norm_final_2': 8.052,
     'lambda_q2_2': 8.0,
     'lambda_k2_2': 8.0}
    for name, (base, spread) in spreads.items():
        noise = np.random.default_rng([zlib.crc32(name.encode()), seed]).standard_normal(out[name].shape)
        drawn = base * np.exp(spread * noise) if base else spread * noise
        out[name] = jnp.asarray(drawn.astype(out[name].dtype))
    for name, factor in factors.items():
        out[name] = (out[name] * factor).astype(out[name].dtype)
    return out
```

```python
from contextlib import ExitStack

import numpy as np

import concourse.bass as bass
from concourse import mybir

F32 = mybir.dt.float32
F32R = mybir.dt.float32r
BF16 = mybir.dt.bfloat16
I32 = mybir.dt.int32
ACT = mybir.ActivationFunctionType
ALU = mybir.AluOpType
AX_X = mybir.AxisListType.X

P = 128
D = 1024
KD = D // P
SEQ = 512
NB = SEQ // P
META = 16
NKEY = META + SEQ
MC = NB
FF = 2816
NFH = FF // P // 2
HD = 64
NH = 8
EPS = 1e-6
NEG = -1e30
TAKEN = -3e38
TOPK = 128
BUCKETS = 32
QSCALE = HD ** -0.5
LAMBDA0 = 0.8 - 0.6
RSQRT_SEED = float(0x5F3759DF)

NEAR = 2 * P
LEN_A = NEAR + P - 1
LEN_B = NKEY + P - 1
WIN2 = 3 * P
DIST = 7 * P


def bucket(dist):
    exact = BUCKETS // 2
    d = np.maximum(dist, 1).astype(np.float32)
    span = np.float32(np.log(128 / exact))
    large = exact + (np.log(d / np.float32(exact)) / span * np.float32(BUCKETS - exact)).astype(np.int32)
    return np.where(dist < exact, dist, np.minimum(large, BUCKETS - 1))


def bucket_rows():
    out = []
    for length, far in ((LEN_A, P), (LEN_B, 1 << 20)):
        dist = (length - P) - np.arange(length)
        dead = (dist < 0) | (dist >= far)
        hot = np.zeros((BUCKETS + 1, length), np.float32)
        live = np.flatnonzero(~dead)
        hot[bucket(dist[live]), live] = 1.0
        hot[BUCKETS, dead] = 1.0
        out.append(hot)
    return out


PHASES = [("kv1", 4, KD, 1), ("bq1", 2, KD, 1), ("iq1", 2, KD, 1), ("aq1", 4, KD, 2), ("uq1", 4, 2, 1),
          ("gates1", 2 * KD, KD, 1), ("br1", 2 * KD, 4, 1), ("out1", KD, KD, 1),
          ("gu1a", 2 * NFH, KD, 1), ("dn1a", KD, NFH, 1), ("gu1b", 2 * NFH, KD, 1), ("dn1b", KD, NFH, 1),
          ("kv2", 10, KD, 1), ("qa2", 4, KD, 1), ("qb2", 4, KD, 2),
          ("gates2", 2 * KD, KD, 1), ("br2", 2 * KD, 4, 1), ("out2", KD, KD, 1),
          ("gu2a", 2 * NFH, KD, 1), ("dn2a", KD, NFH, 1), ("gu2b", 2 * NFH, KD, 1), ("dn2b", KD, NFH, 1)]
KC = {n: kc for n, _, kc, _ in PHASES}
PAIRS = {n: s // 2 for n, s, _, _ in PHASES}
LOADS = {n: d for n, _, _, d in PHASES}
PAIR0, LOAD0, AFTER = {}, {}, {}
_pairs = _loads = 0
for _i, (_n, _s, _kc, _d) in enumerate(PHASES):
    PAIR0[_n], LOAD0[_n] = _pairs, _loads
    AFTER[_n] = PHASES[_i + 1][0] if _i + 1 < len(PHASES) else None
    _pairs += _s // 2
    _loads += _s // 2 * _d

POOL_LOW = ("gates1", "br1", "gates2", "br2")

ROWS = [("attn_norm_g", KD), ("ffn_norm_g", KD), ("final_norm_g", KD), ("norm_mix_2", KD), ("norm_ffn_2", KD),
        ("norm_final_2", KD), ("b_gates", 2 * KD), ("q_norm_g", 2), ("subln_gain_2", 1)]
ROW = {}
NROWS = 0
for _n, _s in ROWS:
    ROW[_n] = NROWS
    NROWS += _s


def squares_cleared(norm):
    return norm * (KD + 1) + 1


class Tally:

    def __init__(self, eng, sem):
        self.eng, self.sem, self.n, self.off = eng, sem, 0, 0

    def link(self, ins):
        ins.then_inc(self.sem, 1)
        self.n += 1
        self.eng.wait_ge(self.sem, self.off + self.n)

    def enter(self, i, per):
        self.off, self.start, self.per = i * per, self.n, per

    def leave(self, count):
        assert self.n - self.start == self.per, (self.n - self.start, self.per)
        self.off, self.n = 0, self.start + self.per * count


def window1_units():
    for i in range(NB):
        for h in range(NH):
            if i == 0:
                yield i, h, 0, META + P, [(MC, 0, META), (0, META, P)]
            else:
                yield i, h, META + P * (i - 1), NEAR, [(i - 1, 0, P), (i, P, P)]


def latent_units():
    for i in range(NB):
        for h in range(NH):
            yield i, h, META + P * (i + 1), [(MC, 0, META)] + [(c, META + P * c, P) for c in range(i + 1)]


def window2_units():
    for i in range(NB):
        lo, hi = max(i - 1, 0), min(i + 1, NB - 1)
        n = hi - lo + 1
        w, m, bias = (0, n * P, META + P) if i == 0 else (META, 0, 0)
        for h in range(NH):
            yield i, h, lo, n * P, w, m, bias, [(MC, m, META)] + [(lo + c, w + P * c, P) for c in range(n)]


def two_banks(ap, width):
    return ap[:, :, 0:width // 2] if width > 512 else ap[:, 0, 0:width]


def as_halves(ap, width):
    return ap.rearrange("p (a b) -> p a b", a=2) if width > 512 else ap


def build(nc, t, out):
    with ExitStack() as ctx:
        def sem(name):
            return ctx.enter_context(nc.semaphore(name))

        base = -(-nc.sbuf_base // 32) * 32
        top = [base]
        size = {F32: 4, F32R: 4, BF16: 2, I32: 4}

        def at(name, shape, offset, dt=F32):
            n = int(np.prod(shape[1:])) * size[dt]
            assert offset + n <= nc.sbuf_usable_end, (name, offset + n - nc.sbuf_usable_end)
            return nc.alloc_sbuf_tensor_at(name, shape, dt, offset=offset), -(-(offset + n) // 32) * 32

        def keep(name, shape, dt=F32):
            tensor, top[0] = at(name, shape, top[0], dt)
            return tensor

        hT = keep("hT", [P, KD, SEQ])
        stage = keep("stage", [P, 2, NFH * P])
        wh = keep("wh", [P, 2, NFH * P], F32R)
        wl = keep("wl", [P, 2, NFH * P], F32R)
        R = keep("R", [P, SEQ])
        tmp = keep("tmp", [P, 2, SEQ])
        ident = keep("ident", [P, P])
        identb = keep("identb", [P, P], BF16)
        ones = keep("ones", [P, P])
        gvec = keep("gvec", [P, NROWS])
        bhalf = keep("bhalf", [P, 2 * KD])
        kvg = keep("kvg", [P, P])
        ikg = keep("ikg", [P, 2, HD])
        sinkb = keep("sinkb", [P, 2, NH])
        tab = keep("tab", [BUCKETS + 1, 2 * NH])
        wuv = keep("wuv", [P, NH * HD])
        wukT = keep("wukT", [P, 4, P])
        metaT = keep("metaT", [P, 2, KD, META])
        iwn = keep("iwn", [P, NB, 4])
        mx = keep("mx", [P, 2 * NB * NH])
        negm = keep("negm", [P, 2 * NB * NH])
        rsum = keep("rsum", [P, 2 * NB * NH])
        st = keep("st", [P, 12, NH])
        rst = keep("rst", [P, 16])
        rsti = keep("rsti", [P, 16], I32)
        rs = keep("rs", [P, 16])
        lam = keep("lam", [P, 4])
        neglam = keep("neglam", [P, 1])

        gate0 = top[0]
        gate = keep("gate", [P, 2 * KD, SEQ])
        xin, o = at("xin", [P, NB, D], gate0)
        metain, o = at("metain", [META, 2, D], o)
        junk, o = at("junk", [P, D], o)
        wuk, o = at("wuk", [P, NH * HD], o)
        rows, o = at("rows", [NROWS, P], o)
        lam4, o = at("lam4", [P, 4, HD], o)
        lamj, o = at("lamj", [P, HD], o)
        assert o <= top[0]

        hn0 = top[0]
        hn = keep("hn", [P, 2, KD, SEQ], F32R)
        oA, o = at("oA", [P, 2, 4, SEQ], hn0, F32R)
        oB, _ = at("oB", [P, 2, 4, SEQ], o, F32R)
        W3, o = at("W3", [P, 3, NKEY], o)
        PT, o = at("PT", [P, 2, (NB + 1) * P], o)
        lat, o = at("lat", [P, 2, P], o)
        assert o <= top[0]
        W6, o = at("W6", [P, 3, 2, NKEY], gate0)
        PT2, o = at("PT2", [P, 2, (NB + 1) * P], o)
        assert o <= hn0

        ar0 = top[0]
        aqT, o = at("aqT", [P, 4, SEQ], ar0)
        biasA, o = at("biasA", [P, NH, NEAR], o)
        qabs, _ = at("qabs", [P, NH, SEQ], ar0)
        biasB, o = at("biasB", [P, NH, NKEY], o)
        akT, o = at("akT", [P, NKEY], o)
        avn, o = at("avn", [P, NB + 1, P], o)
        cT, o = at("cT", [P, NKEY], o)
        cn, o = at("cn", [P, NB + 1, P], o)
        o1 = o
        bqT, o = at("bqT", [P, 2, SEQ], o)
        bqg, o = at("bqg", [P, 2, 2, SEQ], o, F32R)
        acc, o = at("acc", [P, NB, NKEY], o1)
        W3a, o = at("W3a", [P, 3, NEAR], o)
        o2 = max(o, o1 + 3 * 4 * SEQ * 2)
        bkvT, o = at("bkvT", [P, NKEY], o2)
        ikwT, o = at("ikwT", [P, NKEY], o)
        avT, o = at("avT", [P, NKEY], o)
        ikn, o = at("ikn", [P, NB + 1, P], o)
        ikx, o = at("ikx", [P, NB + 1, HD], o)
        iqT, o3 = at("iqT", [P, 2, SEQ], o2)
        ikT, o3 = at("ikT", [P, NKEY], o3)
        relu, o3 = at("relu", [P, 2, NKEY], o3)
        on, o4 = at("on", [P, NB, SEQ], o2)
        PTa, o4 = at("PTa", [P, 2, NEAR + P], o4)
        o = max(o, o3)
        causal, o = at("causal", [P, NKEY], o)
        assert o4 <= o
        tail = o
        qT, o = at("qT", [P, 4, SEQ], tail)
        selm, _ = at("selm", [P, NB, NKEY], o, BF16)
        diag, o6 = at("diag", [P, NB, P], o)
        sq, o6 = at("sq", [P, SEQ], o6)
        sqacc, _ = at("sqacc", [P, 2, SEQ], tail)
        hotA, o5 = at("hotA", [BUCKETS + 1, LEN_A], tail)
        hotB, o5 = at("hotB", [BUCKETS + 1, LEN_B], o5)
        fA, o5 = at("fA", [NH, LEN_A], o5)
        assert o5 <= o
        fB, _ = at("fB", [NH, LEN_B], o1)
        qaT, o = at("qaT", [P, 4, SEQ], ar0)
        kaT, o = at("kaT", [P, 4, NKEY], o)
        kbT, o = at("kbT", [P, NKEY], o)
        yw, _ = at("yw", [P, NB, SEQ], o)
        van, o = at("van", [P, NB + 1, SEQ], o)
        vbn, o = at("vbn", [P, NB + 1, P], o)
        qbT, o = at("qbT", [P, 4, SEQ], o)
        dist, o = at("dist", [P, DIST], o)
        biasD, o = at("biasD", [P, 4, NKEY], o)
        o1 = o
        biasW, o = at("biasW", [P, NH, META + WIN2 + META], o1)
        vaT, o2 = at("vaT", [P, 4, NKEY], o1)
        vbT, o2 = at("vbT", [P, NKEY], o2)
        assert max(o, o2) <= tail
        yn, _ = at("yn", [P, NB, SEQ], tail)
        W3b, o = at("W3b", [P, 3, META + WIN2], ar0)
        PTb, o = at("PTb", [P, 2, WIN2 + P], o)
        mix, o = at("mix", [P, 2, KD, SEQ], ar0, F32R)
        mix32, _ = at("mix32", [P, 3, SEQ], o)
        hid, o = at("hid", [P, 2, NFH, SEQ], ar0, F32R)
        ft, o = at("ft", [P, 5, SEQ], o)
        assert o <= tail
        hgf, _ = at("hgf", [P, KD, SEQ], hn0)
        yout, _ = at("yout", [P, 2, D], gate0)

        psL = ctx.enter_context(nc.psum_tensor("psL", [P, 2, 512], F32))
        psS = ctx.enter_context(nc.psum_tensor("psS", [P, 4, 512], F32))
        psT = ctx.enter_context(nc.psum_tensor("psT", [P, 2, 512], F32))

        fA_dram = nc.dram_tensor("bias_by_distance_A", [NH, P, LEN_A + 1], F32).ap()
        fB_dram = nc.dram_tensor("bias_by_distance_B", [NH, P, LEN_B + 1], F32).ap()

        w_in = [sem(f"w_in{b}") for b in range(2)]
        hi = [sem(f"hi{b}") for b in range(2)]
        lo = [sem(f"lo{b}") for b in range(2)]
        mm = [sem(f"mm{b}") for b in range(2)]
        ev = [sem(f"ev{b}") for b in range(2)]
        dve_own = sem("dve_own")
        pool_own = sem("pool_own")
        x_in, meta_in, rows_in, tab_in, vec_in, wuk_in, lam_in, lam_sum = [
            sem(n) for n in "x_in meta_in rows_in tab_in vec_in wuk_in lam_in lam_sum".split()]
        consts, zeros, gvec_t, gvec_ok, x_t, x_taken, xhi, xlo, x_sq, meta_sq, meta_ok, meta_t, metaT_ok = [
            sem(n) for n in "consts zeros gvec_t gvec_ok x_t x_taken xhi xlo x_sq meta_sq meta_ok meta_t metaT_ok".split()]
        f_mm, fA_ok, f_out, bias_in = [sem(n) for n in "f_mm fA_ok f_out bias_in".split()]
        diag_ok, bcast, R_ok, ssq_in, ssq_mm = [
            sem(n) for n in "diag_ok bcast R_ok ssq_in ssq_mm".split()]
        nat_t, nat_taken, nat_ok, key_t, key_taken, bqhi, bqlo = [
            sem(n) for n in "nat_t nat_taken nat_ok key_t key_taken bqhi bqlo".split()]
        lg_mm, lg_taken, lg_used = [sem(n) for n in "lg_mm lg_taken lg_used".split()]
        sel_ok, qabs_mm, qabs_ok = [sem(n) for n in "sel_ok qabs_mm qabs_ok".split()]
        th_ok = [sem(f"th_ok{b}") for b in range(2)]
        ph = {}
        for n in ("w1", "la", "df", "w2"):
            ph[n] = {k: sem(f"{n}_{k}") for k in "s neg p pt ptx pv lat o es on".split()}
        oT_mm, oT_taken, o_hi, o_lo = [sem(n) for n in "oT_mm oT_taken o_hi o_lo".split()]
        mix_ok, mix_hi, mix_lo, t_ok, hid_ok, hid_hi, hid_lo = [
            sem(n) for n in "mix_ok mix_hi mix_lo t_ok hid_ok hid_hi hid_lo".split()]
        h_sq, h_sq2, x2_sq, h_gain, hg_hi, hg_lo = [sem(n) for n in "h_sq h_sq2 x2_sq h_gain hg_hi hg_lo".split()]
        biasD_ok, biasW_ok, dist_ok, df_sum, y_sq, lam_e = [
            sem(n) for n in "biasD_ok biasW_ok dist_ok df_sum y_sq lam_e".split()]
        fin_gain, fin_t, fin_ok, fin_out = sem("fin_gain"), sem("fin_t"), sem("fin_ok"), [sem("fin_out0"), sem("fin_out1")]

        block = ctx.enter_context(nc.Block())

        def by_rows(w, k0=0, kc=None):
            v = w.rearrange("(k p) n -> p k n", p=P)
            return v if kc is None else v[:, k0:k0 + kc, :]

        win1, win2 = by_rows(t["w_in"][0]), by_rows(t["w_in_2"][0])

        @block.sync
        def _(sp):
            def load(name, i, b, src, col, piece=0, width=P):
                kc = KC[name]
                slot = stage[:, b, 0:kc * P].rearrange("p (k n) -> p k n", k=kc)
                if piece == 0 and not (name == "kv1" and isinstance(i, int) and i == 0):
                    sp.wait_ge(lo[b], PAIR0[name] + i)
                    if name in ("kv1", "bq1", "kv2", "qa2"):
                        sp.wait_ge(mm[b], PAIR0[name] + i)
                sp.dma_start(slot[:, :, piece:piece + width], src[:, :, bass.ds(col, width)]).then_inc(w_in[b], 16)

            for n in range(NB):
                sp.dma_start(xin[:, n, :], t["x"][0, n * P:(n + 1) * P, :]).then_inc(x_in, 16)
            for n, col in enumerate((1024, 1408, 512, 640)):
                load("kv1", n // 2, n % 2, win1, col)
            for n in range(2):
                load("bq1", 0, n, win1, 768 + n * P)
            for n in range(2):
                load("iq1", 0, n, win1, 1152 + n * P)
            for n in range(4):
                for half in range(2):
                    load("aq1", n // 2, n % 2, win1, (n + 4 * half) * HD, half * HD, HD)
            for n in range(4):
                load("uq1", n // 2, n % 2, by_rows(t["w_uq"][0]), n * P)

            def layer_rest(l, win, gates_at, wa, wb, wo, wg, wu, wd):
                with sp.Fori(0, PAIRS[f"gates{l}"]) as i:
                    for b in range(2):
                        load(f"gates{l}", i, b, win, i * (2 * P) + (gates_at + b * P))
                with sp.Fori(0, PAIRS[f"br{l}"]) as i:
                    load(f"br{l}", i, 0, by_rows(wa), i * P)
                    load(f"br{l}", i, 1, by_rows(wb), i * P)
                with sp.Fori(0, PAIRS[f"out{l}"]) as i:
                    for b in range(2):
                        load(f"out{l}", i, b, by_rows(wo), i * (2 * P) + b * P)
                for half, ab in enumerate("ab"):
                    with sp.Fori(0, PAIRS[f"gu{l}{ab}"]) as i:
                        load(f"gu{l}{ab}", i, 0, by_rows(wg), i * P + half * NFH * P)
                        load(f"gu{l}{ab}", i, 1, by_rows(wu), i * P + half * NFH * P)
                    with sp.Fori(0, PAIRS[f"dn{l}{ab}"]) as i:
                        for b in range(2):
                            load(f"dn{l}{ab}", i, b, by_rows(wd, half * NFH, NFH), i * (2 * P) + b * P)

            layer_rest(1, win1, 1476, t["w_branch_a"][0], t["w_branch_b"][0], t["w_out"][0],
                       t["w_ffn_gate"][0], t["w_ffn_up"][0], t["w_ffn_down"][0])
            with sp.Fori(0, PAIRS["kv2"] - 1) as i:
                for b in range(2):
                    load("kv2", i, b, win2, i * (2 * P) + (512 + b * P))
            for b in range(2):
                load("kv2", PAIRS["kv2"] - 1, b, win2, 2048 + b * P)
            with sp.Fori(0, PAIRS["qa2"]) as i:
                for b in range(2):
                    load("qa2", i, b, win2, i * (2 * P) + b * P)
            for n in range(4):
                for half in range(2):
                    load("qb2", n // 2, n % 2, win2, 1536 + (n + 4 * half) * HD, half * HD, HD)
            layer_rest(2, win2, 2304, t["w_branch_a_2"][0], t["w_branch_b_2"][0], t["w_out_2"][0],
                       t["w_ff_gate_2"][0], t["w_ff_up_2"][0], t["w_ff_down_2"][0])
            for n in range(NB):
                sp.wait_ge(fin_ok, 2 * n + 2)
                sp.dma_start(out[0, n * P:(n + 1) * P, :], yout[:, n % 2, :]).then_inc(fin_out[n % 2], 16)
            sp.wait_ge(fin_out[0], 32)
            sp.wait_ge(fin_out[1], 32)

        @block.gpsimd
        def _(pool):
            own = Tally(pool, pool_own)
            own.link(pool.memset(ident[:], 0.0))
            own.link(pool.affine_select(out=ident[:], in_=ident[:], compare_op=ALU.not_equal, fill=1.0, base=0,
                                        pattern=[[-1, P]], channel_multiplier=1))
            own.link(pool.tensor_copy(identb[:], ident[:]))
            own.link(pool.memset(tab[BUCKETS:BUCKETS + 1, :], NEG))
            pool.memset(ones[:], 1.0).then_inc(consts, 1)
            for l, name in enumerate(("sinks", "sink_logits_2")):
                src = t[name]
                pool.dma_start(sinkb[:, l, :], bass.AP(tensor=src.tensor, offset=0, ap=[[0, P], [1, NH]])).then_inc(vec_in, 16)
            pool.dma_start(kvg[:], bass.AP(tensor=t["kv_norm_g"].tensor, offset=0, ap=[[0, P], [1, P]])).then_inc(vec_in, 16)
            for n, name in enumerate(("idx_k_ln_g", "idx_k_ln_b")):
                pool.dma_start(ikg[:, n, :], bass.AP(tensor=t[name].tensor, offset=0, ap=[[0, P], [1, HD]])).then_inc(vec_in, 16)
            for n, name in enumerate(("lambda_q1_2", "lambda_k1_2", "lambda_q2_2", "lambda_k2_2")):
                pool.dma_start(lam4[:, n, :], bass.AP(tensor=t[name].tensor, offset=0, ap=[[0, P], [1, HD]])).then_inc(lam_in, 16)
            for tile_ in (cn, ikn, avn):
                pool.memset(tile_[:, MC, :], 0.0)
            own.link(pool.memset(causal[:], 0.0))
            pool.affine_select(out=causal[:], in_=causal[:], compare_op=ALU.is_ge, fill=NEG, base=NKEY - P,
                               pattern=[[-1, NKEY]], channel_multiplier=1).then_inc(zeros, 1)
            pool.wait_ge(fA_ok, 2)
            for f, dram, length in ((fA, fA_dram, LEN_A), (fB, fB_dram, LEN_B)):
                pool.dma_start(dram[:, :, 0:length], f[:].unsqueeze(1).broadcast_to([NH, P, length])).then_inc(f_out, 16)
            pool.wait_ge(f_out, 32)
            for tile_, dram, length, width in ((biasA, fA_dram, LEN_A, NEAR), (biasB, fB_dram, LEN_B, NKEY)):
                pool.dma_start(tile_[:], bass.AP(tensor=dram.tensor, offset=P - 1,
                                                 ap=[[length, P], [P * (length + 1), NH], [1, width]])).then_inc(bias_in, 16)

            def low(name, i, b):
                pool.wait_ge(hi[b], PAIR0[name] + i + 1)
                n = KC[name] * P
                pool.tensor_tensor(wl[:, b, 0:n], stage[:, b, 0:n], wh[:, b, 0:n].bitcast(F32), ALU.subtract).then_inc(lo[b], 1)

            def lows(name):
                with pool.Fori(0, PAIRS[name]) as i:
                    low(name, i, 0)
                    low(name, i, 1)

            lows("gates1")
            lows("br1")
            pool.wait_ge(ev[1], PAIR0["kv2"] + 1)
            pool.iota(dist[:], pattern=[[-1, DIST]], base=3 * P, channel_multiplier=1,
                      allow_small_or_imprecise_dtypes=True).then_inc(dist_ok, 1)
            pool.wait_ge(dist_ok, 2)
            pool.memset(biasD[:, :, 0:META], 0.0)
            for i in range(NB):
                if i:
                    pool.wait_ge(ph["df"]["neg"], 8 * i)
                for h in range(4):
                    pool.tensor_scalar(biasD[:, h, META:NKEY], dist[:, 3 * P - P * i:3 * P - P * i + SEQ],
                                       -(2.0 ** (-8.0 * (h + 1) / 4)), None, ALU.mult).then_inc(biasD_ok, 1)
                if i == 0:
                    pool.wait_ge(nat_t, 3)
                    pool.wait_ge(dist_ok, 3)
                    pool.memset(biasW[:, :, 0:META], 0.0)
                    pool.memset(biasW[:, :, META + WIN2:], 0.0)
                    for h in range(NH):
                        pool.tensor_scalar(biasW[:, h, META:META + WIN2], tmp[:, 0, 0:WIN2],
                                           -(2.0 ** -(h + 1.0)), None, ALU.mult).then_inc(biasW_ok, 1)
            lows("gates2")
            lows("br2")

        @block.scalar
        def _(act):
            act.preload_act_table(ACT.Exp)
            for name, n in ROWS:
                src = t[name].rearrange("a (k p) -> (a k) p", p=P) if len(t[name].shape) == 2 else t[name].rearrange("(k p) -> k p", p=P)
                act.dma_start(rows[ROW[name]:ROW[name] + n, :], src).then_inc(rows_in, 16)
            act.dma_start(tab[0:BUCKETS, :], t["rel_bias"]).then_inc(tab_in, 16)
            act.dma_start(hotA[:], t["hot_a"]).then_inc(tab_in, 16)
            act.dma_start(hotB[:], t["hot_b"]).then_inc(tab_in, 16)
            act.dma_start(metain[:, 0, :], t["meta_tokens"]).then_inc(meta_in, 16)
            act.dma_start(metain[:, 1, :], t["meta_tokens_2"]).then_inc(meta_in, 16)
            act.dma_start(wuk[:], t["w_uk"][0].rearrange("c h d -> c (h d)")).then_inc(wuk_in, 16)
            act.dma_start(wuv[:], t["w_uv"][0].rearrange("c h d -> c (h d)")).then_inc(wuk_in, 16)

            def high(name, i, b):
                act.wait_ge(w_in[b], 16 * (LOAD0[name] + LOADS[name]) + i * (16 * LOADS[name]))
                if not (name == "kv1" and isinstance(i, int) and i == 0):
                    act.wait_ge(mm[b], PAIR0[name] + i)
                n = KC[name] * P
                act.activation(wh[:, b, 0:n], stage[:, b, 0:n], ACT.Copy).then_inc(hi[b], 1)

            def high_next(name, i, last):
                if not last:
                    high(name, i + 1, 0)
                elif AFTER[name]:
                    high(AFTER[name], 0, 0)

            def only_high(name):
                if PAIRS[name] == 2:
                    high(name, 0, 1)
                    high_next(name, 0, False)
                elif PAIRS[name] > 2:
                    with act.Fori(0, PAIRS[name] - 1) as i:
                        high(name, i, 1)
                        high_next(name, i, False)
                high(name, PAIRS[name] - 1, 1)
                high_next(name, PAIRS[name] - 1, True)

            act.wait_ge(x_in, 16 * NB)
            for n in range(NB):
                if n:
                    act.wait_ge(x_sq, n)
                act.activation(junk[:], xin[:, n, :], ACT.Square, accum_out=st[:, 0, n:n + 1]).then_inc(x_sq, 1)
            act.wait_ge(meta_in, 32)
            act.wait_ge(x_sq, NB)
            for n in range(2):
                if n:
                    act.wait_ge(meta_sq, n)
                act.activation(junk[0:META, :], metain[:, n, :], ACT.Square, accum_out=st[0:META, 1, n:n + 1]).then_inc(meta_sq, 1)
            act.wait_ge(lam_sum, 1)
            act.activation(lam[:, 2:4], lam[:, 0:2], ACT.Exp).then_inc(lam_e, 1)
            high("kv1", 0, 0)
            act.wait_ge(gvec_ok, 1)
            for k in range(KD):
                act.wait_ge(x_taken, k + 1)
                g = ROW["attn_norm_g"] + k
                act.activation(hn[:, 0, k, :], hT[:, k, :], ACT.Copy, scale=gvec[:, g:g + 1]).then_inc(xhi, 1)

            for name in ("kv1", "bq1", "iq1", "aq1"):
                only_high(name)
            act.wait_ge(ssq_in, 1)
            for k in range(2):
                g = ROW["q_norm_g"] + k
                act.activation(bqg[:, 0, k, :], bqT[:, k, :], ACT.Copy, scale=gvec[:, g:g + 1]).then_inc(bqhi, 1)
            only_high("uq1")
            for u in range(4 * NB):
                K = META + P * (u // 4 + 1)
                act.wait_ge(lg_mm, u + 1)
                if u >= 2:
                    act.wait_ge(lg_used, u - 1)
                src = psS[:, 2 * (u % 2):2 * (u % 2) + 2, :]
                if K > 512:
                    act.activation(relu[:, u % 2, :].rearrange("p (a b) -> p a b", a=2), src[:, :, 0:K // 2], ACT.Relu).then_inc(lg_taken, 1)
                else:
                    act.activation(relu[:, u % 2, 0:K], src[:, 0, 0:K], ACT.Relu).then_inc(lg_taken, 1)

            def gate_part(l, j):
                name, s = f"gates{l}", (j - 3) // 2
                if j >= 3 and j % 2 and s < 2 * KD:
                    i, b = divmod(s, 2)
                    act.wait_ge(ev[b], PAIR0[name] + i + 1)
                    bias = bhalf[:, s:s + 1] if l == 1 else 0.0
                    act.activation(gate[:, s, :], tmp[:, b, :], ACT.Tanh, bias=bias, scale=0.5).then_inc(th_ok[b], 1)
                if j % 2 == 0 and j // 2 < 2 * KD:
                    i, b = divmod(j // 2, 2)
                    if b == 0:
                        high(name, i, 1)
                    else:
                        high_next(name, i, i == KD - 1)

            def softmax_unit(p, u, tile, col):
                act.wait_ge(p["neg"], u + 1)
                act.activation(tile, tile, ACT.Exp, bias=negm[:, col:col + 1],
                               accum_out=rsum[:, col:col + 1]).then_inc(p["p"], 1)

            def sink_part(p, l, i):
                act.wait_ge(p["es"], 2 * i + 1)
                act.activation(st[:, 3, :], st[:, 2, :], ACT.Exp).then_inc(p["es"], 1)

            def take_pt(p, u, chunks, dst):
                act.wait_ge(p["pt"], u + 1)
                if u >= 2:
                    act.wait_ge(p["pv"], u - 1)
                whole = [c for c in chunks if c[2] == P]
                if any(c[2] == META for c in chunks):
                    act.activation(dst[0:META, dst.shape[-1] - P:], psT[0:META, 1, 0:P], ACT.Copy)
                act.activation(dst[:, 0:len(whole) * P], psT[:, 0, 0:len(whole) * P], ACT.Copy).then_inc(p["ptx"], 1)

            def heads_high(m, dst):
                for i in range(NB):
                    act.wait_ge(oT_taken, NB * m + i + 1)
                    act.activation(dst[:, 0, :, i * P:(i + 1) * P],
                                   tmp[:, i % 2, :].rearrange("p (c q) -> p c q", c=4), ACT.Copy).then_inc(o_hi, 1)

            units = list(window1_units())
            p = ph["w1"]
            for j in range(len(units) + 3):
                if j < len(units):
                    softmax_unit(p, j, W3a[:, j % 3, 0:units[j][3]], j)
                gate_part(1, j)
                if 2 <= j < len(units) + 2:
                    take_pt(p, j - 2, units[j - 2][4], PTa[:, j % 2, :])
                if j >= 3 and (j - 3) % NH == NH - 1:
                    sink_part(p, 0, (j - 3) // NH)
            heads_high(0, oA)
            units = list(latent_units())
            p = ph["la"]
            for j in range(len(units) + 2):
                if j < len(units):
                    softmax_unit(p, j, W3[:, j % 3, 0:units[j][2]], j)
                if j >= 2:
                    take_pt(p, j - 2, units[j - 2][3], PT[:, j % 2, :])
            heads_high(1, oB)

            def branches(l):
                name, m0 = f"br{l}", (l - 1) * KD

                def pair(i, last):
                    high(name, i, 1)
                    high_next(name, i, last)
                    act.wait_ge(mix_ok, m0 + i + 1)
                    act.activation(mix[:, 0, bass.ds(i, 1), :], mix32[:, 2, :], ACT.Copy).then_inc(mix_hi, 1)

                with act.Fori(0, PAIRS[name] - 1) as i:
                    pair(i, False)
                pair(PAIRS[name] - 1, True)

            def squares_and_gain(name, norm, grow):
                def chunk(i, b):
                    act.wait_ge(ev[b], PAIR0[name] + i + 1)
                    act.wait_ge(h_sq2, 2 * i + (squares_cleared(norm) + b))
                    act.activation(sq[:], hT[:, bass.ds(2 * i + b, 1), :], ACT.Square).then_inc(h_sq, 1)
                    act.activation(hn[:, 0, bass.ds(2 * i + b, 1), :], hT[:, bass.ds(2 * i + b, 1), :], ACT.Copy,
                                   scale=gvec[:, bass.ds(2 * i + (grow + b), 1)]).then_inc(hg_hi, 1)

                def pair(i, last):
                    high(name, i, 1)
                    chunk(i, 0)
                    high_next(name, i, last)
                    chunk(i, 1)

                with act.Fori(0, PAIRS[name] - 1) as i:
                    pair(i, False)
                pair(PAIRS[name] - 1, True)

            def swiglu(name, f0, early=0):
                def pair(i, last, early=False):
                    high(name, i, 1)
                    if early:
                        high_next(name, i, last)
                    act.wait_ge(ev[0], PAIR0[name] + i + 1)
                    act.activation(ft[:, 1, :], ft[:, 0, :], ACT.Tanh, scale=0.5).then_inc(t_ok, 1)
                    if not early:
                        high_next(name, i, last)
                    act.wait_ge(hid_ok, f0 + i + 1)
                    act.activation(hid[:, 0, bass.ds(i, 1), :], ft[:, 4, :], ACT.Copy).then_inc(hid_hi, 1)

                for i in range(early):
                    pair(i, False, True)
                with act.Fori(early, PAIRS[name] - 1) as i:
                    pair(i, False)
                pair(PAIRS[name] - 1, True)

            branches(1)
            squares_and_gain("out1", 0, ROW["ffn_norm_g"])
            swiglu("gu1a", 0, 1)
            only_high("dn1a")
            swiglu("gu1b", NFH)
            name = "dn1b"

            def chunk1(i, b):
                act.wait_ge(ev[b], PAIR0[name] + i + 1)
                act.wait_ge(h_sq2, 2 * i + (squares_cleared(1) + b))
                act.activation(sq[:], hT[:, bass.ds(2 * i + b, 1), :], ACT.Square).then_inc(h_sq, 1)
                act.wait_ge(h_gain, 2 * i + b + 1)
                act.activation(hn[:, 0, bass.ds(2 * i + b, 1), :], hT[:, bass.ds(2 * i + b, 1), :], ACT.Copy,
                               scale=gvec[:, bass.ds(2 * i + (ROW["norm_mix_2"] + b), 1)]).then_inc(hg_hi, 1)

            def pair1(i, last):
                high(name, i, 1)
                chunk1(i, 0)
                high_next(name, i, last)
                chunk1(i, 1)

            with act.Fori(0, PAIRS[name] - 1) as i:
                pair1(i, False)
            pair1(PAIRS[name] - 1, True)

            for name in ("kv2", "qa2", "qb2"):
                only_high(name)
            p = ph["df"]
            for j in range(16 + 2):
                if j < 16:
                    for m in range(2):
                        softmax_unit(p, 2 * j + m, W6[:, j % 3, m, :], 2 * j + m)
                if j >= 2:
                    take_pt(p, j - 2, [(MC, 0, META)] + [(c, 0, P) for c in range(NB)], PT2[:, j % 2, :])
            act.wait_ge(p["on"], NB)
            for i in range(NB):
                act.wait_ge(y_sq, 2 * i)
                act.activation(sq[:], yn[:, i, :], ACT.Square).then_inc(y_sq, 1)
            units = list(window2_units())
            p = ph["w2"]
            for j in range(len(units) + 3):
                if j < len(units):
                    softmax_unit(p, j, W3b[:, j % 3, 0:units[j][3] + META], j)
                gate_part(2, j)
                if j >= 2 and j - 2 < len(units):
                    take_pt(p, j - 2, units[j - 2][7], PTb[:, j % 2, :])
                if j >= 3 and (j - 3) % NH == NH - 1:
                    sink_part(p, 1, (j - 3) // NH)
            heads_high(2, oA)
            heads_high(3, oB)
            branches(2)
            squares_and_gain("out2", 2, ROW["norm_ffn_2"])
            swiglu("gu2a", 2 * NFH, 1)
            only_high("dn2a")
            swiglu("gu2b", 3 * NFH)
            name = "dn2b"

            def chunk2(i, b):
                act.wait_ge(ev[b], PAIR0[name] + i + 1)
                act.wait_ge(h_sq2, 2 * i + (squares_cleared(3) + b))
                act.activation(sq[:], hT[:, bass.ds(2 * i + b, 1), :], ACT.Square).then_inc(h_sq, 1)
                act.activation(hgf[:, bass.ds(2 * i + b, 1), :], hT[:, bass.ds(2 * i + b, 1), :], ACT.Copy,
                               scale=gvec[:, bass.ds(2 * i + (ROW["norm_final_2"] + b), 1)]).then_inc(fin_gain, 1)

            def pair2(i, last):
                high(name, i, 1)
                chunk2(i, 0)
                high_next(name, i, last)
                chunk2(i, 1)

            with act.Fori(0, PAIRS[name] - 1) as i:
                pair2(i, False)
            pair2(PAIRS[name] - 1, True)


        @block.vector
        def _(v):
            dv = Tally(v, dve_own)

            def spread(ap, width):
                return ap.unsqueeze(2).broadcast_to([ap.shape[0], ap.shape[1], width])

            def low(name, i, b):
                if name in POOL_LOW:
                    return
                v.wait_ge(hi[b], PAIR0[name] + i + 1)
                n = KC[name] * P
                v.tensor_tensor(wl[:, b, 0:n], stage[:, b, 0:n], wh[:, b, 0:n].bitcast(F32), ALU.subtract).then_inc(lo[b], 1)

            def low_next(name, i, last):
                if not last:
                    low(name, i + 1, 0)
                elif AFTER[name]:
                    low(AFTER[name], 0, 0)

            def done(name, i, b):
                v.wait_ge(mm[b], PAIR0[name] + i + 1)

            def pairs(name, pair, first=0):
                if PAIRS[name] - 1 > first:
                    with v.Fori(first, PAIRS[name] - 1) as i:
                        pair(i, False)
                pair(PAIRS[name] - 1, True)

            def rsqrt(x, y, n, parts=P):
                step, bits = rst[0:parts, 0:n], rsti[0:parts, 0:n]
                dv.link(v.tensor_scalar(bits, x.bitcast(I32), 1, None, ALU.logical_shift_right))
                dv.link(v.tensor_scalar(y.bitcast(I32), bits, -1.0, RSQRT_SEED, ALU.mult, ALU.add))
                for _ in range(3):
                    dv.link(v.scalar_tensor_tensor(out=step, in0=y, scalar=-0.5, in1=y, op0=ALU.mult, op1=ALU.mult))
                    dv.link(v.tensor_tensor(step, step, x, ALU.mult))
                    dv.link(v.scalar_tensor_tensor(out=y, in0=step, scalar=1.5, in1=y, op0=ALU.add, op1=ALU.mult))

            def diagonals(dst, r):
                for n in range(NB):
                    ins = v.tensor_scalar(dst[:, n, :], ident[:], r[:, n:n + 1], None, ALU.mult)
                return ins

            v.wait_ge(gvec_t, 1)
            v.tensor_copy(gvec[:], psT[:, 0, 0:NROWS]).then_inc(gvec_ok, 1)
            v.wait_ge(gvec_ok, 1)
            b0 = ROW["b_gates"]
            dv.link(v.tensor_scalar(bhalf[:], gvec[:, b0:b0 + 2 * KD], 0.5, None, ALU.mult))
            v.wait_ge(lam_in, 64)
            dv.link(v.tensor_tensor_reduce(out=lamj[:], in0=lam4[:, 0, :], in1=lam4[:, 1, :], scale=1.0, scalar=0.0,
                                           op0=ALU.mult, op1=ALU.add, accum_out=lam[:, 0:1]))
            v.tensor_tensor_reduce(out=lamj[:], in0=lam4[:, 2, :], in1=lam4[:, 3, :], scale=1.0, scalar=0.0,
                                   op0=ALU.mult, op1=ALU.add, accum_out=lam[:, 1:2]).then_inc(lam_sum, 1)
            v.wait_ge(f_mm, 1)
            v.tensor_copy(fA[:], psL[0:NH, 0, 0:LEN_A]).then_inc(fA_ok, 1)
            v.wait_ge(f_mm, 2)
            v.tensor_copy(fB[:, 0:512], psL[0:NH, 1, :])
            v.tensor_copy(fB[:, 512:LEN_B], psT[0:NH, 1, 0:LEN_B - 512]).then_inc(fA_ok, 1)
            v.wait_ge(meta_sq, 2)
            dv.link(v.tensor_scalar(st[0:META, 1, 2:4], st[0:META, 1, 0:2], 1.0 / D, EPS, ALU.mult, ALU.add))
            rsqrt(st[0:META, 1, 2:4], rs[0:META, 0:2], 2, META)
            for n in range(2):
                v.tensor_scalar(metain[:, n, :], metain[:, n, :], rs[0:META, n:n + 1], None, ALU.mult).then_inc(meta_ok, 1)
            v.wait_ge(meta_ok, 2)
            for k in range(KD + 1):
                if k < KD:
                    v.wait_ge(x_t, k + 1)
                    v.tensor_copy(hT[:, k, :], psS[:, k % 4, :]).then_inc(x_taken, 1)
                if k:
                    g = ROW["attn_norm_g"] + k - 1
                    v.wait_ge(xhi, k)
                    v.scalar_tensor_tensor(out=hn[:, 1, k - 1, :], in0=hT[:, k - 1, :], scalar=gvec[:, g:g + 1],
                                           in1=hn[:, 0, k - 1, :].bitcast(F32), op0=ALU.mult, op1=ALU.subtract).then_inc(xlo, 1)
            v.wait_ge(meta_t, 1)
            for l, name in enumerate(("attn_norm_g", "norm_mix_2")):
                ins = v.tensor_tensor(metaT[:, l, :, :], psT[:, 0, l * P:(l + 1) * P].rearrange("p (k m) -> p k m", k=KD),
                                      spread(gvec[:, ROW[name]:ROW[name] + KD], META), ALU.mult)
            ins.then_inc(metaT_ok, 1)
            v.wait_ge(x_sq, NB)
            dv.link(v.tensor_scalar(st[:, 0, 4:8], st[:, 0, 0:4], 1.0 / D, EPS, ALU.mult, ALU.add))
            rsqrt(st[:, 0, 4:8], rs[:, 0:4], 4)
            v.wait_ge(consts, 1)
            diagonals(diag, rs[:, 0:4]).then_inc(diag_ok, 1)
            v.wait_ge(lam_e, 1)
            dv.link(v.tensor_tensor(neglam[:], lam[:, 3:4], lam[:, 2:3], ALU.subtract))
            dv.link(v.tensor_scalar(neglam[:], neglam[:], -LAMBDA0, None, ALU.add))
            low("kv1", 0, 0)
            v.wait_ge(bcast, 1)
            v.tensor_copy(R[:], psT[:, 1, :]).then_inc(R_ok, 1)
            v.wait_ge(R_ok, 1)

            def take_keys(name, i, b, dst):
                done(name, i, b)
                v.tensor_tensor(dst[:, META:NKEY], psL[:, b, :], R[:], ALU.mult)
                v.tensor_copy(dst[:, 0:META], psS[:, b, 0:META]).then_inc(ev[b], 1)

            def take_scaled(name, i, b, dst, by, scale=1.0):
                done(name, i, b)
                v.scalar_tensor_tensor(out=dst, in0=psL[:, b, :], scalar=scale, in1=by, op0=ALU.mult, op1=ALU.mult).then_inc(ev[b], 1)

            keys = [bkvT[:], ikwT[:], akT[:], avT[:]]
            for i in range(2):
                low("kv1", i, 1)
                take_keys("kv1", i, 0, keys[2 * i])
                low_next("kv1", i, i == 1)
                take_keys("kv1", i, 1, keys[2 * i + 1])
            v.wait_ge(f_out, 32)
            low("bq1", 0, 1)
            take_scaled("bq1", 0, 0, bqT[:, 0, :], R[:])
            low_next("bq1", 0, True)
            take_scaled("bq1", 0, 1, bqT[:, 1, :], R[:])
            v.wait_ge(ev[0], PAIR0["bq1"] + 1)
            v.wait_ge(ev[1], PAIR0["bq1"] + 1)
            dv.link(v.tensor_tensor(sq[:], bqT[:, 0, :], bqT[:, 0, :], ALU.mult))
            dv.link(v.tensor_tensor(tmp[:, 0, :], bqT[:, 1, :], bqT[:, 1, :], ALU.mult))
            v.tensor_tensor(sq[:], sq[:], tmp[:, 0, :], ALU.add).then_inc(ssq_in, 1)
            v.wait_ge(zeros, 1)
            v.wait_ge(nat_t, 1)
            for n, dst in enumerate((cn, ikn, avn)):
                dv.link(v.tensor_copy(dst[:, 0:NB, :], psS[:, n, :].rearrange("p (c f) -> p c f", c=NB)))
                ins = v.tensor_copy(dst[0:META, MC, :], psT[0:META, 0, n * P:(n + 1) * P])
            ins.then_inc(nat_taken, 1)
            v.wait_ge(nat_taken, 1)
            low("iq1", 0, 1)
            take_scaled("iq1", 0, 0, iqT[:, 0, :], R[:])
            low_next("iq1", 0, True)
            take_scaled("iq1", 0, 1, iqT[:, 1, :], R[:])
            low("aq1", 0, 1)
            take_scaled("aq1", 0, 0, aqT[:, 0, :], R[:], QSCALE)
            NC = NB + 1
            flat = tmp[:, :, :].rearrange("p a n -> p (a n)")
            t5 = flat[:, 0:NC * P].rearrange("p (c f) -> p c f", c=NC)
            dv.link(v.tensor_tensor(t5, cn[:], cn[:], ALU.mult))
            dv.link(v.tensor_reduce(st[:, 6, 0:NC], t5, AX_X, ALU.add))
            dv.link(v.tensor_scalar(st[:, 7, 0:NC], st[:, 6, 0:NC], 1.0 / P, EPS, ALU.mult, ALU.add))
            rsqrt(st[:, 7, 0:NC], rs[:, 0:NC], NC)
            dv.link(v.tensor_tensor(cn[:], cn[:], spread(rs[:, 0:NC], P), ALU.mult))
            v.wait_ge(vec_in, 80)
            v.tensor_tensor(cn[:], cn[:], kvg[:].unsqueeze(1).broadcast_to([P, NC, P]), ALU.mult).then_inc(nat_ok, 1)
            low_next("aq1", 0, False)
            take_scaled("aq1", 0, 1, aqT[:, 1, :], R[:], QSCALE)
            low("aq1", 1, 1)
            t5 = flat[:, 0:NC * HD].rearrange("p (c f) -> p c f", c=NC)
            ik = ikn[:, :, 0:HD]
            dv.link(v.tensor_scalar(iwn[:], ikn[:, 0:NB, HD:HD + 4], (4 * HD) ** -0.5, None, ALU.mult))
            dv.link(v.tensor_reduce(st[:, 6, 0:NC], ik, AX_X, ALU.add))
            dv.link(v.tensor_scalar(st[:, 7, 0:NC], st[:, 6, 0:NC], 1.0 / HD, None, ALU.mult))
            dv.link(v.tensor_tensor(ikx[:], ik, spread(st[:, 7, 0:NC], HD), ALU.subtract))
            dv.link(v.tensor_tensor(t5, ikx[:], ikx[:], ALU.mult))
            dv.link(v.tensor_reduce(st[:, 6, 0:NC], t5, AX_X, ALU.add))
            dv.link(v.tensor_scalar(st[:, 7, 0:NC], st[:, 6, 0:NC], 1.0 / HD, EPS, ALU.mult, ALU.add))
            rsqrt(st[:, 7, 0:NC], rs[:, 0:NC], NC)
            dv.link(v.tensor_tensor(ikx[:], ikx[:], spread(rs[:, 0:NC], HD), ALU.mult))
            dv.link(v.tensor_tensor(ikx[:], ikx[:], ikg[:, 0, :].unsqueeze(1).broadcast_to([P, NC, HD]), ALU.mult))
            for c in range(2):
                ins = v.tensor_tensor(ikn[:, :, c * HD:(c + 1) * HD], ikx[:], ikg[:, 1, :].unsqueeze(1).broadcast_to([P, NC, HD]), ALU.add)
            ins.then_inc(nat_ok, 1)
            take_scaled("aq1", 1, 0, aqT[:, 2, :], R[:], QSCALE)
            low_next("aq1", 1, True)
            v.wait_ge(ssq_mm, 1)
            dv.link(v.tensor_scalar(st[:, 7, 0:4], psT[:, 1, 0:4], 1.0 / 256, EPS, ALU.mult, ALU.add))
            rsqrt(st[:, 7, 0:4], rs[:, 0:4], 4)
            diagonals(diag, rs[:, 0:4]).then_inc(diag_ok, 1)
            v.wait_ge(bqhi, 2)
            for k in range(2):
                g = ROW["q_norm_g"] + k
                v.scalar_tensor_tensor(out=bqg[:, 1, k, :], in0=bqT[:, k, :], scalar=gvec[:, g:g + 1], in1=bqg[:, 0, k, :].bitcast(F32),
                                       op0=ALU.mult, op1=ALU.subtract).then_inc(bqlo, 1)
            take_scaled("aq1", 1, 1, aqT[:, 3, :], R[:], QSCALE)
            low("uq1", 0, 1)
            v.wait_ge(key_t, 1)
            for n, dst in enumerate((cT, ikT)):
                v.tensor_copy(dst[:, META:NKEY], psS[:, n, :])
                v.tensor_copy(dst[:, 0:META], psT[:, 0, n * META:(n + 1) * META])
            v.tensor_copy(wukT[:], psS[:, 2, :].rearrange("p (c f) -> p c f", c=4)).then_inc(key_taken, 1)
            v.wait_ge(bcast, 2)
            v.tensor_copy(sq[:], psT[:, 1, :]).then_inc(R_ok, 1)
            v.wait_ge(R_ok, 2)
            for i in range(2):
                if i:
                    low("uq1", i, 1)
                take_scaled("uq1", i, 0, qT[:, 2 * i, :], sq[:])
                low_next("uq1", i, i == 1)
                take_scaled("uq1", i, 1, qT[:, 2 * i + 1, :], sq[:])
            for u in range(4 * NB):
                i, h = divmod(u, 4)
                K = META + P * (i + 1)
                v.wait_ge(lg_taken, u + 1)
                if h:
                    v.wait_ge(lg_used, u)
                v.scalar_tensor_tensor(out=acc[:, i, 0:K], in0=relu[:, u % 2, 0:K], scalar=iwn[:, i, h:h + 1],
                                       in1=acc[:, i, 0:K] if h else causal[:, NKEY - K:NKEY], op0=ALU.mult, op1=ALU.add).then_inc(lg_used, 1)
            v.wait_ge(lg_used, 4 * NB)

            def gate_part(l, j):
                if j >= 2 and j % 2 == 0 and (j - 2) // 2 < 2 * KD:
                    name, (i, b) = f"gates{l}", divmod((j - 2) // 2, 2)
                    done(name, i, b)
                    if l == 2 or i:
                        v.wait_ge(th_ok[b], KD * (l - 1) + i)
                    v.tensor_tensor(tmp[:, b, :], psL[:, b, :], R[:], ALU.mult).then_inc(ev[b], 1)

            best = st[:, 9, :]
            ROUNDS = TOPK // 8

            def top_rounds(j):
                blk, n = divmod(j, ROUNDS // 2)
                K = META + P * (blk + 1)
                for _ in range(2):
                    dv.link(v.max(best, acc[:, blk, 0:K]))
                    dv.link(v.match_replace(acc[:, blk, 0:K], best, acc[:, blk, 0:K], TAKEN))
                if n == ROUNDS // 2 - 1:
                    v.tensor_scalar(selm[:, blk, 0:K], acc[:, blk, 0:K], TAKEN / 2, NEG, ALU.is_gt, ALU.mult).then_inc(sel_ok, 1)

            def biased(p, u, tile, scores, bias, least, col):
                dv.link(v.tensor_tensor_reduce(out=tile, in0=scores, in1=bias, scale=1.0, scalar=least,
                                               op0=ALU.add, op1=ALU.max, accum_out=mx[:, col:col + 1]))
                v.tensor_scalar(negm[:, col:col + 1], mx[:, col:col + 1], -1.0, None, ALU.mult).then_inc(p["neg"], 1)

            def sink_sum(p, l, i):
                v.wait_ge(p["neg"], NH * (i + 1))
                v.tensor_tensor(st[:, 2, :], sinkb[:, l, :], negm[:, i * NH:(i + 1) * NH], ALU.add).then_inc(p["es"], 1)

            def sink_normed(p, i, dst):
                v.wait_ge(p["es"], 2 * i + 2)
                dv.link(v.tensor_tensor(st[:, 4, :], st[:, 3, :], rsum[:, i * NH:(i + 1) * NH], ALU.add))
                dv.link(v.reciprocal(st[:, 5, :], st[:, 4, :]))
                v.wait_ge(p["pv"], NH * (i + 1))
                v.tensor_tensor(dst[:, i, :].rearrange("p (h d) -> p h d", h=NH), psS[:, 2 * (i % 2) + 1, :].rearrange("p (h d) -> p h d", h=NH),
                                spread(st[:, 5, :], HD), ALU.mult).then_inc(p["on"], 1)

            def heads_low(m, dst, gain=None):
                for i in range(NB + 1):
                    if i < NB:
                        v.wait_ge(oT_mm, NB * m + i + 1)
                        if i >= 2 or m == 3:
                            v.wait_ge(o_lo, NB * m + i - 1)
                        if gain is None:
                            v.tensor_copy(tmp[:, i % 2, :], psS[:, i, :]).then_inc(oT_taken, 1)
                        else:
                            v.tensor_scalar(tmp[:, i % 2, :], psS[:, i, :], gain, 1.0 - LAMBDA0, ALU.mult, ALU.mult).then_inc(oT_taken, 1)
                    if i:
                        v.wait_ge(o_hi, NB * m + i)
                        c = slice((i - 1) * P, i * P)
                        v.tensor_tensor(dst[:, 1, :, c], tmp[:, (i - 1) % 2, :].rearrange("p (c q) -> p c q", c=4),
                                        dst[:, 0, :, c].bitcast(F32), ALU.subtract).then_inc(o_lo, 1)

            v.wait_ge(bias_in, 32)
            units = list(window1_units())
            p = ph["w1"]
            for j in range(len(units) + 4):
                if j < len(units):
                    i, h, _, W, _ = units[j]
                    v.wait_ge(p["s"], j + 1)
                    if j >= 3:
                        v.wait_ge(p["pt"], j - 2)
                    biased(p, j, W3a[:, j % 3, 0:W], psS[:, 2 * (j % 2), 0:W], biasA[:, h, NEAR - W:NEAR], sinkb[:, 0, h:h + 1], j)
                    if h == NH - 1:
                        sink_sum(p, 0, i)
                    top_rounds(j)
                gate_part(1, j)
                if j >= 4 and (j - 4) % NH == NH - 1:
                    sink_normed(p, (j - 4) // NH, on)
            for b in range(2):
                v.wait_ge(th_ok[b], KD)
            heads_low(0, oA)
            for h in range(NH):
                v.wait_ge(qabs_mm, h + 1)
                v.tensor_scalar(qabs[:, h, :], psL[:, h % 2, :], QSCALE, None, ALU.mult).then_inc(qabs_ok, 1)
            units = list(latent_units())
            p = ph["la"]
            for j in range(len(units) + 6):
                if j < len(units):
                    i, h, K, _ = units[j]
                    v.wait_ge(p["s"], j + 1)
                    if j >= 3:
                        v.wait_ge(p["pt"], j - 2)
                    biased(p, j, as_halves(W3[:, j % 3, 0:K], K), two_banks(psS[:, 2 * (j % 2):2 * (j % 2) + 2, :], K),
                           as_halves(biasB[:, h, NKEY - K:NKEY], K), TAKEN, j)
                if j >= 5 and (j - 5) % NH == NH - 1:
                    i = (j - 5) // NH
                    v.wait_ge(p["p"], NH * (i + 1))
                    dv.link(v.reciprocal(st[:, 5, :], rsum[:, i * NH:(i + 1) * NH]))
                    v.wait_ge(p["o"], NH * (i + 1))
                    v.tensor_tensor(on[:, i, :].rearrange("p (h d) -> p h d", h=NH), psL[:, 1, :].rearrange("p (h d) -> p h d", h=NH),
                                    spread(st[:, 5, :], HD), ALU.mult).then_inc(p["on"], 1)
                if 3 <= j < len(units) + 3:
                    u = j - 3
                    v.wait_ge(p["pv"], u + 1)
                    if u >= 2:
                        v.wait_ge(p["o"], u - 1)
                    v.tensor_copy(lat[:, u % 2, :], psL[:, 0, 0:P]).then_inc(p["lat"], 1)
            heads_low(1, oB)

            def branches(l):
                name, m0 = f"br{l}", (l - 1) * KD

                def pair(i, last):
                    low(name, i, 1)
                    done(name, i, 0)
                    v.scalar_tensor_tensor(out=mix32[:, 0, :], in0=gate[:, bass.ds(i, 1), :], scalar=1.0, in1=psL[:, 0, :],
                                           op0=ALU.add, op1=ALU.mult).then_inc(ev[0], 1)
                    low_next(name, i, last)
                    done(name, i, 1)
                    v.scalar_tensor_tensor(out=mix32[:, 1, :], in0=gate[:, bass.ds(i + KD, 1), :], scalar=1.0, in1=psL[:, 1, :],
                                           op0=ALU.add, op1=ALU.mult).then_inc(ev[1], 1)
                    for b in range(2):
                        v.wait_ge(ev[b], PAIR0[name] + i + 1)
                    v.tensor_tensor(mix32[:, 2, :], mix32[:, 0, :], mix32[:, 1, :], ALU.add).then_inc(mix_ok, 1)
                    v.wait_ge(mix_hi, m0 + i + 1)
                    v.tensor_tensor(mix[:, 1, bass.ds(i, 1), :], mix32[:, 2, :], mix[:, 0, bass.ds(i, 1), :].bitcast(F32),
                                    ALU.subtract).then_inc(mix_lo, 1)

                pairs(name, pair)

            def clear_squares():
                v.memset(sqacc[:, 0, :], 0.0).then_inc(h_sq2, 1)

            def add_squares(norm, n):
                v.wait_ge(h_sq, n + (norm * KD + 1))
                v.wait_ge(h_sq2, n + squares_cleared(norm))
                v.tensor_tensor(sqacc[:, 0, :], sqacc[:, 0, :], sq[:], ALU.add).then_inc(h_sq2, 1)

            def gain_low(n, count, grow):
                v.wait_ge(hg_hi, count + 1)
                v.scalar_tensor_tensor(out=hn[:, 1, bass.ds(n, 1), :], in0=hT[:, bass.ds(n, 1), :], scalar=gvec[:, bass.ds(n + grow, 1)],
                                       in1=hn[:, 0, bass.ds(n, 1), :].bitcast(F32), op0=ALU.mult, op1=ALU.subtract).then_inc(hg_lo, 1)

            def out_project(l, norm, hg0, grow):
                name = f"out{l}"

                def chunk(i, b):
                    n = 2 * i + b
                    done(name, i, b)
                    v.scalar_tensor_tensor(out=hT[:, bass.ds(n, 1), :], in0=psL[:, b, :], scalar=0.5, in1=hT[:, bass.ds(n, 1), :],
                                           op0=ALU.mult, op1=ALU.add).then_inc(ev[b], 1)
                    add_squares(norm, n)
                    gain_low(n, 2 * i + (hg0 + b), grow)

                def pair(i, last):
                    low(name, i, 1)
                    chunk(i, 0)
                    low_next(name, i, last)
                    chunk(i, 1)

                clear_squares()
                pairs(name, pair)

            def new_rms(ssq_count):
                v.wait_ge(ssq_mm, ssq_count)
                dv.link(v.tensor_scalar(st[:, 8, 0:4], psT[:, 1, 0:4], 1.0 / D, EPS, ALU.mult, ALU.add))
                rsqrt(st[:, 8, 0:4], rs[:, 0:4], 4)

            def swiglu(name, f0, head=None):
                def pair(i, last, head=None):
                    low(name, i, 1)
                    if head:
                        new_rms(head[0])
                        diagonals(diag, rs[:, 0:4]).then_inc(diag_ok, 1)
                        low_next(name, i, last)
                        v.wait_ge(bcast, head[1])
                        v.tensor_copy(R[:], psT[:, 1, :]).then_inc(R_ok, 1)
                        v.wait_ge(R_ok, head[1])
                    done(name, i, 0)
                    v.tensor_tensor(ft[:, 0, :], psL[:, 0, :], R[:], ALU.mult).then_inc(ev[0], 1)
                    if not head:
                        low_next(name, i, last)
                    v.wait_ge(t_ok, f0 + i + 1)
                    dv.link(v.scalar_tensor_tensor(out=ft[:, 2, :], in0=ft[:, 1, :], scalar=1.0, in1=ft[:, 0, :], op0=ALU.add, op1=ALU.mult))
                    done(name, i, 1)
                    v.tensor_tensor(ft[:, 3, :], psL[:, 1, :], R[:], ALU.mult).then_inc(ev[1], 1)
                    v.wait_ge(ev[1], PAIR0[name] + i + 1)
                    v.scalar_tensor_tensor(out=ft[:, 4, :], in0=ft[:, 2, :], scalar=0.5, in1=ft[:, 3, :], op0=ALU.mult, op1=ALU.mult).then_inc(hid_ok, 1)
                    v.wait_ge(hid_hi, f0 + i + 1)
                    v.tensor_tensor(hid[:, 1, bass.ds(i, 1), :], ft[:, 4, :], hid[:, 0, bass.ds(i, 1), :].bitcast(F32), ALU.subtract).then_inc(hid_lo, 1)

                first = 0
                if head:
                    pair(0, False, head)
                    first = 1
                with v.Fori(first, PAIRS[name] - 1) as i:
                    dv.enter(i - first, 1)
                    pair(i, False)
                dv.leave(PAIRS[name] - 1 - first)
                pair(PAIRS[name] - 1, True)

            def add_down(name, i, b):
                done(name, i, b)
                n = bass.ds(2 * i + b, 1)
                v.tensor_tensor(hT[:, n, :], hT[:, n, :], psL[:, b, :], ALU.add).then_inc(ev[b], 1)

            def down(name):
                def pair(i, last):
                    low(name, i, 1)
                    add_down(name, i, 0)
                    low_next(name, i, last)
                    add_down(name, i, 1)

                pairs(name, pair)

            branches(1)
            out_project(1, 0, 0, ROW["ffn_norm_g"])
            swiglu("gu1a", 0, (2, 3))
            down("dn1a")
            swiglu("gu1b", NFH)

            def end_chunk(i, b):
                n = 2 * i + b
                add_down("dn1b", i, b)
                add_squares(1, n)
                v.tensor_scalar(hT[:, bass.ds(n, 1), :], hT[:, bass.ds(n, 1), :], gvec[:, bass.ds(n + ROW["final_norm_g"], 1)], None,
                                ALU.mult).then_inc(h_gain, 1)
                v.wait_ge(h_gain, 2 * i + b + 1)
                dv.link(v.tensor_tensor(tmp[:, 0, :], hT[:, bass.ds(n, 1), :], hT[:, bass.ds(n, 1), :], ALU.mult))
                v.wait_ge(x2_sq, 2 * i + b + 1)
                v.tensor_tensor(sqacc[:, 1, :], sqacc[:, 1, :], tmp[:, 0, :], ALU.add).then_inc(x2_sq, 1)
                gain_low(n, 2 * i + (KD + b), ROW["norm_mix_2"])

            def end_pair(i, last):
                low("dn1b", i, 1)
                end_chunk(i, 0)
                low_next("dn1b", i, last)
                end_chunk(i, 1)

            clear_squares()
            v.memset(sqacc[:, 1, :], 0.0).then_inc(x2_sq, 1)
            with v.Fori(0, PAIRS["dn1b"] - 1) as i:
                dv.enter(i, 2)
                end_pair(i, False)
            dv.leave(PAIRS["dn1b"] - 1)
            end_pair(PAIRS["dn1b"] - 1, True)

            low("kv2", 0, 1)
            new_rms(3)
            dv.link(v.tensor_tensor(st[:, 9, 0:4], rs[:, 0:4], rs[:, 0:4], ALU.mult))
            dv.link(v.tensor_tensor(st[:, 9, 0:4], st[:, 9, 0:4], psT[:, 1, 4:8], ALU.mult))
            dv.link(v.tensor_scalar(st[:, 9, 0:4], st[:, 9, 0:4], 1.0 / D, EPS, ALU.mult, ALU.add))
            rsqrt(st[:, 9, 0:4], rs[:, 4:8], 4)
            dv.link(v.tensor_tensor(rs[:, 8:12], rs[:, 0:4], rs[:, 4:8], ALU.mult))
            diag2 = tmp[:, 0, :].rearrange("p (n c) -> p n c", n=NB)
            diagonals(diag, rs[:, 0:4])
            diagonals(diag2, rs[:, 8:12]).then_inc(diag_ok, 1)
            low_next("kv2", 0, False)
            v.wait_ge(bcast, 4)
            v.tensor_copy(tmp[:, 1, :], psT[:, 0, :])
            v.tensor_copy(R[:], psT[:, 1, :]).then_inc(R_ok, 1)
            v.wait_ge(R_ok, 4)
            keys = [kaT[:, c, :] for c in range(4)] + [vaT[:, c, :] for c in range(4)] + [kbT[:], vbT[:]]
            for i in range(PAIRS["kv2"]):
                if i:
                    low("kv2", i, 1)
                take_keys("kv2", i, 0, keys[2 * i])
                if i:
                    low_next("kv2", i, i == PAIRS["kv2"] - 1)
                take_keys("kv2", i, 1, keys[2 * i + 1])
                if i < 4:
                    for n in (2 * i, 2 * i + 1):
                        dv.link(v.tensor_tensor(hT[:, n, :], hT[:, n, :], tmp[:, 1, :], ALU.mult))
            v.wait_ge(dist_ok, 1)
            v.scalar_tensor_tensor(out=dist[:], in0=dist[:], scalar=-1.0, in1=dist[:], op0=ALU.mult, op1=ALU.max).then_inc(dist_ok, 1)
            v.wait_ge(dist_ok, 2)
            dv.link(v.tensor_scalar(tmp[:, 0, 0:WIN2], dist[:, NEAR:NEAR + WIN2], float(P), -NEG * 100, ALU.is_gt, ALU.mult))
            v.tensor_tensor(tmp[:, 0, 0:WIN2], tmp[:, 0, 0:WIN2], dist[:, NEAR:NEAR + WIN2], ALU.add).then_inc(dist_ok, 1)
            low("qa2", 0, 1)
            v.wait_ge(nat_t, 2)
            for h in range(4):
                v.tensor_copy(van[:, 0:NB, h * P:(h + 1) * P], psS[:, h, :].rearrange("p (c f) -> p c f", c=NB))
            v.tensor_copy(van[0:META, MC, :], psT[0:META, 0, :]).then_inc(nat_taken, 1)
            v.wait_ge(nat_t, 3)
            v.tensor_copy(vbn[:, 0:NB, :], psS[:, 0, :].rearrange("p (c f) -> p c f", c=NB))
            v.tensor_copy(vbn[0:META, MC, :], psT[0:META, 1, 0:P]).then_inc(nat_taken, 1)
            for name, dst in (("qa2", qaT), ("qb2", qbT)):
                for i in range(2):
                    if i or name == "qb2":
                        low(name, i, 1)
                    take_scaled(name, i, 0, dst[:, 2 * i, :], R[:], QSCALE)
                    low_next(name, i, i == 1)
                    take_scaled(name, i, 1, dst[:, 2 * i + 1, :], R[:], QSCALE)
            p = ph["df"]
            for j in range(16 + 4):
                if j < 16:
                    i, h = divmod(j, 4)
                    for m in range(2):
                        u = 2 * j + m
                        v.wait_ge(p["s"], u + 1)
                        v.wait_ge(biasD_ok, 4 * i + h + 1)
                        if j >= 3 and m == 0:
                            v.wait_ge(p["pt"], j - 2)
                        biased(p, u, as_halves(W6[:, j % 3, m, :], NKEY), two_banks(psS[:, 2 * m:2 * m + 2, :], NKEY),
                               as_halves(biasD[:, h, :], NKEY), TAKEN, u)
                if 1 <= j < 17:
                    u = j - 1
                    v.wait_ge(p["p"], 2 * u + 2)
                    dv.link(v.reciprocal(st[:, 6, 0:1], rsum[:, 2 * u + 1:2 * u + 2]))
                    dv.link(v.scalar_tensor_tensor(out=st[:, 6, 1:2], in0=rsum[:, 2 * u:2 * u + 1], scalar=st[:, 6, 0:1], in1=neglam[:],
                                                   op0=ALU.mult, op1=ALU.mult))
                    v.scalar_tensor_tensor(out=W6[:, u % 3, 0, :], in0=W6[:, u % 3, 1, :], scalar=st[:, 6, 1:2], in1=W6[:, u % 3, 0, :],
                                           op0=ALU.mult, op1=ALU.add).then_inc(df_sum, 1)
                if j >= 4 and (j - 4) % 4 == 3:
                    i = (j - 4) // 4
                    dv.link(v.reciprocal(st[:, 7, 0:4], rsum[:, 8 * i:8 * i + 8:2]))
                    v.wait_ge(p["pv"], 4 * (i + 1))
                    v.tensor_tensor(yn[:, i, :].rearrange("p (h d) -> p h d", h=4), psL[:, i % 2, :].rearrange("p (h d) -> p h d", h=4),
                                    spread(st[:, 7, 0:4], P), ALU.mult).then_inc(p["on"], 1)
            for i in range(NB):
                v.wait_ge(y_sq, 2 * i + 1)
                v.tensor_reduce(st[:, 8 + i // 2, 4 * (i % 2):4 * (i % 2) + 4], sq[:].rearrange("p (h d) -> p h d", h=4), AX_X, ALU.add).then_inc(y_sq, 1)
            v.wait_ge(y_sq, 2 * NB)
            s16 = st[:, 8:10, :].rearrange("p a b -> p (a b)")
            dv.link(v.tensor_scalar(s16, s16, 1.0 / P, EPS, ALU.mult, ALU.add))
            rsqrt(s16, rs[:], 16)
            y16 = yn[:].rearrange("p i (h d) -> p (i h) d", h=4)
            v.tensor_tensor(y16, y16, spread(rs[:], P), ALU.mult).then_inc(p["es"], 1)
            v.wait_ge(biasW_ok, NH)
            units = list(window2_units())
            p = ph["w2"]
            for j in range(len(units) + 5):
                if j < len(units):
                    i, h, _, n, _, _, b, _ = units[j]
                    W = n + META
                    v.wait_ge(p["s"], j + 1)
                    if j >= 3:
                        v.wait_ge(p["pt"], j - 2)
                    biased(p, j, W3b[:, j % 3, 0:W], psS[:, 2 * (j % 2), 0:W], biasW[:, h, b:b + W], sinkb[:, 1, h:h + 1], j)
                    if h == NH - 1:
                        sink_sum(p, 1, i)
                gate_part(2, j)
                if j >= 5 and (j - 5) % NH == NH - 1:
                    sink_normed(p, (j - 5) // NH, yw)
            for b in range(2):
                v.wait_ge(th_ok[b], 2 * KD)
            g = ROW["subln_gain_2"]
            heads_low(2, oA, gvec[:, g:g + 1])
            heads_low(3, oB)
            branches(2)
            out_project(2, 2, 2 * KD, ROW["norm_ffn_2"])
            swiglu("gu2a", 2 * NFH, (4, 5))
            down("dn2a")
            swiglu("gu2b", 3 * NFH)

            def last_pair(i, last):
                low("dn2b", i, 1)
                add_down("dn2b", i, 0)
                add_squares(3, 2 * i)
                low_next("dn2b", i, last)
                add_down("dn2b", i, 1)
                add_squares(3, 2 * i + 1)

            clear_squares()
            pairs("dn2b", last_pair)
            new_rms(5)
            for n in range(NB):
                if n >= 2:
                    v.wait_ge(fin_out[n % 2], 16)
                for half in range(2):
                    v.wait_ge(fin_t, 2 * n + half + 1)
                    v.tensor_scalar(yout[:, n % 2, half * 512:(half + 1) * 512], psS[:, 2 * (n % 2) + half, :], rs[:, n:n + 1], None,
                                    ALU.mult).then_inc(fin_ok, 1)

        @block.tensor
        def _(pe):
            def product(name, i, b, x, meta=None, made=None):
                pe.wait_ge(lo[b], PAIR0[name] + i + 1)
                if not (name == "kv1" and isinstance(i, int) and i == 0):
                    pe.wait_ge(ev[b], PAIR0[name] + i)
                kc = KC[name]
                if meta is not None:
                    for k in range(kc):
                        pe.matmul(psS[:, b, 0:META], stage[:, b, k * P:(k + 1) * P], metaT[:, meta, k, :], start=k == 0, stop=k == kc - 1)
                for k in range(kc):
                    if made:
                        pe.wait_ge(made[0], made[1] + k + 1)
                    for n, (w, part) in enumerate(((wh, 0), (wh, 1), (wl, 0))):
                        ins = pe.matmul(psL[:, b, :], w[:, b, k * P:(k + 1) * P], x[:, part, k, :], start=k + n == 0, stop=k == kc - 1 and n == 2)
                ins.then_inc(mm[b], 1)

            def products(name, x, first=0, meta=None, made=None):
                if made:
                    product(name, first, 0, x, made=made)
                    product(name, first, 1, x)
                    first += 1
                if PAIRS[name] - first > 2:
                    with pe.Fori(first, PAIRS[name]) as i:
                        for b in range(2):
                            product(name, i, b, x, meta=meta)
                else:
                    for i in range(first, PAIRS[name]):
                        for b in range(2):
                            product(name, i, b, x, meta=meta)

            def sums(which, col):
                for n in range(NB):
                    ins = pe.matmul(psT[:, 1, col + n:col + n + 1], which[:, n * P:(n + 1) * P], ones[:, 0:1], start=True, stop=True)
                return ins

            def spread_rms(bank, d):
                return pe.matmul(psT[:, bank, :], ones[:], d.rearrange("p n c -> p (n c)"), start=True, stop=True)

            pe.wait_ge(consts, 1)
            pe.wait_ge(rows_in, 16 * len(ROWS))
            pe.transpose(psT[:, 0, 0:NROWS], rows[:], ident[0:NROWS, 0:NROWS]).then_inc(gvec_t, 1)
            pe.wait_ge(tab_in, 48)
            pe.matmul(psL[0:NH, 0, 0:LEN_A], tab[:, 0:NH], hotA[:], start=True, stop=True).then_inc(f_mm, 1)
            pe.matmul(psL[0:NH, 1, :], tab[:, NH:2 * NH], hotB[:, 0:512], start=True, stop=True)
            pe.matmul(psT[0:NH, 1, 0:LEN_B - 512], tab[:, NH:2 * NH], hotB[:, 512:LEN_B], start=True, stop=True).then_inc(f_mm, 1)
            pe.wait_ge(x_in, 16 * NB)
            for k in range(KD):
                if k >= 4:
                    pe.wait_ge(x_taken, k - 3)
                for n in range(NB):
                    ins = pe.transpose(psS[:, k % 4, n * P:(n + 1) * P], xin[:, n, k * P:(k + 1) * P], ident[:])
                ins.then_inc(x_t, 1)
            pe.wait_ge(gvec_ok, 1)
            pe.wait_ge(meta_ok, 2)
            for l in range(2):
                for k in range(KD):
                    c = l * P + k * META
                    ins = pe.transpose(psT[:, 0, c:c + META], metain[:, l, k * P:(k + 1) * P], ident[0:META, 0:META])
            ins.then_inc(meta_t, 1)
            pe.wait_ge(fA_ok, 2)
            pe.wait_ge(diag_ok, 1)
            spread_rms(1, diag).then_inc(bcast, 1)
            pe.wait_ge(metaT_ok, 1)
            product("kv1", 0, 0, hn, meta=0, made=(xlo, 0))
            product("kv1", 0, 1, hn, meta=0)
            products("kv1", hn, first=1, meta=0)
            products("bq1", hn)
            pe.wait_ge(ev[1], PAIR0["kv1"] + 2)
            pe.wait_ge(ev[0], PAIR0["kv1"] + 2)
            pe.wait_ge(metaT_ok, 1)
            for n, src in enumerate((bkvT, ikwT, avT)):
                for c in range(NB):
                    pe.transpose(psS[:, n, c * P:(c + 1) * P], src[:, META + c * P:META + (c + 1) * P], ident[:])
                ins = pe.transpose(psT[0:META, 0, n * P:(n + 1) * P], src[:, 0:META], ident[:])
            ins.then_inc(nat_t, 1)
            products("iq1", hn)
            pe.wait_ge(ssq_in, 1)
            pe.wait_ge(R_ok, 1)
            sums(sq, 0).then_inc(ssq_mm, 1)
            products("aq1", hn)
            pe.wait_ge(nat_ok, 2)
            pe.wait_ge(nat_taken, 1)
            for n, src in enumerate((cn, ikn)):
                for c in range(NB):
                    pe.transpose(psS[:, n, c * P:(c + 1) * P], src[:, c, :], ident[:])
                pe.transpose(psT[:, 0, n * META:(n + 1) * META], src[0:META, MC, :], ident[0:META, 0:META])
            pe.wait_ge(wuk_in, 32)
            for c in range(4):
                ins = pe.transpose(psS[:, 2, c * P:(c + 1) * P], wuk[:, c * P:(c + 1) * P], ident[:])
            ins.then_inc(key_t, 1)
            pe.wait_ge(diag_ok, 2)
            spread_rms(1, diag).then_inc(bcast, 1)
            pe.wait_ge(bqlo, 2)
            products("uq1", bqg)
            pe.wait_ge(key_taken, 1)
            for u in range(4 * NB):
                i, h = divmod(u, 4)
                K = META + P * (i + 1)
                r = slice(h % 2 * HD, h % 2 * HD + HD)
                if u >= 2:
                    pe.wait_ge(lg_taken, u - 1)
                q = iqT[r, h // 2, i * P:(i + 1) * P]
                if K > 512:
                    pe.matmul(psS[:, 2 * (u % 2), 0:K // 2], q, ikT[r, 0:K // 2], start=True, stop=True)
                    ins = pe.matmul(psS[:, 2 * (u % 2) + 1, 0:K // 2], q, ikT[r, K // 2:K], start=True, stop=True)
                else:
                    ins = pe.matmul(psS[:, 2 * (u % 2), 0:K], q, ikT[r, 0:K], start=True, stop=True)
                ins.then_inc(lg_mm, 1)

            def gate_quarter(l, j, half):
                name, (i, b) = f"gates{l}", divmod(j // 2, 2)
                k0 = (2 * (j % 2) + half) * (KD // 4)
                if k0 == 0:
                    pe.wait_ge(lo[b], PAIR0[name] + i + 1)
                    pe.wait_ge(ev[b], PAIR0[name] + i)
                for k in range(k0, k0 + KD // 4):
                    for n, (w, part) in enumerate(((wh, 0), (wh, 1), (wl, 0))):
                        ins = pe.matmul(psL[:, b, :], w[:, b, k * P:(k + 1) * P], hn[:, part, k, :], start=k + n == 0, stop=k == KD - 1 and n == 2)
                if k0 + KD // 4 == KD:
                    ins.then_inc(mm[b], 1)

            def transposed(p, u, chunks, tile):
                if u:
                    pe.wait_ge(p["ptx"], u)
                n = 0
                for c, col, width in chunks:
                    if width == P:
                        ins = pe.transpose(psT[:, 0, n * P:(n + 1) * P], tile[:, col:col + P], ident[:])
                        n += 1
                    else:
                        pe.transpose(psT[0:META, 1, 0:P], tile[:, col:col + META], ident[:])
                ins.then_inc(p["pt"], 1)

            def pieces(chunks, pt):
                n, found = 0, []
                for c, _, width in chunks:
                    if width == P:
                        found.append((pt[:, n * P:(n + 1) * P], c, P))
                        n += 1
                    else:
                        found.append((pt[0:META, pt.shape[-1] - P:], c, META))
                return found

            def heads_out(m, src):
                for i in range(NB):
                    if m == 3:
                        pe.wait_ge(oT_taken, 2 * NB + i + 1)
                    for c in range(4):
                        ins = pe.transpose(psS[:, i, c * P:(c + 1) * P], src[:, i, c * P:(c + 1) * P], ident[:])
                    ins.then_inc(oT_mm, 1)

            pe.wait_ge(lg_taken, 4 * NB)
            units = list(window1_units())
            p = ph["w1"]
            for j in range(len(units) + 3):
                if j < len(units):
                    i, h, k0, W, _ = units[j]
                    r = slice(h // 4 * HD, h // 4 * HD + HD)
                    if j >= 2:
                        pe.wait_ge(p["neg"], j - 1)
                    pe.matmul(psS[:, 2 * (j % 2), 0:W], aqT[r, h % 4, i * P:(i + 1) * P], akT[r, k0:k0 + W], start=True, stop=True).then_inc(p["s"], 1)
                    gate_quarter(1, j, 0)
                if 2 <= j < len(units) + 2:
                    pe.wait_ge(p["p"], j - 1)
                    transposed(p, j - 2, units[j - 2][4], W3a[:, (j - 2) % 3, :])
                if j < len(units):
                    gate_quarter(1, j, 1)
                if j >= 3:
                    u = j - 3
                    i, h = units[u][:2]
                    pe.wait_ge(p["ptx"], u + 1)
                    if h == 0 and i >= 2:
                        pe.wait_ge(p["on"], i - 1)
                    parts = pieces(units[u][4], PTa[:, u % 2, :])
                    for n, (pt, c, w) in enumerate(parts):
                        ins = pe.matmul(psS[:, 2 * (i % 2) + 1, h * HD:(h + 1) * HD], pt, avn[0:w, c, h // 4 * HD:h // 4 * HD + HD],
                                        start=n == 0, stop=n == len(parts) - 1)
                    ins.then_inc(p["pv"], 1)
            pe.wait_ge(p["on"], NB)
            heads_out(0, on)
            for b in range(2):
                pe.wait_ge(ev[b], PAIR0["br1"])
            for h in range(NH):
                r = slice(h % 2 * HD, h % 2 * HD + HD)
                if h >= 2:
                    pe.wait_ge(qabs_ok, h - 1)
                pe.matmul(psL[:, h % 2, :], wukT[r, h // 2, :], qT[r, h // 2, :], start=True, stop=True).then_inc(qabs_mm, 1)
            pe.wait_ge(qabs_ok, NH)
            pe.wait_ge(sel_ok, NB)
            pe.wait_ge(oT_taken, NB)
            pe.wait_ge(o_lo, NB)
            units = list(latent_units())
            p = ph["la"]
            for j in range(len(units) + 5):
                if j < len(units):
                    i, h, K, _ = units[j]
                    if j >= 2:
                        pe.wait_ge(p["neg"], j - 1)
                    q = qabs[:, h, i * P:(i + 1) * P]
                    cuts = [(0, 0, K)] if K <= 512 else [(0, 0, K // 2), (1, K // 2, K)]
                    for bank, k0, k1 in cuts:
                        dst = psS[:, 2 * (j % 2) + bank, 0:k1 - k0]
                        pe.matmul(dst, q, cT[:, k0:k1], start=True, stop=False)
                        ins = pe.matmul(dst, identb[:], selm[:, i, k0:k1], start=False, stop=True)
                    ins.then_inc(p["s"], 1)
                if 2 <= j < len(units) + 2:
                    pe.wait_ge(p["p"], j - 1)
                    transposed(p, j - 2, units[j - 2][3], W3[:, (j - 2) % 3, :])
                if j >= 4 and j - 4 < len(units):
                    u = j - 4
                    i, h = units[u][:2]
                    pe.wait_ge(p["lat"], u + 1)
                    if h == 0 and i:
                        pe.wait_ge(p["on"], i)
                    pe.matmul(psL[:, 1, h * HD:(h + 1) * HD], lat[:, u % 2, :], wuv[:, h * HD:(h + 1) * HD], start=True, stop=True).then_inc(p["o"], 1)
                if 3 <= j < len(units) + 3:
                    u = j - 3
                    pe.wait_ge(p["ptx"], u + 1)
                    if u:
                        pe.wait_ge(p["lat"], u)
                    parts = pieces(units[u][3], PT[:, u % 2, :])
                    for n, (pt, c, w) in enumerate(parts):
                        ins = pe.matmul(psL[:, 0, 0:P], cn[0:w, c, :], pt, start=n == 0, stop=n == len(parts) - 1)
                    ins.then_inc(p["pv"], 1)
            pe.wait_ge(p["on"], NB)
            heads_out(1, on)
            pe.wait_ge(o_lo, 2 * NB)

            def layer_rest(l, ssq0, norm):
                name = f"br{l}"
                with pe.Fori(0, PAIRS[name]) as i:
                    product(name, i, 0, oA)
                    product(name, i, 1, oB)
                products(f"out{l}", mix, made=(mix_lo, KD * (l - 1)))
                name = f"gu{l}a"
                product(name, 0, 0, hn, made=(hg_lo, KD * (2 * l - 2)))
                pe.wait_ge(h_sq2, squares_cleared(norm) + KD)
                pe.wait_ge(R_ok, ssq0)
                sums(sqacc[:, 0, :], 0).then_inc(ssq_mm, 1)
                product(name, 0, 1, hn)
                pe.wait_ge(diag_ok, ssq0 + 1)
                spread_rms(1, diag).then_inc(bcast, 1)
                products(name, hn, first=1)
                products(f"dn{l}a", hid, made=(hid_lo, NFH * (2 * l - 2)))
                products(f"gu{l}b", hn)
                products(f"dn{l}b", hid, made=(hid_lo, NFH * (2 * l - 1)))

            layer_rest(1, 2, 0)
            product("kv2", 0, 0, hn, meta=1, made=(hg_lo, KD))
            pe.wait_ge(h_sq2, squares_cleared(1) + KD)
            pe.wait_ge(x2_sq, 1 + KD)
            pe.wait_ge(R_ok, 3)
            sums(sqacc[:, 0, :], 0)
            sums(sqacc[:, 1, :], NB).then_inc(ssq_mm, 1)
            product("kv2", 0, 1, hn, meta=1)
            pe.wait_ge(diag_ok, 4)
            spread_rms(0, diag)
            spread_rms(1, tmp[:, 0, :].rearrange("p (n c) -> p n c", n=NB)).then_inc(bcast, 1)
            products("kv2", hn, first=1, meta=1)
            product("qa2", 0, 0, hn)
            for b in range(2):
                pe.wait_ge(ev[b], PAIR0["qa2"])
            for h in range(4):
                for c in range(NB):
                    pe.transpose(psS[:, h, c * P:(c + 1) * P], vaT[:, h, META + c * P:META + (c + 1) * P], ident[:])
                ins = pe.transpose(psT[0:META, 0, h * P:(h + 1) * P], vaT[:, h, 0:META], ident[:])
            ins.then_inc(nat_t, 1)
            product("qa2", 0, 1, hn)
            pe.wait_ge(nat_taken, 2)
            pe.wait_ge(R_ok, 4)
            for c in range(NB):
                pe.transpose(psS[:, 0, c * P:(c + 1) * P], vbT[:, META + c * P:META + (c + 1) * P], ident[:])
            pe.transpose(psT[0:META, 1, 0:P], vbT[:, 0:META], ident[:]).then_inc(nat_t, 1)
            products("qa2", hn, first=1)
            products("qb2", hn)
            for b in range(2):
                pe.wait_ge(ev[b], PAIR0["gates2"])
            pe.wait_ge(nat_taken, 3)
            p = ph["df"]
            all_keys = [(MC, 0, META)] + [(c, META + P * c, P) for c in range(NB)]
            for j in range(16 + 3):
                if j < 16:
                    i, h = divmod(j, 4)
                    for m in range(2):
                        u = 2 * j + m
                        r = slice(m * HD, (m + 1) * HD)
                        if u >= 2:
                            pe.wait_ge(p["neg"], u - 1)
                        q = qaT[r, h, i * P:(i + 1) * P]
                        pe.matmul(psS[:, 2 * m, 0:NKEY // 2], q, kaT[r, h, 0:NKEY // 2], start=True, stop=True)
                        pe.matmul(psS[:, 2 * m + 1, 0:NKEY // 2], q, kaT[r, h, NKEY // 2:NKEY], start=True, stop=True).then_inc(p["s"], 1)
                if 2 <= j < 18:
                    pe.wait_ge(df_sum, j - 1)
                    transposed(p, j - 2, all_keys, W6[:, (j - 2) % 3, 0, :])
                if j >= 3:
                    u = j - 3
                    i, h = divmod(u, 4)
                    pe.wait_ge(p["ptx"], u + 1)
                    if h == 0 and i >= 2:
                        pe.wait_ge(p["on"], i - 1)
                    parts = pieces(all_keys, PT2[:, u % 2, :])
                    for n, (pt, c, w) in enumerate(parts):
                        ins = pe.matmul(psL[:, i % 2, h * P:(h + 1) * P], pt, van[0:w, c, h * P:(h + 1) * P], start=n == 0, stop=n == len(parts) - 1)
                    ins.then_inc(p["pv"], 1)
            pe.wait_ge(p["on"], NB)
            units = list(window2_units())
            p = ph["w2"]
            for j in range(len(units) + 4):
                if j < len(units):
                    i, h, lo_c, W, wcol, mcol, _, _ = units[j]
                    r = slice(h // 4 * HD, h // 4 * HD + HD)
                    if j >= 2:
                        pe.wait_ge(p["neg"], j - 1)
                    q = qbT[r, h % 4, i * P:(i + 1) * P]
                    pe.matmul(psS[:, 2 * (j % 2), mcol:mcol + META], q, kbT[r, 0:META], start=True, stop=True)
                    k0 = META + P * lo_c
                    pe.matmul(psS[:, 2 * (j % 2), wcol:wcol + W], q, kbT[r, k0:k0 + W], start=True, stop=True).then_inc(p["s"], 1)
                    gate_quarter(2, j, 0)
                if 2 <= j < len(units) + 2:
                    pe.wait_ge(p["p"], j - 1)
                    transposed(p, j - 2, units[j - 2][7], W3b[:, (j - 2) % 3, :])
                if j < len(units):
                    gate_quarter(2, j, 1)
                if 3 <= j < len(units) + 3:
                    u = j - 3
                    i, h = units[u][:2]
                    pe.wait_ge(p["ptx"], u + 1)
                    if h == 0 and i >= 2:
                        pe.wait_ge(p["on"], i - 1)
                    parts = pieces(units[u][7], PTb[:, u % 2, :])
                    for n, (pt, c, w) in enumerate(parts):
                        ins = pe.matmul(psS[:, 2 * (i % 2) + 1, h * HD:(h + 1) * HD], pt, vbn[0:w, c, h // 4 * HD:h // 4 * HD + HD],
                                        start=n == 0, stop=n == len(parts) - 1)
                    ins.then_inc(p["pv"], 1)
            pe.wait_ge(p["on"], NB)
            pe.wait_ge(ph["df"]["es"], 1)
            heads_out(2, yn)
            heads_out(3, yw)
            pe.wait_ge(o_lo, 4 * NB)
            layer_rest(2, 4, 2)
            pe.wait_ge(h_sq2, squares_cleared(3) + KD)
            pe.wait_ge(R_ok, 5)
            sums(sqacc[:, 0, :], 0).then_inc(ssq_mm, 1)
            pe.wait_ge(fin_gain, KD)
            for n in range(NB):
                if n >= 2:
                    pe.wait_ge(fin_ok, 2 * (n - 1))
                for half in range(2):
                    for c in range(4):
                        ins = pe.transpose(psS[:, 2 * (n % 2) + half, c * P:(c + 1) * P], hgf[:, 4 * half + c, n * P:(n + 1) * P], ident[:])
                    ins.then_inc(fin_t, 1)


_INS = ["x", "meta_tokens", "attn_norm_g", "w_in", "b_gates", "q_norm_g", "kv_norm_g", "w_uq", "w_uk", "w_uv",
        "idx_k_ln_g", "idx_k_ln_b", "sinks", "rel_bias", "w_branch_a", "w_branch_b", "w_out", "ffn_norm_g",
        "w_ffn_gate", "w_ffn_up", "w_ffn_down", "final_norm_g", "meta_tokens_2", "norm_mix_2", "w_in_2",
        "lambda_q1_2", "lambda_k1_2", "lambda_q2_2", "lambda_k2_2", "subln_gain_2", "sink_logits_2",
        "w_branch_a_2", "w_branch_b_2", "w_out_2", "norm_ffn_2", "w_ff_gate_2", "w_ff_up_2", "w_ff_down_2",
        "norm_final_2"]


def kernel(**inputs):
    import concourse.bacc as _bacc
    from concourse.bass_utils import run_bass_kernel_spmd as _run

    nc = _bacc.Bacc("TRN2", target_bir_lowering=False, num_devices=1)
    arrays, t = {}, {}
    for name in _INS:
        a = np.ascontiguousarray(inputs[name])
        arrays[f"in_{name}"] = a
        t[name] = nc.dram_tensor(f"in_{name}", a.shape, mybir.dt.from_np(a.dtype), kind="ExternalInput").ap()
    for name, a in zip(("hot_a", "hot_b"), bucket_rows()):
        arrays[f"const_{name}"] = a
        t[name] = nc.dram_tensor(f"const_{name}", a.shape, F32, kind="ExternalInput").ap()
    out = nc.dram_tensor("out_0", (1, SEQ, D), F32, kind="ExternalOutput").ap()
    build(nc, t, out)
    r = _run(nc, [arrays], core_ids=[0])
    return r.results[0]["out_0"]
```

```python
from contextlib import ExitStack

import numpy as np

import concourse.bass as bass
from concourse import mybir

F32 = mybir.dt.float32
F32R = mybir.dt.float32r
BF16 = mybir.dt.bfloat16
I32 = mybir.dt.int32
ACT = mybir.ActivationFunctionType
ALU = mybir.AluOpType
AX_X = mybir.AxisListType.X

P = 128
D = 1024
KD = D // P
SEQ = 512
NB = SEQ // P
META = 16
NKEY = META + SEQ
MC = NB
FF = 2816
NFH = FF // P // 2
HD = 64
NH = 8
EPS = 1e-6
NEG = -1e30
TAKEN = -3e38
TOPK = 128
BUCKETS = 32
QSCALE = HD ** -0.5
LAMBDA0 = 0.8 - 0.6
RSQRT_SEED = float(0x5F3759DF)

NEAR = 2 * P
LEN_A = NEAR + P - 1
LEN_B = NKEY + P - 1
WIN2 = 3 * P
DIST = 7 * P


def bucket(dist):
    exact = BUCKETS // 2
    d = np.maximum(dist, 1).astype(np.float32)
    span = np.float32(np.log(128 / exact))
    large = exact + (np.log(d / np.float32(exact)) / span * np.float32(BUCKETS - exact)).astype(np.int32)
    return np.where(dist < exact, dist, np.minimum(large, BUCKETS - 1))


def bucket_rows():
    out = []
    for length, far in ((LEN_A, P), (LEN_B, 1 << 20)):
        dist = (length - P) - np.arange(length)
        dead = (dist < 0) | (dist >= far)
        hot = np.zeros((BUCKETS + 1, length), np.float32)
        live = np.flatnonzero(~dead)
        hot[bucket(dist[live]), live] = 1.0
        hot[BUCKETS, dead] = 1.0
        out.append(hot)
    return out


PHASES = [("kv1", 4, KD, 1), ("bq1", 2, KD, 1), ("iq1", 2, KD, 1), ("aq1", 4, KD, 2), ("uq1", 4, 2, 1),
          ("gates1", 2 * KD, KD, 1), ("br1", 2 * KD, 4, 1), ("out1", KD, KD, 1),
          ("gu1a", 2 * NFH, KD, 1), ("dn1a", KD, NFH, 1), ("gu1b", 2 * NFH, KD, 1), ("dn1b", KD, NFH, 1),
          ("kv2", 10, KD, 1), ("qa2", 4, KD, 1), ("qb2", 4, KD, 2),
          ("gates2", 2 * KD, KD, 1), ("br2", 2 * KD, 4, 1), ("out2", KD, KD, 1),
          ("gu2a", 2 * NFH, KD, 1), ("dn2a", KD, NFH, 1), ("gu2b", 2 * NFH, KD, 1), ("dn2b", KD, NFH, 1)]
KC = {n: kc for n, _, kc, _ in PHASES}
PAIRS = {n: s // 2 for n, s, _, _ in PHASES}
LOADS = {n: d for n, _, _, d in PHASES}
PAIR0, LOAD0, AFTER = {}, {}, {}
_pairs = _loads = 0
for _i, (_n, _s, _kc, _d) in enumerate(PHASES):
    PAIR0[_n], LOAD0[_n] = _pairs, _loads
    AFTER[_n] = PHASES[_i + 1][0] if _i + 1 < len(PHASES) else None
    _pairs += _s // 2
    _loads += _s // 2 * _d

POOL_LOW = ("iq1", "aq1", "uq1", "gates1", "br1", "qa2", "qb2", "gates2", "br2")

ROWS = [("attn_norm_g", KD), ("ffn_norm_g", KD), ("final_norm_g", KD), ("norm_mix_2", KD), ("norm_ffn_2", KD),
        ("norm_final_2", KD), ("b_gates", 2 * KD), ("q_norm_g", 2), ("subln_gain_2", 1)]
ROW = {}
NROWS = 0
for _n, _s in ROWS:
    ROW[_n] = NROWS
    NROWS += _s


def squares_cleared(norm):
    return norm * (KD + 1) + 1


class Tally:

    def __init__(self, eng, sem):
        self.eng, self.sem, self.n, self.off = eng, sem, 0, 0

    def link(self, ins):
        ins.then_inc(self.sem, 1)
        self.n += 1
        self.eng.wait_ge(self.sem, self.off + self.n)

    def enter(self, i, per):
        self.off, self.start, self.per = i * per, self.n, per

    def leave(self, count):
        assert self.n - self.start == self.per, (self.n - self.start, self.per)
        self.off, self.n = 0, self.start + self.per * count


def window1_units():
    for i in range(NB):
        for h in range(NH):
            if i == 0:
                yield i, h, 0, META + P, [(MC, 0, META), (0, META, P)]
            else:
                yield i, h, META + P * (i - 1), NEAR, [(i - 1, 0, P), (i, P, P)]


def latent_units():
    for i in range(NB):
        for h in range(NH):
            yield i, h, META + P * (i + 1), [(MC, 0, META)] + [(c, META + P * c, P) for c in range(i + 1)]


def window2_units():
    for i in range(NB):
        lo, hi = max(i - 1, 0), min(i + 1, NB - 1)
        n = hi - lo + 1
        w, m, bias = (0, n * P, META + P) if i == 0 else (META, 0, 0)
        for h in range(NH):
            yield i, h, lo, n * P, w, m, bias, [(MC, m, META)] + [(lo + c, w + P * c, P) for c in range(n)]


def two_banks(ap, width):
    return ap[:, :, 0:width // 2] if width > 512 else ap[:, 0, 0:width]


def as_halves(ap, width):
    return ap.rearrange("p (a b) -> p a b", a=2) if width > 512 else ap


GATE_QUARTERS = {1: [2] * 29 + [1] * 6, 2: [4] + [2] * 24 + [1] * 10 + [2]}
GATE_START = {l: [n for n, c in enumerate(q) for _ in range(c)][0::4] for l, q in GATE_QUARTERS.items()}
GATE_DONE = {l: [n for n, c in enumerate(q) for _ in range(c)][3::4] for l, q in GATE_QUARTERS.items()}
assert all(sum(q) == 4 * 2 * KD for q in GATE_QUARTERS.values())


Y_NORM = [8, 10, 12, 14]


def build(nc, t, out):
    with ExitStack() as ctx:
        def sem(name):
            return ctx.enter_context(nc.semaphore(name))

        base = -(-nc.sbuf_base // 32) * 32
        top = [base]
        size = {F32: 4, F32R: 4, BF16: 2, I32: 4}

        def at(name, shape, offset, dt=F32):
            n = int(np.prod(shape[1:])) * size[dt]
            assert offset + n <= nc.sbuf_usable_end, (name, offset + n - nc.sbuf_usable_end)
            return nc.alloc_sbuf_tensor_at(name, shape, dt, offset=offset), -(-(offset + n) // 32) * 32

        def keep(name, shape, dt=F32):
            tensor, top[0] = at(name, shape, top[0], dt)
            return tensor

        hT = keep("hT", [P, KD, SEQ])
        stage = keep("stage", [P, 2, NFH * P])
        wh = keep("wh", [P, 2, NFH * P], F32R)
        wl = keep("wl", [P, 2, NFH * P], F32R)
        R = keep("R", [P, SEQ])
        tmp = keep("tmp", [P, 2, SEQ])
        ident = keep("ident", [P, P])
        identb = keep("identb", [P, P], BF16)
        ones = keep("ones", [P, P])
        gvec = keep("gvec", [P, NROWS])
        bhalf = keep("bhalf", [P, 2 * KD])
        kvg = keep("kvg", [P, P])
        ikg = keep("ikg", [P, 2, HD])
        sinkb = keep("sinkb", [P, 2, NH])
        tab = keep("tab", [BUCKETS + 1, 2 * NH])
        wuv = keep("wuv", [P, NH * HD])
        wukT = keep("wukT", [P, 4, P])
        metaT = keep("metaT", [P, 2, KD, META])
        iwn = keep("iwn", [P, NB, 4])
        mx = keep("mx", [P, 2 * NB * NH])
        negm = keep("negm", [P, 2 * NB * NH])
        rsum = keep("rsum", [P, 2 * NB * NH])
        st = keep("st", [P, 12, NH])
        rst = keep("rst", [P, 16])
        rsti = keep("rsti", [P, 16], I32)
        rs = keep("rs", [P, 16])
        lam = keep("lam", [P, 4])
        neglam = keep("neglam", [P, 1])
        subg = keep("subg", [P, 1])

        gate0 = top[0]
        gate = keep("gate", [P, 2 * KD, SEQ])
        xin, o = at("xin", [P, NB, D], gate0)
        metain, o = at("metain", [META, 2, D], o)
        junk, o = at("junk", [P, D], o)
        wuk, o = at("wuk", [P, NH * HD], o)
        rows, o = at("rows", [NROWS, P], o)
        lam4, o = at("lam4", [P, 4, HD], o)
        lamj, o = at("lamj", [P, HD], o)
        assert o <= top[0]

        hn0 = top[0]
        hn = keep("hn", [P, 2, KD, SEQ], F32R)
        oA, o = at("oA", [P, 2, 4, SEQ], hn0, F32R)
        oB, _ = at("oB", [P, 2, 4, SEQ], o, F32R)
        W3, o = at("W3", [P, 3, NKEY], o)
        PT, o = at("PT", [P, 2, (NB + 1) * P], o)
        lat, o = at("lat", [P, 2, P], o)
        assert o <= top[0]
        W6, o = at("W6", [P, 3, 2, NKEY], gate0)
        PT2, o = at("PT2", [P, 2, (NB + 1) * P], o)
        assert o <= hn0

        ar0 = top[0]
        squares, _ = at("squares", [P, D], ar0)
        aqT, o = at("aqT", [P, 4, SEQ], ar0)
        biasA, o = at("biasA", [P, NH, NEAR], o)
        qabs, _ = at("qabs", [P, NH, SEQ], ar0)
        biasB, o = at("biasB", [P, NH, NKEY], o)
        akT, o = at("akT", [P, NKEY], o)
        avn, o = at("avn", [P, NB + 1, P], o)
        cT, o = at("cT", [P, NKEY], o)
        cn, o = at("cn", [P, NB + 1, P], o)
        o1 = o
        bqT, o = at("bqT", [P, 2, SEQ], o)
        bqg, o = at("bqg", [P, 2, 2, SEQ], o, F32R)
        acc, o = at("acc", [P, NB, NKEY], o1)
        W3a, o = at("W3a", [P, 3, NEAR], o)
        o2 = max(o, o1 + 3 * 4 * SEQ * 2)
        bkvT, o = at("bkvT", [P, NKEY], o2)
        ikwT, o = at("ikwT", [P, NKEY], o)
        avT, o = at("avT", [P, NKEY], o)
        ikn, o = at("ikn", [P, NB + 1, P], o)
        ikx, o = at("ikx", [P, NB + 1, HD], o)
        iqT, o3 = at("iqT", [P, 2, SEQ], o2)
        ikT, o3 = at("ikT", [P, NKEY], o3)
        relu, o3 = at("relu", [P, 2, NKEY], o3)
        on, o4 = at("on", [P, NB, SEQ], o2)
        PTa, o4 = at("PTa", [P, 2, NEAR + P], o4)
        o = max(o, o3)
        causal, o = at("causal", [P, NKEY], o)
        assert o4 <= o
        tail = o
        qT, o = at("qT", [P, 4, SEQ], tail)
        selm, _ = at("selm", [P, NB, NKEY], o, BF16)
        diag, o6 = at("diag", [P, NB, P], o)
        sq, o6 = at("sq", [P, SEQ], o6)
        sqacc, _ = at("sqacc", [P, 2, SEQ], tail)
        hotA, o5 = at("hotA", [BUCKETS + 1, LEN_A], tail)
        hotB, o5 = at("hotB", [BUCKETS + 1, LEN_B], o5)
        assert o5 <= o
        fA, o7 = at("fA", [NH, LEN_A], gate0)
        fB, o7 = at("fB", [NH, LEN_B], o7)
        qaT, o = at("qaT", [P, 4, SEQ], ar0)
        kaT, o = at("kaT", [P, 4, NKEY], o)
        kbT, o = at("kbT", [P, NKEY], o)
        yw, _ = at("yw", [P, NB, SEQ], o)
        van, o = at("van", [P, NB + 1, SEQ], o)
        vbn, o = at("vbn", [P, NB + 1, P], o)
        qbT, o = at("qbT", [P, 4, SEQ], o)
        dist, o = at("dist", [P, DIST], o)
        biasD, o = at("biasD", [P, 4, NKEY], o)
        o1 = o
        biasW, o = at("biasW", [P, NH, META + WIN2 + META], o1)
        vaT, o2 = at("vaT", [P, 4, NKEY], o1)
        vbT, o2 = at("vbT", [P, NKEY], o2)
        assert max(o, o2) <= tail
        yn, _ = at("yn", [P, NB, SEQ], tail)
        W3b, o = at("W3b", [P, 3, META + WIN2], ar0)
        PTb, o = at("PTb", [P, 2, WIN2 + P], o)
        mix, o = at("mix", [P, 2, KD, SEQ], ar0, F32R)
        mix32, _ = at("mix32", [P, 3, SEQ], o)
        hid, o = at("hid", [P, 2, NFH, SEQ], ar0, F32R)
        ft, o = at("ft", [P, 5, SEQ], o)
        assert o <= tail
        hgf, _ = at("hgf", [P, KD, SEQ], hn0)
        yout, _ = at("yout", [P, 2, D], gate0)

        psL = ctx.enter_context(nc.psum_tensor("psL", [P, 2, 512], F32))
        psS = ctx.enter_context(nc.psum_tensor("psS", [P, 4, 512], F32))

        def o_bank(i):
            return psS[:, 1, :] if i == 1 else psL[:, 1, :]

        psT = ctx.enter_context(nc.psum_tensor("psT", [P, 2, 512], F32))

        fA_dram = nc.dram_tensor("bias_by_distance_A", [NH, P, LEN_A + 1], F32).ap()
        fB_dram = nc.dram_tensor("bias_by_distance_B", [NH, P, LEN_B + 1], F32).ap()

        w_in = [sem(f"w_in{b}") for b in range(2)]
        hi = [sem(f"hi{b}") for b in range(2)]
        lo = [sem(f"lo{b}") for b in range(2)]
        mm = [sem(f"mm{b}") for b in range(2)]
        ev = [sem(f"ev{b}") for b in range(2)]
        x_in = [sem(f"x_in{q}") for q in range(4)]
        dve_own = sem("dve_own")
        pool_own = sem("pool_own")
        meta_in, g1_in, rows_in, tab_in, vec_in, wuk_in, lam_in, lam_sum = [
            sem(n) for n in "meta_in g1_in rows_in tab_in vec_in wuk_in lam_in lam_sum".split()]
        consts, zeros, gvec_t, gvec_ok, x_t, x_taken, xhi, xlo, x_sq, meta_sq, meta_ok, meta_t, metaT_ok = [
            sem(n) for n in "consts zeros gvec_t gvec_ok x_t x_taken xhi xlo x_sq meta_sq meta_ok meta_t metaT_ok".split()]
        f_mm, fA_ok, f_out, bias_in = [sem(n) for n in "f_mm fA_ok f_out bias_in".split()]
        diag_ok, bcast, R_ok, ssq_in, ssq_mm = [
            sem(n) for n in "diag_ok bcast R_ok ssq_in ssq_mm".split()]
        nat_t, nat_taken, nat_ok, key_t, key_taken, bqhi, bqlo = [
            sem(n) for n in "nat_t nat_taken nat_ok key_t key_taken bqhi bqlo".split()]
        lg_mm, lg_taken, lg_used = [sem(n) for n in "lg_mm lg_taken lg_used".split()]
        sel_ok, qabs_mm, qabs_ok = [sem(n) for n in "sel_ok qabs_mm qabs_ok".split()]
        th_ok = [sem(f"th_ok{b}") for b in range(2)]
        ph = {}
        for n in ("w1", "la", "df", "w2"):
            ph[n] = {k: sem(f"{n}_{k}") for k in "s neg p pt ptx pv lat o es on".split()}
        oT_mm, o_hi, o_lo = [sem(n) for n in "oT_mm o_hi o_lo".split()]
        mix_ok, mix_hi, mix_lo, t_ok, hid_ok, hid_hi, hid_lo = [
            sem(n) for n in "mix_ok mix_hi mix_lo t_ok hid_ok hid_hi hid_lo".split()]
        h_sq, h_sq2, x2_sq, h_gain, hg_hi, hg_lo = [sem(n) for n in "h_sq h_sq2 x2_sq h_gain hg_hi hg_lo".split()]
        biasD_ok, biasW_ok, dist_ok, df_sum, y_sq, lam_e = [
            sem(n) for n in "biasD_ok biasW_ok dist_ok df_sum y_sq lam_e".split()]
        fin_gain, fin_t, fin_ok, fin_out = sem("fin_gain"), sem("fin_t"), sem("fin_ok"), [sem("fin_out0"), sem("fin_out1")]

        block = ctx.enter_context(nc.Block())

        def by_rows(w, k0=0, kc=None):
            v = w.rearrange("(k p) n -> p k n", p=P)
            return v if kc is None else v[:, k0:k0 + kc, :]

        win1, win2 = by_rows(t["w_in"][0]), by_rows(t["w_in_2"][0])

        @block.sync
        def _(sp):
            def load(name, i, b, src, col, piece=0, width=P):
                kc = KC[name]
                slot = stage[:, b, 0:kc * P].rearrange("p (k n) -> p k n", k=kc)
                if piece == 0 and not (name == "kv1" and isinstance(i, int) and i == 0):
                    sp.wait_ge(lo[b], PAIR0[name] + i)
                    if name in ("kv1", "bq1", "kv2", "qa2"):
                        sp.wait_ge(mm[b], PAIR0[name] + i)
                sp.dma_start(slot[:, :, piece:piece + width], src[:, :, bass.ds(col, width)]).then_inc(w_in[b], 16)

            kv_cols = (1024, 1408, 512, 640)
            XQ = D // 4
            for q in range(4):
                sp.dma_start(xin[:, :, q * XQ:(q + 1) * XQ], t["x"][0].rearrange("(n p) d -> p n d", p=P)[:, :, q * XQ:(q + 1) * XQ]).then_inc(x_in[q], 16)
                if q == 0:
                    load("kv1", 0, 0, win1, kv_cols[0])
            load("kv1", 0, 1, win1, kv_cols[1])
            for name, n in ROWS[1:]:
                src = t[name].rearrange("a (k p) -> (a k) p", p=P) if len(t[name].shape) == 2 else t[name].rearrange("(k p) -> k p", p=P)
                sp.dma_start(rows[ROW[name]:ROW[name] + n, :], src).then_inc(rows_in, 16)
            sp.dma_start(tab[0:BUCKETS, :], t["rel_bias"]).then_inc(tab_in, 16)
            sp.dma_start(hotA[:], t["hot_a"]).then_inc(tab_in, 16)
            sp.dma_start(hotB[:], t["hot_b"]).then_inc(tab_in, 16)
            for n in range(2, 4):
                load("kv1", 1, n % 2, win1, kv_cols[n])
            sp.dma_start(wuk[:], t["w_uk"][0].rearrange("c h d -> c (h d)")).then_inc(wuk_in, 16)
            sp.dma_start(wuv[:], t["w_uv"][0].rearrange("c h d -> c (h d)")).then_inc(wuk_in, 16)
            for n in range(2):
                load("bq1", 0, n, win1, 768 + n * P)
            for n in range(2):
                load("iq1", 0, n, win1, 1152 + n * P)
            for n in range(4):
                for half in range(2):
                    load("aq1", n // 2, n % 2, win1, (n + 4 * half) * HD, half * HD, HD)
            for n in range(4):
                load("uq1", n // 2, n % 2, by_rows(t["w_uq"][0]), n * P)

            def layer_rest(l, win, gates_at, wa, wb, wo, wg, wu, wd):
                with sp.Fori(0, PAIRS[f"gates{l}"]) as i:
                    for b in range(2):
                        load(f"gates{l}", i, b, win, i * (2 * P) + (gates_at + b * P))
                with sp.Fori(0, PAIRS[f"br{l}"]) as i:
                    load(f"br{l}", i, 0, by_rows(wa), i * P)
                    load(f"br{l}", i, 1, by_rows(wb), i * P)
                with sp.Fori(0, PAIRS[f"out{l}"]) as i:
                    for b in range(2):
                        load(f"out{l}", i, b, by_rows(wo), i * (2 * P) + b * P)
                for half, ab in enumerate("ab"):
                    with sp.Fori(0, PAIRS[f"gu{l}{ab}"]) as i:
                        load(f"gu{l}{ab}", i, 0, by_rows(wg), i * P + half * NFH * P)
                        load(f"gu{l}{ab}", i, 1, by_rows(wu), i * P + half * NFH * P)
                    with sp.Fori(0, PAIRS[f"dn{l}{ab}"]) as i:
                        for b in range(2):
                            load(f"dn{l}{ab}", i, b, by_rows(wd, half * NFH, NFH), i * (2 * P) + b * P)

            layer_rest(1, win1, 1476, t["w_branch_a"][0], t["w_branch_b"][0], t["w_out"][0],
                       t["w_ffn_gate"][0], t["w_ffn_up"][0], t["w_ffn_down"][0])
            with sp.Fori(0, PAIRS["kv2"] - 1) as i:
                for b in range(2):
                    load("kv2", i, b, win2, i * (2 * P) + (512 + b * P))
            for b in range(2):
                load("kv2", PAIRS["kv2"] - 1, b, win2, 2048 + b * P)
            with sp.Fori(0, PAIRS["qa2"]) as i:
                for b in range(2):
                    load("qa2", i, b, win2, i * (2 * P) + b * P)
            for n in range(4):
                for half in range(2):
                    load("qb2", n // 2, n % 2, win2, 1536 + (n + 4 * half) * HD, half * HD, HD)
            layer_rest(2, win2, 2304, t["w_branch_a_2"][0], t["w_branch_b_2"][0], t["w_out_2"][0],
                       t["w_ff_gate_2"][0], t["w_ff_up_2"][0], t["w_ff_down_2"][0])
            for n in range(NB):
                sp.wait_ge(fin_ok, 2 * n + 2)
                sp.dma_start(out[0, n * P:(n + 1) * P, :], yout[:, n % 2, :]).then_inc(fin_out[n % 2], 16)
            sp.wait_ge(fin_out[0], 32)
            sp.wait_ge(fin_out[1], 32)

        @block.gpsimd
        def _(pool):
            own = Tally(pool, pool_own)
            own.link(pool.memset(ident[:], 0.0))
            own.link(pool.affine_select(out=ident[:], in_=ident[:], compare_op=ALU.not_equal, fill=1.0, base=0,
                                        pattern=[[-1, P]], channel_multiplier=1))
            own.link(pool.tensor_copy(identb[:], ident[:]))
            own.link(pool.memset(tab[BUCKETS:BUCKETS + 1, :], NEG))
            pool.memset(ones[:], 1.0).then_inc(consts, 1)
            for l, name in enumerate(("sinks", "sink_logits_2")):
                src = t[name]
                pool.dma_start(sinkb[:, l, :], bass.AP(tensor=src.tensor, offset=0, ap=[[0, P], [1, NH]])).then_inc(vec_in, 16)
            pool.dma_start(kvg[:], bass.AP(tensor=t["kv_norm_g"].tensor, offset=0, ap=[[0, P], [1, P]])).then_inc(vec_in, 16)
            for n, name in enumerate(("idx_k_ln_g", "idx_k_ln_b")):
                pool.dma_start(ikg[:, n, :], bass.AP(tensor=t[name].tensor, offset=0, ap=[[0, P], [1, HD]])).then_inc(vec_in, 16)
            for n, name in enumerate(("lambda_q1_2", "lambda_k1_2", "lambda_q2_2", "lambda_k2_2")):
                pool.dma_start(lam4[:, n, :], bass.AP(tensor=t[name].tensor, offset=0, ap=[[0, P], [1, HD]])).then_inc(lam_in, 16)
            for tile_ in (cn, ikn, avn):
                pool.memset(tile_[:, MC, :], 0.0)
            own.link(pool.memset(causal[:], 0.0))
            pool.affine_select(out=causal[:], in_=causal[:], compare_op=ALU.is_ge, fill=NEG, base=NKEY - P,
                               pattern=[[-1, NKEY]], channel_multiplier=1).then_inc(zeros, 1)
            def low(name, i, b):
                pool.wait_ge(hi[b], PAIR0[name] + i + 1)
                n = KC[name] * P
                pool.tensor_tensor(wl[:, b, 0:n], stage[:, b, 0:n], wh[:, b, 0:n].bitcast(F32), ALU.subtract).then_inc(lo[b], 1)

            def low_pair(name, i):
                low(name, i, 0)
                low(name, i, 1)

            def lows(name):
                with pool.Fori(0, PAIRS[name]) as i:
                    low_pair(name, i)

            tables = ((fA, fA_dram, LEN_A, biasA, NEAR), (fB, fB_dram, LEN_B, biasB, NKEY))

            def bias_out(h):
                for f, dram, length, _, _ in tables:
                    pool.dma_start(dram[h:h + 2, :, 0:length], f[h:h + 2, :].unsqueeze(1).broadcast_to([2, P, length])).then_inc(f_out, 16)

            def bias_back(h):
                for _, dram, length, tile_, width in tables:
                    src = bass.AP(tensor=dram.tensor, offset=h * P * (length + 1) + P - 1, ap=[[length, P], [P * (length + 1), 2], [1, width]])
                    pool.dma_start(tile_[:, h:h + 2, :], src).then_inc(bias_in, 16)

            pool.wait_ge(fA_ok, 2)
            bias_out(0)
            bias_out(2)
            low_pair("iq1", 0)
            bias_out(4)
            bias_out(6)
            low_pair("aq1", 0)
            pool.wait_ge(f_out, 8 * 16)
            bias_back(0)
            low_pair("aq1", 1)
            bias_back(2)
            low_pair("uq1", 0)
            bias_back(4)
            low_pair("uq1", 1)
            bias_back(6)
            lows("gates1")
            lows("br1")
            pool.wait_ge(ev[1], PAIR0["kv2"] + 1)
            pool.iota(dist[:], pattern=[[-1, DIST]], base=3 * P, channel_multiplier=1,
                      allow_small_or_imprecise_dtypes=True).then_inc(dist_ok, 1)

            def bias_block(i):
                if i:
                    pool.wait_ge(ph["df"]["neg"], 8 * i)
                for h in range(4):
                    pool.tensor_scalar(biasD[:, h, META:NKEY], dist[:, 3 * P - P * i:3 * P - P * i + SEQ],
                                       -(2.0 ** (-8.0 * (h + 1) / 4)), None, ALU.mult).then_inc(biasD_ok, 1)

            def bias_window(h0, h1):
                for h in range(h0, h1):
                    pool.tensor_scalar(biasW[:, h, META:META + WIN2], tmp[:, 0, 0:WIN2],
                                       -(2.0 ** -(h + 1.0)), None, ALU.mult).then_inc(biasW_ok, 1)

            low_pair("qa2", 0)
            pool.wait_ge(dist_ok, 2)
            pool.memset(biasD[:, :, 0:META], 0.0)
            low_pair("qa2", 1)
            low_pair("qb2", 0)
            low_pair("qb2", 1)
            bias_block(0)
            bias_block(1)
            pool.wait_ge(nat_t, 3)
            pool.wait_ge(dist_ok, 3)
            pool.memset(biasW[:, :, 0:META], 0.0)
            pool.memset(biasW[:, :, META + WIN2:], 0.0)
            bias_window(0, NH // 2)
            bias_block(2)
            bias_window(NH // 2, NH)
            bias_block(3)
            lows("gates2")
            lows("br2")

        @block.scalar
        def _(act):
            act.preload_act_table(ACT.Exp)
            act.dma_start(rows[0:KD, :], t["attn_norm_g"].rearrange("a (k p) -> (a k) p", p=P)).then_inc(g1_in, 16)
            act.dma_start(metain[:, 0, :], t["meta_tokens"]).then_inc(meta_in, 16)
            act.dma_start(metain[:, 1, :], t["meta_tokens_2"]).then_inc(meta_in, 16)

            def high(name, i, b):
                act.wait_ge(w_in[b], 16 * (LOAD0[name] + LOADS[name]) + i * (16 * LOADS[name]))
                if not (name == "kv1" and isinstance(i, int) and i == 0):
                    act.wait_ge(mm[b], PAIR0[name] + i)
                n = KC[name] * P
                act.activation(wh[:, b, 0:n], stage[:, b, 0:n], ACT.Copy).then_inc(hi[b], 1)

            def high_next(name, i, last):
                if not last:
                    high(name, i + 1, 0)
                elif AFTER[name]:
                    high(AFTER[name], 0, 0)

            def only_high(name):
                if PAIRS[name] == 2:
                    high(name, 0, 1)
                    high_next(name, 0, False)
                elif PAIRS[name] > 2:
                    with act.Fori(0, PAIRS[name] - 1) as i:
                        high(name, i, 1)
                        high_next(name, i, False)
                high(name, PAIRS[name] - 1, 1)
                high_next(name, PAIRS[name] - 1, True)

            for k in range(KD):
                act.wait_ge(x_t, k + 1)
                act.activation(hT[:, k, :], psS[:, k % 4, :], ACT.Copy).then_inc(x_taken, 1)
                if k == 0:
                    act.wait_ge(gvec_ok, 1)
                act.wait_ge(x_taken, k + 1)
                g = ROW["attn_norm_g"] + k
                act.activation(hn[:, 0, k, :], hT[:, k, :], ACT.Copy, scale=gvec[:, g:g + 1]).then_inc(xhi, 1)
                if k == 1:
                    high("kv1", 0, 0)
                if k == 3:
                    act.wait_ge(meta_in, 32)
                    for n in range(2):
                        if n:
                            act.wait_ge(meta_sq, n)
                        act.activation(junk[0:META, :], metain[:, n, :], ACT.Square, accum_out=st[0:META, 1, n:n + 1]).then_inc(meta_sq, 1)
            high("kv1", 0, 1)
            act.wait_ge(meta_sq, 2)
            for q in range(4):
                act.wait_ge(x_in[q], 16)
            for n in range(NB - 1):
                if n:
                    act.wait_ge(x_sq, n)
                act.activation(junk[:], xin[:, n, :], ACT.Square, accum_out=st[:, 0, n:n + 1]).then_inc(x_sq, 1)
            act.wait_ge(lam_sum, 1)
            act.activation(lam[:, 2:4], lam[:, 0:2], ACT.Exp).then_inc(lam_e, 1)

            high("kv1", 1, 0)
            high("kv1", 1, 1)
            high_next("kv1", 1, True)
            for name in ("bq1", "iq1", "aq1"):
                only_high(name)
            act.wait_ge(ssq_in, 1)
            for k in range(2):
                g = ROW["q_norm_g"] + k
                act.activation(bqg[:, 0, k, :], bqT[:, k, :], ACT.Copy, scale=gvec[:, g:g + 1]).then_inc(bqhi, 1)
            only_high("uq1")
            for u in range(4 * NB):
                K = META + P * (u // 4 + 1)
                act.wait_ge(lg_mm, u + 1)
                if u >= 2:
                    act.wait_ge(lg_used, u - 1)
                src = psS[:, 2 * (u % 2):2 * (u % 2) + 2, :]
                if K > 512:
                    act.activation(relu[:, u % 2, :].rearrange("p (a b) -> p a b", a=2), src[:, :, 0:K // 2], ACT.Relu).then_inc(lg_taken, 1)
                else:
                    act.activation(relu[:, u % 2, 0:K], src[:, 0, 0:K], ACT.Relu).then_inc(lg_taken, 1)

            def gate_high(l, j):
                for step in range(2 * KD):
                    if GATE_START[l][step] == j:
                        if step % 2 == 0:
                            high(f"gates{l}", step // 2, 1)
                        else:
                            high_next(f"gates{l}", step // 2, step == 2 * KD - 1)

            def gate_tanh(l, j):
                for step in range(2 * KD):
                    if GATE_DONE[l][step] == j - 2:
                        i, b = divmod(step, 2)
                        act.wait_ge(ev[b], PAIR0[f"gates{l}"] + i + 1)
                        bias = bhalf[:, step:step + 1] if l == 1 else 0.0
                        act.activation(gate[:, step, :], tmp[:, b, :], ACT.Tanh, bias=bias, scale=0.5).then_inc(th_ok[b], 1)

            def softmax_unit(p, u, tile, col):
                act.wait_ge(p["neg"], u + 1)
                act.activation(tile, tile, ACT.Exp, bias=negm[:, col:col + 1],
                               accum_out=rsum[:, col:col + 1]).then_inc(p["p"], 1)

            def sink_part(p, l, i):
                act.wait_ge(p["es"], 2 * i + 1)
                act.activation(st[:, 3, :], st[:, 2, :], ACT.Exp).then_inc(p["es"], 1)

            def take_pt(p, u, chunks, dst):
                act.wait_ge(p["pt"], u + 1)
                if u >= 2:
                    act.wait_ge(p["pv"], u - 1)
                whole = [c for c in chunks if c[2] == P]
                if any(c[2] == META for c in chunks):
                    act.activation(dst[0:META, dst.shape[-1] - P:], psT[0:META, 1, 0:P], ACT.Copy)
                act.activation(dst[:, 0:len(whole) * P], psT[:, 0, 0:len(whole) * P], ACT.Copy).then_inc(p["ptx"], 1)

            def heads_high(m, dst, gain=1.0):
                for i in range(NB):
                    act.wait_ge(oT_mm, NB * m + i + 1)
                    act.activation(dst[:, 0, :, i * P:(i + 1) * P], psS[:, i, :].rearrange("p (c q) -> p c q", c=4),
                                   ACT.Copy, scale=gain).then_inc(o_hi, 1)

            units = list(window1_units())
            p = ph["w1"]
            for j in range(len(units) + 5):
                gate_high(1, j)
                if j < len(units):
                    softmax_unit(p, j, W3a[:, j % 3, 0:units[j][3]], j)
                gate_tanh(1, j)
                if 2 <= j < len(units) + 2:
                    take_pt(p, j - 2, units[j - 2][4], PTa[:, j % 2, :])
                if 3 <= j < len(units) + 3 and (j - 3) % NH == NH - 1:
                    sink_part(p, 0, (j - 3) // NH)
            heads_high(0, oA)
            units = list(latent_units())
            p = ph["la"]
            for j in range(len(units) + 2):
                if j < len(units):
                    softmax_unit(p, j, W3[:, j % 3, 0:units[j][2]], j)
                if j >= 2:
                    take_pt(p, j - 2, units[j - 2][3], PT[:, j % 2, :])
            heads_high(1, oB)

            def branches(l):
                name, m0 = f"br{l}", (l - 1) * KD

                def pair(i, last):
                    high_next(name, i, last)
                    if not last:
                        high(name, i + 1, 1)
                    act.wait_ge(mix_ok, m0 + i + 1)
                    act.activation(mix[:, 0, bass.ds(i, 1), :], mix32[:, 2, :], ACT.Copy).then_inc(mix_hi, 1)

                high(name, 0, 1)
                with act.Fori(0, PAIRS[name] - 1) as i:
                    pair(i, False)
                pair(PAIRS[name] - 1, True)

            def squares_and_gain(name, norm, grow):
                def chunk(i, b):
                    act.wait_ge(ev[b], PAIR0[name] + i + 1)
                    act.wait_ge(h_sq2, 2 * i + (squares_cleared(norm) + b))
                    act.activation(sq[:], hT[:, bass.ds(2 * i + b, 1), :], ACT.Square).then_inc(h_sq, 1)
                    act.activation(hn[:, 0, bass.ds(2 * i + b, 1), :], hT[:, bass.ds(2 * i + b, 1), :], ACT.Copy,
                                   scale=gvec[:, bass.ds(2 * i + (grow + b), 1)]).then_inc(hg_hi, 1)

                def pair(i, last):
                    high(name, i, 1)
                    chunk(i, 0)
                    high_next(name, i, last)
                    chunk(i, 1)

                with act.Fori(0, PAIRS[name] - 1) as i:
                    pair(i, False)
                pair(PAIRS[name] - 1, True)

            def swiglu(name, f0, early=0):
                def pair(i, last, early=False):
                    high(name, i, 1)
                    if early:
                        high_next(name, i, last)
                    act.wait_ge(ev[0], PAIR0[name] + i + 1)
                    act.activation(ft[:, 1, :], ft[:, 0, :], ACT.Tanh, scale=0.5).then_inc(t_ok, 1)
                    if not early:
                        high_next(name, i, last)
                    act.wait_ge(hid_ok, f0 + i + 1)
                    act.activation(hid[:, 0, bass.ds(i, 1), :], ft[:, 4, :], ACT.Copy).then_inc(hid_hi, 1)

                for i in range(early):
                    pair(i, False, True)
                with act.Fori(early, PAIRS[name] - 1) as i:
                    pair(i, False)
                pair(PAIRS[name] - 1, True)

            branches(1)
            squares_and_gain("out1", 0, ROW["ffn_norm_g"])
            swiglu("gu1a", 0, 1)
            only_high("dn1a")
            swiglu("gu1b", NFH)
            name = "dn1b"

            def chunk1(i, b):
                act.wait_ge(ev[b], PAIR0[name] + i + 1)
                act.wait_ge(h_sq2, 2 * i + (squares_cleared(1) + b))
                act.activation(sq[:], hT[:, bass.ds(2 * i + b, 1), :], ACT.Square).then_inc(h_sq, 1)
                act.wait_ge(h_gain, 2 * i + b + 1)
                act.activation(hn[:, 0, bass.ds(2 * i + b, 1), :], hT[:, bass.ds(2 * i + b, 1), :], ACT.Copy,
                               scale=gvec[:, bass.ds(2 * i + (ROW["norm_mix_2"] + b), 1)]).then_inc(hg_hi, 1)

            def pair1(i, last):
                high(name, i, 1)
                chunk1(i, 0)
                high_next(name, i, last)
                chunk1(i, 1)

            with act.Fori(0, PAIRS[name] - 1) as i:
                pair1(i, False)
            pair1(PAIRS[name] - 1, True)

            for name in ("kv2", "qa2", "qb2"):
                only_high(name)
            p = ph["df"]
            for j in range(16 + 2):
                if j < 16:
                    for m in range(2):
                        softmax_unit(p, 2 * j + m, W6[:, j % 3, m, :], 2 * j + m)
                if j >= 2:
                    take_pt(p, j - 2, [(MC, 0, META)] + [(c, 0, P) for c in range(NB)], PT2[:, j % 2, :])
            units = list(window2_units())
            p = ph["w2"]
            for j in range(len(units) + 6):
                gate_high(2, j)
                if j < len(units):
                    softmax_unit(p, j, W3b[:, j % 3, 0:units[j][3] + META], j)
                gate_tanh(2, j)
                if j in Y_NORM:
                    i = Y_NORM.index(j)
                    act.wait_ge(ph["df"]["on"], NB)
                    if i:
                        act.wait_ge(y_sq, 2 * i)
                    act.activation(sq[:], yn[:, i, :], ACT.Square).then_inc(y_sq, 1)
                if j >= 2 and j - 2 < len(units):
                    take_pt(p, j - 2, units[j - 2][7], PTb[:, j % 2, :])
                if 3 <= j < len(units) + 3 and (j - 3) % NH == NH - 1:
                    sink_part(p, 1, (j - 3) // NH)
            heads_high(2, oA, subg[:])
            heads_high(3, oB)
            branches(2)
            squares_and_gain("out2", 2, ROW["norm_ffn_2"])
            swiglu("gu2a", 2 * NFH, 1)
            only_high("dn2a")
            swiglu("gu2b", 3 * NFH)
            name = "dn2b"

            def chunk2(i, b):
                act.wait_ge(ev[b], PAIR0[name] + i + 1)
                act.wait_ge(h_sq2, 2 * i + (squares_cleared(3) + b))
                act.activation(sq[:], hT[:, bass.ds(2 * i + b, 1), :], ACT.Square).then_inc(h_sq, 1)
                act.activation(hgf[:, bass.ds(2 * i + b, 1), :], hT[:, bass.ds(2 * i + b, 1), :], ACT.Copy,
                               scale=gvec[:, bass.ds(2 * i + (ROW["norm_final_2"] + b), 1)]).then_inc(fin_gain, 1)

            def pair2(i, last):
                high(name, i, 1)
                chunk2(i, 0)
                high_next(name, i, last)
                chunk2(i, 1)

            with act.Fori(0, PAIRS[name] - 1) as i:
                pair2(i, False)
            pair2(PAIRS[name] - 1, True)


        @block.vector
        def _(v):
            dv = Tally(v, dve_own)

            def spread(ap, width):
                return ap.unsqueeze(2).broadcast_to([ap.shape[0], ap.shape[1], width])

            def low(name, i, b):
                if name in POOL_LOW:
                    return
                v.wait_ge(hi[b], PAIR0[name] + i + 1)
                n = KC[name] * P
                v.tensor_tensor(wl[:, b, 0:n], stage[:, b, 0:n], wh[:, b, 0:n].bitcast(F32), ALU.subtract).then_inc(lo[b], 1)

            def low_next(name, i, last):
                if not last:
                    low(name, i + 1, 0)
                elif AFTER[name]:
                    low(AFTER[name], 0, 0)

            def done(name, i, b):
                v.wait_ge(mm[b], PAIR0[name] + i + 1)

            def pairs(name, pair, first=0):
                if PAIRS[name] - 1 > first:
                    with v.Fori(first, PAIRS[name] - 1) as i:
                        pair(i, False)
                pair(PAIRS[name] - 1, True)

            def rsqrt(x, y, n, parts=P):
                step, bits = rst[0:parts, 0:n], rsti[0:parts, 0:n]
                dv.link(v.tensor_scalar(bits, x.bitcast(I32), 1, None, ALU.logical_shift_right))
                dv.link(v.tensor_scalar(y.bitcast(I32), bits, -1.0, RSQRT_SEED, ALU.mult, ALU.add))
                for _ in range(3):
                    dv.link(v.scalar_tensor_tensor(out=step, in0=y, scalar=-0.5, in1=y, op0=ALU.mult, op1=ALU.mult))
                    dv.link(v.tensor_tensor(step, step, x, ALU.mult))
                    dv.link(v.scalar_tensor_tensor(out=y, in0=step, scalar=1.5, in1=y, op0=ALU.add, op1=ALU.mult))

            def diagonals(dst, r):
                for n in range(NB):
                    ins = v.tensor_scalar(dst[:, n, :], ident[:], r[:, n:n + 1], None, ALU.mult)
                return ins

            def x_low(k):
                g = ROW["attn_norm_g"] + k
                v.wait_ge(xhi, k + 1)
                v.scalar_tensor_tensor(out=hn[:, 1, k, :], in0=hT[:, k, :], scalar=gvec[:, g:g + 1],
                                       in1=hn[:, 0, k, :].bitcast(F32), op0=ALU.mult, op1=ALU.subtract).then_inc(xlo, 1)

            v.wait_ge(gvec_t, 1)
            v.tensor_copy(gvec[:, 0:KD], psT[:, 1, 0:KD]).then_inc(gvec_ok, 1)
            v.wait_ge(gvec_ok, 1)
            x_low(0)
            x_low(1)
            low("kv1", 0, 0)
            x_low(2)
            x_low(3)
            v.wait_ge(meta_sq, 2)
            dv.link(v.tensor_scalar(st[0:META, 1, 2:4], st[0:META, 1, 0:2], 1.0 / D, EPS, ALU.mult, ALU.add))
            rsqrt(st[0:META, 1, 2:4], rs[0:META, 0:2], 2, META)
            x_low(4)
            for n in range(2):
                v.tensor_scalar(metain[:, n, :], metain[:, n, :], rs[0:META, n:n + 1], None, ALU.mult).then_inc(meta_ok, 1)
            for k in range(5, KD):
                x_low(k)
            low("kv1", 0, 1)
            v.wait_ge(gvec_t, 2)
            v.tensor_copy(gvec[:, KD:], psT[:, 1, KD:NROWS]).then_inc(gvec_ok, 1)
            v.wait_ge(gvec_ok, 2)
            v.wait_ge(meta_t, 1)
            for l, name in enumerate(("attn_norm_g", "norm_mix_2")):
                ins = v.tensor_tensor(metaT[:, l, :, :], psT[:, 0, l * P:(l + 1) * P].rearrange("p (k m) -> p k m", k=KD),
                                      spread(gvec[:, ROW[name]:ROW[name] + KD], META), ALU.mult)
            ins.then_inc(metaT_ok, 1)
            v.wait_ge(lam_in, 64)
            dv.link(v.tensor_tensor_reduce(out=lamj[:], in0=lam4[:, 0, :], in1=lam4[:, 1, :], scale=1.0, scalar=0.0,
                                           op0=ALU.mult, op1=ALU.add, accum_out=lam[:, 0:1]))
            dv.link(v.tensor_tensor_reduce(out=lamj[:], in0=lam4[:, 2, :], in1=lam4[:, 3, :], scale=1.0, scalar=0.0,
                                           op0=ALU.mult, op1=ALU.add, accum_out=lam[:, 1:2]))
            v.memset(lamj[:, 0:1], 0.0).then_inc(lam_sum, 1)
            for q in range(4):
                v.wait_ge(x_in[q], 16)
            for n in range(NB - 1, NB):
                dv.link(v.tensor_tensor_reduce(out=squares[:], in0=xin[:, n, :], in1=xin[:, n, :], scale=1.0, scalar=0.0,
                                               op0=ALU.mult, op1=ALU.add, accum_out=st[:, 0, n:n + 1]))
            v.wait_ge(x_sq, NB - 1)
            dv.link(v.tensor_scalar(st[:, 0, 4:8], st[:, 0, 0:4], 1.0 / D, EPS, ALU.mult, ALU.add))
            rsqrt(st[:, 0, 4:8], rs[:, 0:4], 4)
            v.wait_ge(consts, 1)
            diagonals(diag, rs[:, 0:4]).then_inc(diag_ok, 1)
            v.wait_ge(bcast, 1)
            v.tensor_copy(R[:], psT[:, 1, :]).then_inc(R_ok, 1)
            v.wait_ge(R_ok, 1)

            def start_rest():
                b0 = ROW["b_gates"]
                g = ROW["subln_gain_2"]
                dv.link(v.tensor_scalar(subg[:], gvec[:, g:g + 1], 1.0 - LAMBDA0, None, ALU.mult))
                dv.link(v.tensor_scalar(bhalf[:], gvec[:, b0:b0 + 2 * KD], 0.5, None, ALU.mult))
                v.wait_ge(f_mm, 1)
                v.tensor_copy(fA[:], psS[0:NH, 2, 0:LEN_A]).then_inc(fA_ok, 1)
                v.wait_ge(f_mm, 2)
                v.tensor_copy(fB[:, 0:512], psS[0:NH, 3, :])
                v.tensor_copy(fB[:, 512:LEN_B], psT[0:NH, 0, 0:LEN_B - 512]).then_inc(fA_ok, 1)
                v.wait_ge(lam_e, 1)
                dv.link(v.tensor_tensor(neglam[:], lam[:, 3:4], lam[:, 2:3], ALU.subtract))
                dv.link(v.tensor_scalar(neglam[:], neglam[:], -LAMBDA0, None, ALU.add))

            def take_keys(name, i, b, dst):
                done(name, i, b)
                v.tensor_tensor(dst[:, META:NKEY], psL[:, b, :], R[:], ALU.mult)
                v.tensor_copy(dst[:, 0:META], psS[:, b, 0:META]).then_inc(ev[b], 1)

            def take_scaled(name, i, b, dst, by, scale=1.0):
                done(name, i, b)
                v.scalar_tensor_tensor(out=dst, in0=psL[:, b, :], scalar=scale, in1=by, op0=ALU.mult, op1=ALU.mult).then_inc(ev[b], 1)

            keys = [bkvT[:], ikwT[:], akT[:], avT[:]]
            for i in range(2):
                if i:
                    low("kv1", i, 1)
                take_keys("kv1", i, 0, keys[2 * i])
                low_next("kv1", i, i == 1)
                take_keys("kv1", i, 1, keys[2 * i + 1])
                if i == 0:
                    start_rest()
            low("bq1", 0, 1)
            take_scaled("bq1", 0, 0, bqT[:, 0, :], R[:])
            low_next("bq1", 0, True)
            take_scaled("bq1", 0, 1, bqT[:, 1, :], R[:])
            v.wait_ge(ev[0], PAIR0["bq1"] + 1)
            v.wait_ge(ev[1], PAIR0["bq1"] + 1)
            dv.link(v.tensor_tensor(sq[:], bqT[:, 0, :], bqT[:, 0, :], ALU.mult))
            dv.link(v.tensor_tensor(tmp[:, 0, :], bqT[:, 1, :], bqT[:, 1, :], ALU.mult))
            v.tensor_tensor(sq[:], sq[:], tmp[:, 0, :], ALU.add).then_inc(ssq_in, 1)
            v.wait_ge(zeros, 1)
            v.wait_ge(nat_t, 1)
            for n, dst in enumerate((cn, ikn, avn)):
                dv.link(v.tensor_copy(dst[:, 0:NB, :], psS[:, n, :].rearrange("p (c f) -> p c f", c=NB)))
                ins = v.tensor_copy(dst[0:META, MC, :], psT[0:META, 0, n * P:(n + 1) * P])
            ins.then_inc(nat_taken, 1)
            v.wait_ge(nat_taken, 1)
            low("iq1", 0, 1)
            take_scaled("iq1", 0, 0, iqT[:, 0, :], R[:])
            low_next("iq1", 0, True)
            take_scaled("iq1", 0, 1, iqT[:, 1, :], R[:])
            low("aq1", 0, 1)
            take_scaled("aq1", 0, 0, aqT[:, 0, :], R[:], QSCALE)
            NC = NB + 1
            flat = tmp[:, :, :].rearrange("p a n -> p (a n)")
            t5 = flat[:, 0:NC * P].rearrange("p (c f) -> p c f", c=NC)
            dv.link(v.tensor_tensor(t5, cn[:], cn[:], ALU.mult))
            dv.link(v.tensor_reduce(st[:, 6, 0:NC], t5, AX_X, ALU.add))
            dv.link(v.tensor_scalar(st[:, 7, 0:NC], st[:, 6, 0:NC], 1.0 / P, EPS, ALU.mult, ALU.add))
            rsqrt(st[:, 7, 0:NC], rs[:, 0:NC], NC)
            dv.link(v.tensor_tensor(cn[:], cn[:], spread(rs[:, 0:NC], P), ALU.mult))
            v.wait_ge(vec_in, 80)
            v.tensor_tensor(cn[:], cn[:], kvg[:].unsqueeze(1).broadcast_to([P, NC, P]), ALU.mult).then_inc(nat_ok, 1)
            low_next("aq1", 0, False)
            take_scaled("aq1", 0, 1, aqT[:, 1, :], R[:], QSCALE)
            low("aq1", 1, 1)
            t5 = flat[:, 0:NC * HD].rearrange("p (c f) -> p c f", c=NC)
            ik = ikn[:, :, 0:HD]
            dv.link(v.tensor_scalar(iwn[:], ikn[:, 0:NB, HD:HD + 4], (4 * HD) ** -0.5, None, ALU.mult))
            dv.link(v.tensor_reduce(st[:, 6, 0:NC], ik, AX_X, ALU.add))
            dv.link(v.tensor_scalar(st[:, 7, 0:NC], st[:, 6, 0:NC], 1.0 / HD, None, ALU.mult))
            dv.link(v.tensor_tensor(ikx[:], ik, spread(st[:, 7, 0:NC], HD), ALU.subtract))
            dv.link(v.tensor_tensor(t5, ikx[:], ikx[:], ALU.mult))
            dv.link(v.tensor_reduce(st[:, 6, 0:NC], t5, AX_X, ALU.add))
            dv.link(v.tensor_scalar(st[:, 7, 0:NC], st[:, 6, 0:NC], 1.0 / HD, EPS, ALU.mult, ALU.add))
            rsqrt(st[:, 7, 0:NC], rs[:, 0:NC], NC)
            dv.link(v.tensor_tensor(ikx[:], ikx[:], spread(rs[:, 0:NC], HD), ALU.mult))
            dv.link(v.tensor_tensor(ikx[:], ikx[:], ikg[:, 0, :].unsqueeze(1).broadcast_to([P, NC, HD]), ALU.mult))
            for c in range(2):
                ins = v.tensor_tensor(ikn[:, :, c * HD:(c + 1) * HD], ikx[:], ikg[:, 1, :].unsqueeze(1).broadcast_to([P, NC, HD]), ALU.add)
            ins.then_inc(nat_ok, 1)
            take_scaled("aq1", 1, 0, aqT[:, 2, :], R[:], QSCALE)
            low_next("aq1", 1, True)
            v.wait_ge(ssq_mm, 1)
            dv.link(v.tensor_scalar(st[:, 7, 0:4], psT[:, 1, 0:4], 1.0 / 256, EPS, ALU.mult, ALU.add))
            rsqrt(st[:, 7, 0:4], rs[:, 0:4], 4)
            diagonals(diag, rs[:, 0:4]).then_inc(diag_ok, 1)
            v.wait_ge(bqhi, 2)
            for k in range(2):
                g = ROW["q_norm_g"] + k
                v.scalar_tensor_tensor(out=bqg[:, 1, k, :], in0=bqT[:, k, :], scalar=gvec[:, g:g + 1], in1=bqg[:, 0, k, :].bitcast(F32),
                                       op0=ALU.mult, op1=ALU.subtract).then_inc(bqlo, 1)
            take_scaled("aq1", 1, 1, aqT[:, 3, :], R[:], QSCALE)
            low("uq1", 0, 1)
            v.wait_ge(key_t, 1)
            for n, dst in enumerate((cT, ikT)):
                v.tensor_copy(dst[:, META:NKEY], psS[:, n, :])
                v.tensor_copy(dst[:, 0:META], psT[:, 0, n * META:(n + 1) * META])
            v.tensor_copy(wukT[:], psS[:, 2, :].rearrange("p (c f) -> p c f", c=4)).then_inc(key_taken, 1)
            v.wait_ge(bcast, 2)
            v.tensor_copy(sq[:], psT[:, 1, :]).then_inc(R_ok, 1)
            v.wait_ge(R_ok, 2)
            for i in range(2):
                if i:
                    low("uq1", i, 1)
                take_scaled("uq1", i, 0, qT[:, 2 * i, :], sq[:])
                low_next("uq1", i, i == 1)
                take_scaled("uq1", i, 1, qT[:, 2 * i + 1, :], sq[:])
            for u in range(4 * NB):
                i, h = divmod(u, 4)
                K = META + P * (i + 1)
                v.wait_ge(lg_taken, u + 1)
                if h:
                    v.wait_ge(lg_used, u)
                v.scalar_tensor_tensor(out=acc[:, i, 0:K], in0=relu[:, u % 2, 0:K], scalar=iwn[:, i, h:h + 1],
                                       in1=acc[:, i, 0:K] if h else causal[:, NKEY - K:NKEY], op0=ALU.mult, op1=ALU.add).then_inc(lg_used, 1)
            v.wait_ge(lg_used, 4 * NB)

            def gate_part(l, j):
                for step in range(2 * KD):
                    if GATE_DONE[l][step] == j - 1:
                        name, (i, b) = f"gates{l}", divmod(step, 2)
                        done(name, i, b)
                        if l == 2 or i:
                            v.wait_ge(th_ok[b], KD * (l - 1) + i)
                        v.tensor_tensor(tmp[:, b, :], psL[:, b, :], R[:], ALU.mult).then_inc(ev[b], 1)

            best = st[:, 9, :]
            ROUNDS = TOPK // 8

            def top_rounds(j):
                blk, n = divmod(j, ROUNDS // 2)
                K = META + P * (blk + 1)
                for _ in range(2):
                    dv.link(v.max(best, acc[:, blk, 0:K]))
                    dv.link(v.match_replace(acc[:, blk, 0:K], best, acc[:, blk, 0:K], TAKEN))
                if n == ROUNDS // 2 - 1:
                    v.tensor_scalar(selm[:, blk, 0:K], acc[:, blk, 0:K], TAKEN / 2, NEG, ALU.is_gt, ALU.mult).then_inc(sel_ok, 1)

            def biased(p, u, tile, scores, bias, least, col):
                dv.link(v.tensor_tensor_reduce(out=tile, in0=scores, in1=bias, scale=1.0, scalar=least,
                                               op0=ALU.add, op1=ALU.max, accum_out=mx[:, col:col + 1]))
                v.tensor_scalar(negm[:, col:col + 1], mx[:, col:col + 1], -1.0, None, ALU.mult).then_inc(p["neg"], 1)

            def sink_sum(p, l, i):
                v.wait_ge(p["neg"], NH * (i + 1))
                v.tensor_tensor(st[:, 2, :], sinkb[:, l, :], negm[:, i * NH:(i + 1) * NH], ALU.add).then_inc(p["es"], 1)

            def sink_normed(p, i, dst):
                v.wait_ge(p["es"], 2 * i + 2)
                dv.link(v.tensor_tensor(st[:, 4, :], st[:, 3, :], rsum[:, i * NH:(i + 1) * NH], ALU.add))
                dv.link(v.reciprocal(st[:, 5, :], st[:, 4, :]))
                v.wait_ge(p["pv"], NH * (i + 1))
                v.tensor_tensor(dst[:, i, :].rearrange("p (h d) -> p h d", h=NH), psS[:, 2 * (i % 2) + 1, :].rearrange("p (h d) -> p h d", h=NH),
                                spread(st[:, 5, :], HD), ALU.mult).then_inc(p["on"], 1)

            def heads_low(m, dst, gain=1.0):
                for i in range(NB):
                    v.wait_ge(o_hi, NB * m + i + 1)
                    c = slice(i * P, (i + 1) * P)
                    v.scalar_tensor_tensor(out=dst[:, 1, :, c], in0=psS[:, i, :].rearrange("p (c q) -> p c q", c=4), scalar=gain,
                                           in1=dst[:, 0, :, c].bitcast(F32), op0=ALU.mult, op1=ALU.subtract).then_inc(o_lo, 1)

            v.wait_ge(bias_in, 8 * 16)
            units = list(window1_units())
            p = ph["w1"]
            for j in range(len(units) + 4):
                if j < len(units):
                    i, h, _, W, _ = units[j]
                    v.wait_ge(p["s"], j + 1)
                    if j >= 3:
                        v.wait_ge(p["pt"], j - 2)
                    biased(p, j, W3a[:, j % 3, 0:W], psS[:, 2 * (j % 2), 0:W], biasA[:, h, NEAR - W:NEAR], sinkb[:, 0, h:h + 1], j)
                    if h == NH - 1:
                        sink_sum(p, 0, i)
                    top_rounds(j)
                gate_part(1, j)
                if j >= 4 and (j - 4) % NH == NH - 1:
                    sink_normed(p, (j - 4) // NH, on)
            heads_low(0, oA)
            for h in range(NH):
                v.wait_ge(qabs_mm, h + 1)
                v.tensor_scalar(qabs[:, h, :], psL[:, h % 2, :], QSCALE, None, ALU.mult).then_inc(qabs_ok, 1)
            units = list(latent_units())
            p = ph["la"]
            for j in range(len(units) + 6):
                if j < len(units):
                    i, h, K, _ = units[j]
                    v.wait_ge(p["s"], j + 1)
                    if j >= 3:
                        v.wait_ge(p["pt"], j - 2)
                    biased(p, j, as_halves(W3[:, j % 3, 0:K], K), two_banks(psS[:, 2 * (j % 2):2 * (j % 2) + 2, :], K),
                           as_halves(biasB[:, h, NKEY - K:NKEY], K), TAKEN, j)
                if j >= 5 and (j - 5) % NH == NH - 1:
                    i = (j - 5) // NH
                    v.wait_ge(p["p"], NH * (i + 1))
                    dv.link(v.reciprocal(st[:, 5, :], rsum[:, i * NH:(i + 1) * NH]))
                    v.wait_ge(p["o"], NH * (i + 1))
                    v.tensor_tensor(on[:, i, :].rearrange("p (h d) -> p h d", h=NH), o_bank(i).rearrange("p (h d) -> p h d", h=NH),
                                    spread(st[:, 5, :], HD), ALU.mult).then_inc(p["on"], 1)
                if 3 <= j < len(units) + 3:
                    u = j - 3
                    v.wait_ge(p["pv"], u + 1)
                    if u >= 2:
                        v.wait_ge(p["o"], u - 1)
                    v.tensor_copy(lat[:, u % 2, :], psL[:, 0, 0:P]).then_inc(p["lat"], 1)
            heads_low(1, oB)

            def branches(l):
                name, m0 = f"br{l}", (l - 1) * KD

                def pair(i, last):
                    low(name, i, 1)
                    done(name, i, 0)
                    v.scalar_tensor_tensor(out=mix32[:, 0, :], in0=gate[:, bass.ds(i, 1), :], scalar=1.0, in1=psL[:, 0, :],
                                           op0=ALU.add, op1=ALU.mult).then_inc(ev[0], 1)
                    low_next(name, i, last)
                    done(name, i, 1)
                    v.scalar_tensor_tensor(out=mix32[:, 1, :], in0=gate[:, bass.ds(i + KD, 1), :], scalar=1.0, in1=psL[:, 1, :],
                                           op0=ALU.add, op1=ALU.mult).then_inc(ev[1], 1)
                    for b in range(2):
                        v.wait_ge(ev[b], PAIR0[name] + i + 1)
                    v.tensor_tensor(mix32[:, 2, :], mix32[:, 0, :], mix32[:, 1, :], ALU.add).then_inc(mix_ok, 1)
                    v.wait_ge(mix_hi, m0 + i + 1)
                    v.tensor_tensor(mix[:, 1, bass.ds(i, 1), :], mix32[:, 2, :], mix[:, 0, bass.ds(i, 1), :].bitcast(F32),
                                    ALU.subtract).then_inc(mix_lo, 1)

                pairs(name, pair)

            def clear_squares():
                v.memset(sqacc[:, 0, :], 0.0).then_inc(h_sq2, 1)

            def add_squares(norm, n):
                v.wait_ge(h_sq, n + (norm * KD + 1))
                v.wait_ge(h_sq2, n + squares_cleared(norm))
                v.tensor_tensor(sqacc[:, 0, :], sqacc[:, 0, :], sq[:], ALU.add).then_inc(h_sq2, 1)

            def gain_low(n, count, grow):
                v.wait_ge(hg_hi, count + 1)
                v.scalar_tensor_tensor(out=hn[:, 1, bass.ds(n, 1), :], in0=hT[:, bass.ds(n, 1), :], scalar=gvec[:, bass.ds(n + grow, 1)],
                                       in1=hn[:, 0, bass.ds(n, 1), :].bitcast(F32), op0=ALU.mult, op1=ALU.subtract).then_inc(hg_lo, 1)

            def out_project(l, norm, hg0, grow):
                name = f"out{l}"

                def chunk(i, b):
                    n = 2 * i + b
                    done(name, i, b)
                    v.scalar_tensor_tensor(out=hT[:, bass.ds(n, 1), :], in0=psL[:, b, :], scalar=0.5, in1=hT[:, bass.ds(n, 1), :],
                                           op0=ALU.mult, op1=ALU.add).then_inc(ev[b], 1)
                    add_squares(norm, n)
                    gain_low(n, 2 * i + (hg0 + b), grow)

                def pair(i, last):
                    low(name, i, 1)
                    chunk(i, 0)
                    low_next(name, i, last)
                    chunk(i, 1)

                clear_squares()
                pairs(name, pair)

            def new_rms(ssq_count):
                v.wait_ge(ssq_mm, ssq_count)
                dv.link(v.tensor_scalar(st[:, 8, 0:4], psT[:, 1, 0:4], 1.0 / D, EPS, ALU.mult, ALU.add))
                rsqrt(st[:, 8, 0:4], rs[:, 0:4], 4)

            def swiglu(name, f0, head=None):
                def pair(i, last, head=None):
                    low(name, i, 1)
                    if head:
                        new_rms(head[0])
                        diagonals(diag, rs[:, 0:4]).then_inc(diag_ok, 1)
                        low_next(name, i, last)
                        v.wait_ge(bcast, head[1])
                        v.tensor_copy(R[:], psT[:, 1, :]).then_inc(R_ok, 1)
                        v.wait_ge(R_ok, head[1])
                    done(name, i, 0)
                    v.tensor_tensor(ft[:, 0, :], psL[:, 0, :], R[:], ALU.mult).then_inc(ev[0], 1)
                    if not head:
                        low_next(name, i, last)
                    v.wait_ge(t_ok, f0 + i + 1)
                    dv.link(v.scalar_tensor_tensor(out=ft[:, 2, :], in0=ft[:, 1, :], scalar=1.0, in1=ft[:, 0, :], op0=ALU.add, op1=ALU.mult))
                    done(name, i, 1)
                    v.tensor_tensor(ft[:, 3, :], psL[:, 1, :], R[:], ALU.mult).then_inc(ev[1], 1)
                    v.wait_ge(ev[1], PAIR0[name] + i + 1)
                    v.scalar_tensor_tensor(out=ft[:, 4, :], in0=ft[:, 2, :], scalar=0.5, in1=ft[:, 3, :], op0=ALU.mult, op1=ALU.mult).then_inc(hid_ok, 1)
                    v.wait_ge(hid_hi, f0 + i + 1)
                    v.tensor_tensor(hid[:, 1, bass.ds(i, 1), :], ft[:, 4, :], hid[:, 0, bass.ds(i, 1), :].bitcast(F32), ALU.subtract).then_inc(hid_lo, 1)

                first = 0
                if head:
                    pair(0, False, head)
                    first = 1
                with v.Fori(first, PAIRS[name] - 1) as i:
                    dv.enter(i - first, 1)
                    pair(i, False)
                dv.leave(PAIRS[name] - 1 - first)
                pair(PAIRS[name] - 1, True)

            def add_down(name, i, b):
                done(name, i, b)
                n = bass.ds(2 * i + b, 1)
                v.tensor_tensor(hT[:, n, :], hT[:, n, :], psL[:, b, :], ALU.add).then_inc(ev[b], 1)

            def down(name):
                def pair(i, last):
                    low(name, i, 1)
                    add_down(name, i, 0)
                    low_next(name, i, last)
                    add_down(name, i, 1)

                pairs(name, pair)

            branches(1)
            out_project(1, 0, 0, ROW["ffn_norm_g"])
            swiglu("gu1a", 0, (2, 3))
            down("dn1a")
            swiglu("gu1b", NFH)

            def end_chunk(i, b):
                n = 2 * i + b
                add_down("dn1b", i, b)
                add_squares(1, n)
                v.tensor_scalar(hT[:, bass.ds(n, 1), :], hT[:, bass.ds(n, 1), :], gvec[:, bass.ds(n + ROW["final_norm_g"], 1)], None,
                                ALU.mult).then_inc(h_gain, 1)
                v.wait_ge(h_gain, 2 * i + b + 1)
                dv.link(v.tensor_tensor(tmp[:, 0, :], hT[:, bass.ds(n, 1), :], hT[:, bass.ds(n, 1), :], ALU.mult))
                v.wait_ge(x2_sq, 2 * i + b + 1)
                v.tensor_tensor(sqacc[:, 1, :], sqacc[:, 1, :], tmp[:, 0, :], ALU.add).then_inc(x2_sq, 1)
                gain_low(n, 2 * i + (KD + b), ROW["norm_mix_2"])

            def end_pair(i, last):
                low("dn1b", i, 1)
                end_chunk(i, 0)
                low_next("dn1b", i, last)
                end_chunk(i, 1)

            clear_squares()
            v.memset(sqacc[:, 1, :], 0.0).then_inc(x2_sq, 1)
            with v.Fori(0, PAIRS["dn1b"] - 1) as i:
                dv.enter(i, 2)
                end_pair(i, False)
            dv.leave(PAIRS["dn1b"] - 1)
            end_pair(PAIRS["dn1b"] - 1, True)

            low("kv2", 0, 1)
            new_rms(3)
            dv.link(v.tensor_tensor(st[:, 9, 0:4], rs[:, 0:4], rs[:, 0:4], ALU.mult))
            dv.link(v.tensor_tensor(st[:, 9, 0:4], st[:, 9, 0:4], psT[:, 1, 4:8], ALU.mult))
            dv.link(v.tensor_scalar(st[:, 9, 0:4], st[:, 9, 0:4], 1.0 / D, EPS, ALU.mult, ALU.add))
            rsqrt(st[:, 9, 0:4], rs[:, 4:8], 4)
            dv.link(v.tensor_tensor(rs[:, 8:12], rs[:, 0:4], rs[:, 4:8], ALU.mult))
            diag2 = tmp[:, 0, :].rearrange("p (n c) -> p n c", n=NB)
            diagonals(diag, rs[:, 0:4])
            diagonals(diag2, rs[:, 8:12]).then_inc(diag_ok, 1)
            low_next("kv2", 0, False)
            v.wait_ge(bcast, 4)
            v.tensor_copy(tmp[:, 1, :], psT[:, 0, :])
            v.tensor_copy(R[:], psT[:, 1, :]).then_inc(R_ok, 1)
            v.wait_ge(R_ok, 4)
            keys = [kaT[:, c, :] for c in range(4)] + [vaT[:, c, :] for c in range(4)] + [kbT[:], vbT[:]]
            for i in range(PAIRS["kv2"]):
                if i:
                    low("kv2", i, 1)
                take_keys("kv2", i, 0, keys[2 * i])
                if i:
                    low_next("kv2", i, i == PAIRS["kv2"] - 1)
                take_keys("kv2", i, 1, keys[2 * i + 1])
                if i < 4:
                    for n in (2 * i, 2 * i + 1):
                        dv.link(v.tensor_tensor(hT[:, n, :], hT[:, n, :], tmp[:, 1, :], ALU.mult))
            v.wait_ge(dist_ok, 1)
            v.scalar_tensor_tensor(out=dist[:], in0=dist[:], scalar=-1.0, in1=dist[:], op0=ALU.mult, op1=ALU.max).then_inc(dist_ok, 1)
            v.wait_ge(dist_ok, 2)
            dv.link(v.tensor_scalar(tmp[:, 0, 0:WIN2], dist[:, NEAR:NEAR + WIN2], float(P), -NEG * 100, ALU.is_gt, ALU.mult))
            v.tensor_tensor(tmp[:, 0, 0:WIN2], tmp[:, 0, 0:WIN2], dist[:, NEAR:NEAR + WIN2], ALU.add).then_inc(dist_ok, 1)
            low("qa2", 0, 1)
            v.wait_ge(nat_t, 2)
            for h in range(4):
                v.tensor_copy(van[:, 0:NB, h * P:(h + 1) * P], psS[:, h, :].rearrange("p (c f) -> p c f", c=NB))
            v.tensor_copy(van[0:META, MC, :], psT[0:META, 0, :]).then_inc(nat_taken, 1)
            v.wait_ge(nat_t, 3)
            v.tensor_copy(vbn[:, 0:NB, :], psS[:, 0, :].rearrange("p (c f) -> p c f", c=NB))
            v.tensor_copy(vbn[0:META, MC, :], psT[0:META, 1, 0:P]).then_inc(nat_taken, 1)
            for name, dst in (("qa2", qaT), ("qb2", qbT)):
                for i in range(2):
                    if i or name == "qb2":
                        low(name, i, 1)
                    take_scaled(name, i, 0, dst[:, 2 * i, :], R[:], QSCALE)
                    low_next(name, i, i == 1)
                    take_scaled(name, i, 1, dst[:, 2 * i + 1, :], R[:], QSCALE)
            p = ph["df"]
            for j in range(16 + 4):
                if j < 16:
                    i, h = divmod(j, 4)
                    for m in range(2):
                        u = 2 * j + m
                        v.wait_ge(p["s"], u + 1)
                        v.wait_ge(biasD_ok, 4 * i + h + 1)
                        if j >= 3 and m == 0:
                            v.wait_ge(p["pt"], j - 2)
                        biased(p, u, as_halves(W6[:, j % 3, m, :], NKEY), two_banks(psS[:, 2 * m:2 * m + 2, :], NKEY),
                               as_halves(biasD[:, h, :], NKEY), TAKEN, u)
                if 1 <= j < 17:
                    u = j - 1
                    v.wait_ge(p["p"], 2 * u + 2)
                    dv.link(v.reciprocal(st[:, 6, 0:1], rsum[:, 2 * u + 1:2 * u + 2]))
                    dv.link(v.scalar_tensor_tensor(out=st[:, 6, 1:2], in0=rsum[:, 2 * u:2 * u + 1], scalar=st[:, 6, 0:1], in1=neglam[:],
                                                   op0=ALU.mult, op1=ALU.mult))
                    v.scalar_tensor_tensor(out=W6[:, u % 3, 0, :], in0=W6[:, u % 3, 1, :], scalar=st[:, 6, 1:2], in1=W6[:, u % 3, 0, :],
                                           op0=ALU.mult, op1=ALU.add).then_inc(df_sum, 1)
                if j >= 4 and (j - 4) % 4 == 3:
                    i = (j - 4) // 4
                    dv.link(v.reciprocal(st[:, 7, 0:4], rsum[:, 8 * i:8 * i + 8:2]))
                    v.wait_ge(p["pv"], 4 * (i + 1))
                    v.tensor_tensor(yn[:, i, :].rearrange("p (h d) -> p h d", h=4), psL[:, i % 2, :].rearrange("p (h d) -> p h d", h=4),
                                    spread(st[:, 7, 0:4], P), ALU.mult).then_inc(p["on"], 1)
            v.wait_ge(biasW_ok, NH)
            units = list(window2_units())
            p = ph["w2"]
            for j in range(len(units) + 5):
                if j < len(units):
                    i, h, _, n, _, _, b, _ = units[j]
                    W = n + META
                    v.wait_ge(p["s"], j + 1)
                    if j >= 3:
                        v.wait_ge(p["pt"], j - 2)
                    biased(p, j, W3b[:, j % 3, 0:W], psS[:, 2 * (j % 2), 0:W], biasW[:, h, b:b + W], sinkb[:, 1, h:h + 1], j)
                    if h == NH - 1:
                        sink_sum(p, 1, i)
                gate_part(2, j)
                if j - 1 in Y_NORM:
                    i = Y_NORM.index(j - 1)
                    v.wait_ge(y_sq, 2 * i + 1)
                    v.tensor_reduce(st[:, 8 + i // 2, 4 * (i % 2):4 * (i % 2) + 4], sq[:].rearrange("p (h d) -> p h d", h=4), AX_X, ALU.add).then_inc(y_sq, 1)
                if j == Y_NORM[-1] + 2:
                    v.wait_ge(y_sq, 2 * NB)
                    s16 = st[:, 8:10, :].rearrange("p a b -> p (a b)")
                    dv.link(v.tensor_scalar(s16, s16, 1.0 / P, EPS, ALU.mult, ALU.add))
                    rsqrt(s16, rs[:], 16)
                    y16 = yn[:].rearrange("p i (h d) -> p (i h) d", h=4)
                    v.tensor_tensor(y16, y16, spread(rs[:], P), ALU.mult).then_inc(ph["df"]["es"], 1)
                if j >= 5 and (j - 5) % NH == NH - 1:
                    sink_normed(p, (j - 5) // NH, yw)
            heads_low(2, oA, subg[:])
            heads_low(3, oB)
            branches(2)
            out_project(2, 2, 2 * KD, ROW["norm_ffn_2"])
            swiglu("gu2a", 2 * NFH, (4, 5))
            down("dn2a")
            swiglu("gu2b", 3 * NFH)

            def last_pair(i, last):
                low("dn2b", i, 1)
                add_down("dn2b", i, 0)
                add_squares(3, 2 * i)
                low_next("dn2b", i, last)
                add_down("dn2b", i, 1)
                add_squares(3, 2 * i + 1)

            clear_squares()
            pairs("dn2b", last_pair)
            new_rms(5)
            for n in range(NB):
                if n >= 2:
                    v.wait_ge(fin_out[n % 2], 16)
                for half in range(2):
                    v.wait_ge(fin_t, 2 * n + half + 1)
                    v.tensor_scalar(yout[:, n % 2, half * 512:(half + 1) * 512], psS[:, 2 * (n % 2) + half, :], rs[:, n:n + 1], None,
                                    ALU.mult).then_inc(fin_ok, 1)

        @block.tensor
        def _(pe):
            def product(name, i, b, x, meta=None, made=None, between=None):
                pe.wait_ge(lo[b], PAIR0[name] + i + 1)
                if not (name == "kv1" and isinstance(i, int) and i == 0):
                    pe.wait_ge(ev[b], PAIR0[name] + i)
                kc = KC[name]
                for k in range(kc):
                    if made:
                        pe.wait_ge(made[0], made[1] + k + 1)
                    for n, (w, part) in enumerate(((wh, 0), (wh, 1), (wl, 0))):
                        ins = pe.matmul(psL[:, b, :], w[:, b, k * P:(k + 1) * P], x[:, part, k, :], start=k + n == 0, stop=k == kc - 1 and n == 2)
                if between:
                    between()
                if meta is not None:
                    if name == "kv1":
                        pe.wait_ge(metaT_ok, 1)
                    for k in range(kc):
                        ins = pe.matmul(psS[:, b, 0:META], stage[:, b, k * P:(k + 1) * P], metaT[:, meta, k, :], start=k == 0, stop=k == kc - 1)
                ins.then_inc(mm[b], 1)

            def products(name, x, first=0, meta=None, made=None):
                if made:
                    product(name, first, 0, x, made=made)
                    product(name, first, 1, x)
                    first += 1
                if PAIRS[name] - first > 2:
                    with pe.Fori(first, PAIRS[name]) as i:
                        for b in range(2):
                            product(name, i, b, x, meta=meta)
                else:
                    for i in range(first, PAIRS[name]):
                        for b in range(2):
                            product(name, i, b, x, meta=meta)

            def sums(which, col):
                for n in range(NB):
                    ins = pe.matmul(psT[:, 1, col + n:col + n + 1], which[:, n * P:(n + 1) * P], ones[:, 0:1], start=True, stop=True)
                return ins

            def spread_rms(bank, d):
                return pe.matmul(psT[:, bank, :], ones[:], d.rearrange("p n c -> p (n c)"), start=True, stop=True)

            pe.wait_ge(consts, 1)
            pe.wait_ge(g1_in, 16)
            pe.transpose(psT[:, 1, 0:KD], rows[0:KD, :], ident[0:KD, 0:KD]).then_inc(gvec_t, 1)
            for k in range(KD):
                if k % 2 == 0:
                    pe.wait_ge(x_in[k // 2], 16)
                if k >= 4:
                    pe.wait_ge(x_taken, k - 3)
                for n in range(NB):
                    ins = pe.transpose(psS[:, k % 4, n * P:(n + 1) * P], xin[:, n, k * P:(k + 1) * P], ident[:])
                ins.then_inc(x_t, 1)

            def meta_columns():
                pe.wait_ge(meta_ok, 2)
                for l in range(2):
                    for k in range(KD):
                        c = l * P + k * META
                        ins = pe.transpose(psT[:, 0, c:c + META], metain[:, l, k * P:(k + 1) * P], ident[0:META, 0:META])
                ins.then_inc(meta_t, 1)
                pe.wait_ge(rows_in, 16 * (len(ROWS) - 1))
                pe.wait_ge(gvec_ok, 1)
                pe.transpose(psT[:, 1, 0:NROWS], rows[:], ident[0:NROWS, 0:NROWS]).then_inc(gvec_t, 1)

            product("kv1", 0, 0, hn, meta=0, made=(xlo, 0), between=meta_columns)
            product("kv1", 0, 1, hn, meta=0)
            pe.wait_ge(diag_ok, 1)
            spread_rms(1, diag).then_inc(bcast, 1)
            pe.wait_ge(tab_in, 48)
            pe.matmul(psS[0:NH, 2, 0:LEN_A], tab[:, 0:NH], hotA[:], start=True, stop=True).then_inc(f_mm, 1)
            pe.matmul(psS[0:NH, 3, :], tab[:, NH:2 * NH], hotB[:, 0:512], start=True, stop=True)
            pe.matmul(psT[0:NH, 0, 0:LEN_B - 512], tab[:, NH:2 * NH], hotB[:, 512:LEN_B], start=True, stop=True).then_inc(f_mm, 1)
            products("kv1", hn, first=1, meta=0)
            products("bq1", hn)
            pe.wait_ge(ev[1], PAIR0["kv1"] + 2)
            pe.wait_ge(ev[0], PAIR0["kv1"] + 2)
            pe.wait_ge(fA_ok, 2)
            for n, src in enumerate((bkvT, ikwT, avT)):
                for c in range(NB):
                    pe.transpose(psS[:, n, c * P:(c + 1) * P], src[:, META + c * P:META + (c + 1) * P], ident[:])
                ins = pe.transpose(psT[0:META, 0, n * P:(n + 1) * P], src[:, 0:META], ident[:])
            ins.then_inc(nat_t, 1)
            products("iq1", hn)
            pe.wait_ge(ssq_in, 1)
            pe.wait_ge(R_ok, 1)
            sums(sq, 0).then_inc(ssq_mm, 1)
            products("aq1", hn)
            pe.wait_ge(nat_ok, 2)
            pe.wait_ge(nat_taken, 1)
            for n, src in enumerate((cn, ikn)):
                for c in range(NB):
                    pe.transpose(psS[:, n, c * P:(c + 1) * P], src[:, c, :], ident[:])
                pe.transpose(psT[:, 0, n * META:(n + 1) * META], src[0:META, MC, :], ident[0:META, 0:META])
            pe.wait_ge(wuk_in, 32)
            for c in range(4):
                ins = pe.transpose(psS[:, 2, c * P:(c + 1) * P], wuk[:, c * P:(c + 1) * P], ident[:])
            ins.then_inc(key_t, 1)
            pe.wait_ge(diag_ok, 2)
            spread_rms(1, diag).then_inc(bcast, 1)
            pe.wait_ge(bqlo, 2)
            products("uq1", bqg)
            pe.wait_ge(key_taken, 1)
            for u in range(4 * NB):
                i, h = divmod(u, 4)
                K = META + P * (i + 1)
                r = slice(h % 2 * HD, h % 2 * HD + HD)
                if u >= 2:
                    pe.wait_ge(lg_taken, u - 1)
                q = iqT[r, h // 2, i * P:(i + 1) * P]
                if K > 512:
                    pe.matmul(psS[:, 2 * (u % 2), 0:K // 2], q, ikT[r, 0:K // 2], start=True, stop=True)
                    ins = pe.matmul(psS[:, 2 * (u % 2) + 1, 0:K // 2], q, ikT[r, K // 2:K], start=True, stop=True)
                else:
                    ins = pe.matmul(psS[:, 2 * (u % 2), 0:K], q, ikT[r, 0:K], start=True, stop=True)
                ins.then_inc(lg_mm, 1)

            def gate_quarters(l, j, part):
                name, before, count = f"gates{l}", sum(GATE_QUARTERS[l][:j]), (GATE_QUARTERS[l] + [0, 0])[j]
                mine = range(before, before + count - count // 2) if part == 0 else range(before + count - count // 2, before + count)
                for quarter in mine:
                    i, b = divmod(quarter // 4, 2)
                    k0 = quarter % 4 * (KD // 4)
                    if k0 == 0:
                        pe.wait_ge(lo[b], PAIR0[name] + i + 1)
                        pe.wait_ge(ev[b], PAIR0[name] + i)
                    for k in range(k0, k0 + KD // 4):
                        for n, (w, part_) in enumerate(((wh, 0), (wh, 1), (wl, 0))):
                            ins = pe.matmul(psL[:, b, :], w[:, b, k * P:(k + 1) * P], hn[:, part_, k, :], start=k + n == 0, stop=k == KD - 1 and n == 2)
                    if k0 + KD // 4 == KD:
                        ins.then_inc(mm[b], 1)

            def transposed(p, u, chunks, tile):
                if u:
                    pe.wait_ge(p["ptx"], u)
                n = 0
                for c, col, width in chunks:
                    if width == P:
                        ins = pe.transpose(psT[:, 0, n * P:(n + 1) * P], tile[:, col:col + P], ident[:])
                        n += 1
                    else:
                        pe.transpose(psT[0:META, 1, 0:P], tile[:, col:col + META], ident[:])
                ins.then_inc(p["pt"], 1)

            def pieces(chunks, pt):
                n, found = 0, []
                for c, _, width in chunks:
                    if width == P:
                        found.append((pt[:, n * P:(n + 1) * P], c, P))
                        n += 1
                    else:
                        found.append((pt[0:META, pt.shape[-1] - P:], c, META))
                return found

            def heads_out(m, src):
                for i in range(NB):
                    if m == 3:
                        pe.wait_ge(o_lo, 2 * NB + i + 1)
                    for c in range(4):
                        ins = pe.transpose(psS[:, i, c * P:(c + 1) * P], src[:, i, c * P:(c + 1) * P], ident[:])
                    ins.then_inc(oT_mm, 1)

            pe.wait_ge(lg_taken, 4 * NB)
            units = list(window1_units())
            p = ph["w1"]
            for j in range(len(units) + 3):
                if j < len(units):
                    i, h, k0, W, _ = units[j]
                    r = slice(h // 4 * HD, h // 4 * HD + HD)
                    if j >= 2:
                        pe.wait_ge(p["neg"], j - 1)
                    pe.matmul(psS[:, 2 * (j % 2), 0:W], aqT[r, h % 4, i * P:(i + 1) * P], akT[r, k0:k0 + W], start=True, stop=True).then_inc(p["s"], 1)
                gate_quarters(1, j, 0)
                if 2 <= j < len(units) + 2:
                    pe.wait_ge(p["p"], j - 1)
                    transposed(p, j - 2, units[j - 2][4], W3a[:, (j - 2) % 3, :])
                gate_quarters(1, j, 1)
                if j >= 3:
                    u = j - 3
                    i, h = units[u][:2]
                    pe.wait_ge(p["ptx"], u + 1)
                    if h == 0 and i >= 2:
                        pe.wait_ge(p["on"], i - 1)
                    parts = pieces(units[u][4], PTa[:, u % 2, :])
                    for n, (pt, c, w) in enumerate(parts):
                        ins = pe.matmul(psS[:, 2 * (i % 2) + 1, h * HD:(h + 1) * HD], pt, avn[0:w, c, h // 4 * HD:h // 4 * HD + HD],
                                        start=n == 0, stop=n == len(parts) - 1)
                    ins.then_inc(p["pv"], 1)
            pe.wait_ge(p["on"], NB)
            heads_out(0, on)
            for b in range(2):
                pe.wait_ge(ev[b], PAIR0["br1"])
            for h in range(NH):
                r = slice(h % 2 * HD, h % 2 * HD + HD)
                if h >= 2:
                    pe.wait_ge(qabs_ok, h - 1)
                pe.matmul(psL[:, h % 2, :], wukT[r, h // 2, :], qT[r, h // 2, :], start=True, stop=True).then_inc(qabs_mm, 1)
            pe.wait_ge(qabs_ok, NH)
            pe.wait_ge(sel_ok, NB)
            pe.wait_ge(o_lo, NB)
            units = list(latent_units())
            p = ph["la"]
            for j in range(len(units) + 5):
                if j < len(units):
                    i, h, K, _ = units[j]
                    if j >= 2:
                        pe.wait_ge(p["neg"], j - 1)
                    if i == NB - 1 and h == 0:
                        pe.wait_ge(p["on"], 2)
                    q = qabs[:, h, i * P:(i + 1) * P]
                    cuts = [(0, 0, K)] if K <= 512 else [(0, 0, K // 2), (1, K // 2, K)]
                    for bank, k0, k1 in cuts:
                        dst = psS[:, 2 * (j % 2) + bank, 0:k1 - k0]
                        pe.matmul(dst, q, cT[:, k0:k1], start=True, stop=False)
                        ins = pe.matmul(dst, identb[:], selm[:, i, k0:k1], start=False, stop=True)
                    ins.then_inc(p["s"], 1)
                if 2 <= j < len(units) + 2:
                    pe.wait_ge(p["p"], j - 1)
                    transposed(p, j - 2, units[j - 2][3], W3[:, (j - 2) % 3, :])
                if j >= 4 and j - 4 < len(units):
                    u = j - 4
                    i, h = units[u][:2]
                    pe.wait_ge(p["lat"], u + 1)
                    if h == 0 and i >= 2:
                        pe.wait_ge(p["on"], i - 1 if i == 2 else i)
                    pe.matmul(o_bank(i)[:, h * HD:(h + 1) * HD], lat[:, u % 2, :], wuv[:, h * HD:(h + 1) * HD], start=True, stop=True).then_inc(p["o"], 1)
                if 3 <= j < len(units) + 3:
                    u = j - 3
                    pe.wait_ge(p["ptx"], u + 1)
                    if u:
                        pe.wait_ge(p["lat"], u)
                    parts = pieces(units[u][3], PT[:, u % 2, :])
                    for n, (pt, c, w) in enumerate(parts):
                        ins = pe.matmul(psL[:, 0, 0:P], cn[0:w, c, :], pt, start=n == 0, stop=n == len(parts) - 1)
                    ins.then_inc(p["pv"], 1)
            pe.wait_ge(p["on"], NB)
            heads_out(1, on)
            pe.wait_ge(p["lat"], len(units))

            def layer_rest(l, ssq0, norm):
                name = f"br{l}"
                pe.wait_ge(o_lo, (2 * l - 1) * NB)
                product(name, 0, 0, oA)
                pe.wait_ge(o_lo, 2 * l * NB)
                product(name, 0, 1, oB)
                with pe.Fori(1, PAIRS[name]) as i:
                    product(name, i, 0, oA)
                    product(name, i, 1, oB)
                products(f"out{l}", mix, made=(mix_lo, KD * (l - 1)))
                name = f"gu{l}a"
                product(name, 0, 0, hn, made=(hg_lo, KD * (2 * l - 2)))
                pe.wait_ge(h_sq2, squares_cleared(norm) + KD)
                pe.wait_ge(R_ok, ssq0)
                sums(sqacc[:, 0, :], 0).then_inc(ssq_mm, 1)
                product(name, 0, 1, hn)
                pe.wait_ge(diag_ok, ssq0 + 1)
                spread_rms(1, diag).then_inc(bcast, 1)
                products(name, hn, first=1)
                products(f"dn{l}a", hid, made=(hid_lo, NFH * (2 * l - 2)))
                products(f"gu{l}b", hn)
                products(f"dn{l}b", hid, made=(hid_lo, NFH * (2 * l - 1)))

            layer_rest(1, 2, 0)
            product("kv2", 0, 0, hn, meta=1, made=(hg_lo, KD))
            pe.wait_ge(h_sq2, squares_cleared(1) + KD)
            pe.wait_ge(x2_sq, 1 + KD)
            pe.wait_ge(R_ok, 3)
            sums(sqacc[:, 0, :], 0)
            sums(sqacc[:, 1, :], NB).then_inc(ssq_mm, 1)
            product("kv2", 0, 1, hn, meta=1)
            pe.wait_ge(diag_ok, 4)
            spread_rms(0, diag)
            spread_rms(1, tmp[:, 0, :].rearrange("p (n c) -> p n c", n=NB)).then_inc(bcast, 1)
            products("kv2", hn, first=1, meta=1)
            product("qa2", 0, 0, hn)
            for b in range(2):
                pe.wait_ge(ev[b], PAIR0["qa2"])
            for h in range(4):
                for c in range(NB):
                    pe.transpose(psS[:, h, c * P:(c + 1) * P], vaT[:, h, META + c * P:META + (c + 1) * P], ident[:])
                ins = pe.transpose(psT[0:META, 0, h * P:(h + 1) * P], vaT[:, h, 0:META], ident[:])
            ins.then_inc(nat_t, 1)
            product("qa2", 0, 1, hn)
            pe.wait_ge(nat_taken, 2)
            pe.wait_ge(R_ok, 4)
            for c in range(NB):
                pe.transpose(psS[:, 0, c * P:(c + 1) * P], vbT[:, META + c * P:META + (c + 1) * P], ident[:])
            pe.transpose(psT[0:META, 1, 0:P], vbT[:, 0:META], ident[:]).then_inc(nat_t, 1)
            products("qa2", hn, first=1)
            products("qb2", hn)
            for b in range(2):
                pe.wait_ge(ev[b], PAIR0["gates2"])
            pe.wait_ge(nat_taken, 3)
            p = ph["df"]
            all_keys = [(MC, 0, META)] + [(c, META + P * c, P) for c in range(NB)]
            for j in range(16 + 3):
                if j < 16:
                    i, h = divmod(j, 4)
                    for m in range(2):
                        u = 2 * j + m
                        r = slice(m * HD, (m + 1) * HD)
                        if u >= 2:
                            pe.wait_ge(p["neg"], u - 1)
                        q = qaT[r, h, i * P:(i + 1) * P]
                        pe.matmul(psS[:, 2 * m, 0:NKEY // 2], q, kaT[r, h, 0:NKEY // 2], start=True, stop=True)
                        pe.matmul(psS[:, 2 * m + 1, 0:NKEY // 2], q, kaT[r, h, NKEY // 2:NKEY], start=True, stop=True).then_inc(p["s"], 1)
                if 2 <= j < 18:
                    pe.wait_ge(df_sum, j - 1)
                    transposed(p, j - 2, all_keys, W6[:, (j - 2) % 3, 0, :])
                if j >= 3:
                    u = j - 3
                    i, h = divmod(u, 4)
                    pe.wait_ge(p["ptx"], u + 1)
                    if h == 0 and i >= 2:
                        pe.wait_ge(p["on"], i - 1)
                    parts = pieces(all_keys, PT2[:, u % 2, :])
                    for n, (pt, c, w) in enumerate(parts):
                        ins = pe.matmul(psL[:, i % 2, h * P:(h + 1) * P], pt, van[0:w, c, h * P:(h + 1) * P], start=n == 0, stop=n == len(parts) - 1)
                    ins.then_inc(p["pv"], 1)
            pe.wait_ge(p["on"], NB)
            units = list(window2_units())
            p = ph["w2"]
            for j in range(len(units) + 4):
                if j < len(units):
                    i, h, lo_c, W, wcol, mcol, _, _ = units[j]
                    r = slice(h // 4 * HD, h // 4 * HD + HD)
                    if j >= 2:
                        pe.wait_ge(p["neg"], j - 1)
                    q = qbT[r, h % 4, i * P:(i + 1) * P]
                    pe.matmul(psS[:, 2 * (j % 2), mcol:mcol + META], q, kbT[r, 0:META], start=True, stop=True)
                    k0 = META + P * lo_c
                    pe.matmul(psS[:, 2 * (j % 2), wcol:wcol + W], q, kbT[r, k0:k0 + W], start=True, stop=True).then_inc(p["s"], 1)
                gate_quarters(2, j, 0)
                if 2 <= j < len(units) + 2:
                    pe.wait_ge(p["p"], j - 1)
                    transposed(p, j - 2, units[j - 2][7], W3b[:, (j - 2) % 3, :])
                gate_quarters(2, j, 1)
                if 3 <= j < len(units) + 3:
                    u = j - 3
                    i, h = units[u][:2]
                    pe.wait_ge(p["ptx"], u + 1)
                    if h == 0 and i >= 2:
                        pe.wait_ge(p["on"], i - 1)
                    parts = pieces(units[u][7], PTb[:, u % 2, :])
                    for n, (pt, c, w) in enumerate(parts):
                        ins = pe.matmul(psS[:, 2 * (i % 2) + 1, h * HD:(h + 1) * HD], pt, vbn[0:w, c, h // 4 * HD:h // 4 * HD + HD],
                                        start=n == 0, stop=n == len(parts) - 1)
                    ins.then_inc(p["pv"], 1)
            pe.wait_ge(p["on"], NB)
            pe.wait_ge(ph["df"]["es"], 1)
            heads_out(2, yn)
            heads_out(3, yw)
            layer_rest(2, 4, 2)
            pe.wait_ge(h_sq2, squares_cleared(3) + KD)
            pe.wait_ge(R_ok, 5)
            sums(sqacc[:, 0, :], 0).then_inc(ssq_mm, 1)
            pe.wait_ge(fin_gain, KD)
            for n in range(NB):
                if n >= 2:
                    pe.wait_ge(fin_ok, 2 * (n - 1))
                for half in range(2):
                    for c in range(4):
                        ins = pe.transpose(psS[:, 2 * (n % 2) + half, c * P:(c + 1) * P], hgf[:, 4 * half + c, n * P:(n + 1) * P], ident[:])
                    ins.then_inc(fin_t, 1)


_INS = ["x", "meta_tokens", "attn_norm_g", "w_in", "b_gates", "q_norm_g", "kv_norm_g", "w_uq", "w_uk", "w_uv",
        "idx_k_ln_g", "idx_k_ln_b", "sinks", "rel_bias", "w_branch_a", "w_branch_b", "w_out", "ffn_norm_g",
        "w_ffn_gate", "w_ffn_up", "w_ffn_down", "final_norm_g", "meta_tokens_2", "norm_mix_2", "w_in_2",
        "lambda_q1_2", "lambda_k1_2", "lambda_q2_2", "lambda_k2_2", "subln_gain_2", "sink_logits_2",
        "w_branch_a_2", "w_branch_b_2", "w_out_2", "norm_ffn_2", "w_ff_gate_2", "w_ff_up_2", "w_ff_down_2",
        "norm_final_2"]


def kernel(**inputs):
    import concourse.bacc as _bacc
    from concourse.bass_utils import run_bass_kernel_spmd as _run

    nc = _bacc.Bacc("TRN2", target_bir_lowering=False, num_devices=1)
    arrays, t = {}, {}
    for name in _INS:
        a = np.ascontiguousarray(inputs[name])
        arrays[f"in_{name}"] = a
        t[name] = nc.dram_tensor(f"in_{name}", a.shape, mybir.dt.from_np(a.dtype), kind="ExternalInput").ap()
    for name, a in zip(("hot_a", "hot_b"), bucket_rows()):
        arrays[f"const_{name}"] = a
        t[name] = nc.dram_tensor(f"const_{name}", a.shape, F32, kind="ExternalInput").ap()
    out = nc.dram_tensor("out_0", (1, SEQ, D), F32, kind="ExternalOutput").ap()
    build(nc, t, out)
    r = _run(nc, [arrays], core_ids=[0])
    return r.results[0]["out_0"]
```

```python
from contextlib import ExitStack

import numpy as np

import concourse.bass as bass
from concourse import mybir

F32 = mybir.dt.float32
F32R = mybir.dt.float32r
BF16 = mybir.dt.bfloat16
I32 = mybir.dt.int32
ACT = mybir.ActivationFunctionType
ALU = mybir.AluOpType
AX_X = mybir.AxisListType.X

P = 128
D = 1024
KD = D // P
SEQ = 512
NB = SEQ // P
META = 16
NKEY = META + SEQ
MC = NB
FF = 2816
NFH = FF // P // 2
HD = 64
NH = 8
EPS = 1e-6
NEG = -1e30
TAKEN = -3e38
TOPK = 128
BUCKETS = 32
QSCALE = HD ** -0.5
LAMBDA0 = 0.8 - 0.6
RSQRT_SEED = float(0x5F3759DF)

NEAR = 2 * P
LEN_A = NEAR + P - 1
LEN_B = NKEY + P - 1
WIN2 = 3 * P
DIST = 7 * P


def bucket(dist):
    exact = BUCKETS // 2
    d = np.maximum(dist, 1).astype(np.float32)
    span = np.float32(np.log(128 / exact))
    large = exact + (np.log(d / np.float32(exact)) / span * np.float32(BUCKETS - exact)).astype(np.int32)
    return np.where(dist < exact, dist, np.minimum(large, BUCKETS - 1))


def bucket_rows():
    out = []
    for length, far in ((LEN_A, P), (LEN_B, 1 << 20)):
        dist = (length - P) - np.arange(length)
        dead = (dist < 0) | (dist >= far)
        hot = np.zeros((BUCKETS + 1, length), np.float32)
        live = np.flatnonzero(~dead)
        hot[bucket(dist[live]), live] = 1.0
        hot[BUCKETS, dead] = 1.0
        out.append(hot)
    return out


PHASES = [("kv1", 4, KD, 1), ("bq1", 2, KD, 1), ("iq1", 2, KD, 1), ("aq1", 4, KD, 2), ("uq1", 4, 2, 1),
          ("gates1", 2 * KD, KD, 1), ("br1", 2 * KD, 4, 1), ("out1", KD, KD, 1),
          ("gu1a", 2 * NFH, KD, 1), ("dn1a", KD, NFH, 1), ("gu1b", 2 * NFH, KD, 1), ("dn1b", KD, NFH, 1),
          ("kv2", 10, KD, 1), ("qa2", 4, KD, 1), ("qb2", 4, KD, 2),
          ("gates2", 2 * KD, KD, 1), ("br2", 2 * KD, 4, 1), ("out2", KD, KD, 1),
          ("gu2a", 2 * NFH, KD, 1), ("dn2a", KD, NFH, 1), ("gu2b", 2 * NFH, KD, 1), ("dn2b", KD, NFH, 1)]
KC = {n: kc for n, _, kc, _ in PHASES}
PAIRS = {n: s // 2 for n, s, _, _ in PHASES}
LOADS = {n: d for n, _, _, d in PHASES}
PAIR0, LOAD0, AFTER = {}, {}, {}
_pairs = _loads = 0
for _i, (_n, _s, _kc, _d) in enumerate(PHASES):
    PAIR0[_n], LOAD0[_n] = _pairs, _loads
    AFTER[_n] = PHASES[_i + 1][0] if _i + 1 < len(PHASES) else None
    _pairs += _s // 2
    _loads += _s // 2 * _d

POOL_LOW = ("iq1", "aq1", "uq1", "gates1", "br1", "qa2", "qb2", "gates2", "br2")

ROWS = [("attn_norm_g", KD), ("ffn_norm_g", KD), ("final_norm_g", KD), ("norm_mix_2", KD), ("norm_ffn_2", KD),
        ("norm_final_2", KD), ("b_gates", 2 * KD), ("q_norm_g", 2), ("subln_gain_2", 1)]
ROW = {}
NROWS = 0
for _n, _s in ROWS:
    ROW[_n] = NROWS
    NROWS += _s


def squares_cleared(norm):
    return norm * (KD + 1) + 1


class Tally:

    def __init__(self, eng, sem):
        self.eng, self.sem, self.n, self.off = eng, sem, 0, 0

    def link(self, ins):
        ins.then_inc(self.sem, 1)
        self.n += 1
        self.eng.wait_ge(self.sem, self.off + self.n)

    def enter(self, i, per):
        self.off, self.start, self.per = i * per, self.n, per

    def leave(self, count):
        assert self.n - self.start == self.per, (self.n - self.start, self.per)
        self.off, self.n = 0, self.start + self.per * count


def window1_units():
    for i in range(NB):
        for h in range(NH):
            if i == 0:
                yield i, h, 0, META + P, [(MC, 0, META), (0, META, P)]
            else:
                yield i, h, META + P * (i - 1), NEAR, [(i - 1, 0, P), (i, P, P)]


def latent_units():
    for i in range(NB):
        for h in range(NH):
            yield i, h, META + P * (i + 1), [(MC, 0, META)] + [(c, META + P * c, P) for c in range(i + 1)]


def window2_units():
    for i in range(NB):
        lo, hi = max(i - 1, 0), min(i + 1, NB - 1)
        n = hi - lo + 1
        w, m, bias = (0, n * P, META + P) if i == 0 else (META, 0, 0)
        for h in range(NH):
            yield i, h, lo, n * P, w, m, bias, [(MC, m, META)] + [(lo + c, w + P * c, P) for c in range(n)]


def two_banks(ap, width):
    return ap[:, :, 0:width // 2] if width > 512 else ap[:, 0, 0:width]


def as_halves(ap, width):
    return ap.rearrange("p (a b) -> p a b", a=2) if width > 512 else ap


GATE_QUARTERS = {1: [1] * 6 + [2] * 29, 2: [4] + [2] * 24 + [1] * 10 + [2]}
GATE_START = {l: [n for n, c in enumerate(q) for _ in range(c)][0::4] for l, q in GATE_QUARTERS.items()}
GATE_DONE = {l: [n for n, c in enumerate(q) for _ in range(c)][3::4] for l, q in GATE_QUARTERS.items()}
assert all(sum(q) == 4 * 2 * KD for q in GATE_QUARTERS.values())


UQ_AFTER = {3: (0, 1), 7: (1, 0), 11: (1, 1)}
Y_NORM = [8, 10, 12, 14]


def build(nc, t, out):
    with ExitStack() as ctx:
        def sem(name):
            return ctx.enter_context(nc.semaphore(name))

        base = -(-nc.sbuf_base // 32) * 32
        top = [base]
        size = {F32: 4, F32R: 4, BF16: 2, I32: 4}

        def at(name, shape, offset, dt=F32):
            n = int(np.prod(shape[1:])) * size[dt]
            assert offset + n <= nc.sbuf_usable_end, (name, offset + n - nc.sbuf_usable_end)
            return nc.alloc_sbuf_tensor_at(name, shape, dt, offset=offset), -(-(offset + n) // 32) * 32

        def keep(name, shape, dt=F32):
            tensor, top[0] = at(name, shape, top[0], dt)
            return tensor

        hT = keep("hT", [P, KD, SEQ])
        stage = keep("stage", [P, 2, NFH * P])
        wh = keep("wh", [P, 2, NFH * P], F32R)
        wl = keep("wl", [P, 2, NFH * P], F32R)
        Rk = keep("Rk", [P, NKEY])
        R = Rk[:, META:NKEY]
        tmp = keep("tmp", [P, 2, SEQ])
        ident = keep("ident", [P, P])
        identb = keep("identb", [P, P], BF16)
        ones = keep("ones", [P, P])
        gvec = keep("gvec", [P, NROWS])
        bhalf = keep("bhalf", [P, 2 * KD])
        g12 = keep("g12", [P, KD])
        kvg = keep("kvg", [P, P])
        ikg = keep("ikg", [P, 2, HD])
        sinkb = keep("sinkb", [P, 2, NH])
        tab = keep("tab", [BUCKETS + 1, 2 * NH])
        wuv = keep("wuv", [P, NH * HD])
        wukT = keep("wukT", [P, 4, P])
        metaT = keep("metaT", [P, 2, KD, META])
        iwn = keep("iwn", [P, NB, 4])
        mx = keep("mx", [P, 2 * NB * NH])
        negm = keep("negm", [P, 2 * NB * NH])
        rsum = keep("rsum", [P, 2 * NB * NH])
        st = keep("st", [P, 12, NH])
        rst = keep("rst", [P, 16])
        rs = keep("rs", [P, 16])
        lam = keep("lam", [P, 4])
        neglam = keep("neglam", [P, 1])
        subg = keep("subg", [P, 1])

        gate0 = top[0]
        gate = keep("gate", [P, 2 * KD, SEQ])
        xin, o = at("xin", [P, NB, D], gate0)
        metain, o = at("metain", [META, 2, D], o)
        junk, o = at("junk", [P, D], o)
        wuk, o = at("wuk", [P, NH * HD], o)
        rows, o = at("rows", [NROWS, P], o)
        lam4, o = at("lam4", [P, 4, HD], o)
        lamj, o = at("lamj", [P, HD], o)
        assert o <= top[0]

        hn0 = top[0]
        hn = keep("hn", [P, 2, KD, NKEY], F32R)
        oA, o = at("oA", [P, 2, 4, SEQ], hn0, F32R)
        oB, _ = at("oB", [P, 2, 4, SEQ], o, F32R)
        W3, o = at("W3", [P, 3, NKEY], o)
        PT, o = at("PT", [P, 2, (NB + 1) * P], o)
        lat, o = at("lat", [P, 2, P], o)
        assert o <= top[0]
        W6, o = at("W6", [P, 3, 2, NKEY], gate0)
        PT2, o = at("PT2", [P, 2, (NB + 1) * P], o)
        assert o <= hn0

        ar0 = top[0]
        squares, _ = at("squares", [P, D], ar0)
        aqT, o = at("aqT", [P, 4, SEQ], ar0)
        biasA, o = at("biasA", [P, NH, NEAR], o)
        qabs, _ = at("qabs", [P, NH, SEQ], ar0)
        biasB, o = at("biasB", [P, NH, NKEY], o)
        akT, o = at("akT", [P, NKEY], o)
        avn, o = at("avn", [P, NB + 1, P], o)
        cT, o = at("cT", [P, NKEY], o)
        cn, o = at("cn", [P, NB + 1, P], o)
        o1 = o
        bqT, o = at("bqT", [P, 2, SEQ], o)
        acc, o = at("acc", [P, NB, NKEY], o1)
        W3a, o = at("W3a", [P, 3, NEAR], o)
        o2 = max(o, o1 + 3 * 4 * SEQ * 2)
        bkvT, o = at("bkvT", [P, NKEY], o2)
        ikwT, o = at("ikwT", [P, NKEY], o)
        avT, o = at("avT", [P, NKEY], o)
        ikn, o = at("ikn", [P, NB + 1, P], o)
        ikx, o = at("ikx", [P, NB + 1, HD], o)
        iqT, o3 = at("iqT", [P, 2, SEQ], o2)
        ikT, o3 = at("ikT", [P, NKEY], o3)
        relu, o3 = at("relu", [P, 2, NKEY], o3)
        on, o4 = at("on", [P, NB, SEQ], o2)
        PTa, o4 = at("PTa", [P, 2, NEAR + P], o4)
        o = max(o, o3)
        causal, o = at("causal", [P, NKEY], o)
        assert o4 <= o
        tail = o
        qT, o = at("qT", [P, 4, SEQ], tail)
        selm, _ = at("selm", [P, NB, NKEY], o, BF16)
        diag, o6 = at("diag", [P, NB, P], o)
        sq, o6 = at("sq", [P, SEQ], o6)
        sqacc, _ = at("sqacc", [P, 2, SEQ], tail)
        hotA, o5 = at("hotA", [BUCKETS + 1, LEN_A], tail)
        hotB, o5 = at("hotB", [BUCKETS + 1, LEN_B], o5)
        assert o5 <= o
        fA, o7 = at("fA", [NH, LEN_A], gate0)
        fB, o7 = at("fB", [NH, LEN_B], o7)
        bqg, o7 = at("bqg", [P, 2, 2, SEQ], o7, F32R)
        qaT, o = at("qaT", [P, 4, SEQ], ar0)
        kaT, o = at("kaT", [P, 4, NKEY], o)
        kbT, o = at("kbT", [P, NKEY], o)
        yw, _ = at("yw", [P, NB, SEQ], o)
        van, o = at("van", [P, NB + 1, SEQ], o)
        vbn, o = at("vbn", [P, NB + 1, P], o)
        qbT, o = at("qbT", [P, 4, SEQ], o)
        dist, o = at("dist", [P, DIST], o)
        biasD, o = at("biasD", [P, 4, NKEY], o)
        o1 = o
        biasW, o = at("biasW", [P, NH, META + WIN2 + META], o1)
        vaT, o2 = at("vaT", [P, 4, NKEY], o1)
        vbT, o2 = at("vbT", [P, NKEY], o2)
        assert max(o, o2) <= tail
        yn, _ = at("yn", [P, NB, SEQ], tail)
        W3b, o = at("W3b", [P, 3, META + WIN2], ar0)
        PTb, o = at("PTb", [P, 2, WIN2 + P], o)
        mix, o = at("mix", [P, 2, KD, SEQ], ar0, F32R)
        mix32, _ = at("mix32", [P, 3, SEQ], o)
        hid, o = at("hid", [P, 2, NFH, SEQ], ar0, F32R)
        ft, o = at("ft", [P, 5, SEQ], o)
        assert o <= tail
        hgf, _ = at("hgf", [P, KD, SEQ], hn0)
        yout, _ = at("yout", [P, NB, D], gate0)

        psL = ctx.enter_context(nc.psum_tensor("psL", [P, 2, 512], F32))
        psS = ctx.enter_context(nc.psum_tensor("psS", [P, 4, 512], F32))

        def x_bank(k):
            return (psL[:, k % 2, :], psS[:, 2 + k % 2, :])[k // 2 % 2]

        def o_bank(i):
            return psS[:, 1, :] if i == 1 else psL[:, 1, :]

        psT = ctx.enter_context(nc.psum_tensor("psT", [P, 2, 512], F32))

        def fin_bank(n, half):
            return psS[:, n, :] if half == 0 else (psL[:, 0, :], psL[:, 1, :], psT[:, 0, :], psS[:, 0, :])[n]

        fA_dram = nc.dram_tensor("bias_by_distance_A", [NH, P, LEN_A + 1], F32).ap()
        fB_dram = nc.dram_tensor("bias_by_distance_B", [NH, P, LEN_B + 1], F32).ap()

        w_in = [sem(f"w_in{b}") for b in range(2)]
        hi = [sem(f"hi{b}") for b in range(2)]
        lo = [sem(f"lo{b}") for b in range(2)]
        mm = [sem(f"mm{b}") for b in range(2)]
        ev = [sem(f"ev{b}") for b in range(2)]
        x_in = [sem(f"x_in{q}") for q in range(4)]
        dve_own = sem("dve_own")
        pool_own = sem("pool_own")
        meta_in, g1_in, rows_in, tab_in, vec_in, wuk_in, lam_in, lam_sum = [
            sem(n) for n in "meta_in g1_in rows_in tab_in vec_in wuk_in lam_in lam_sum".split()]
        consts, zeros, gvec_t, gvec_ok, x_t, x_taken, xlo, x_sq, meta_sq, meta_ok, meta_t, metaT_ok, mhi, mlo = [
            sem(n) for n in "consts zeros gvec_t gvec_ok x_t x_taken xlo x_sq meta_sq meta_ok meta_t metaT_ok mhi mlo".split()]
        f_mm, fA_ok, f_out, bias_in = [sem(n) for n in "f_mm fA_ok f_out bias_in".split()]
        diag_ok, bcast, R_ok, ssq_in, ssq_mm = [
            sem(n) for n in "diag_ok bcast R_ok ssq_in ssq_mm".split()]
        nat_t, nat_taken, nat_ok, key_t, key_taken, bqhi, bqlo = [
            sem(n) for n in "nat_t nat_taken nat_ok key_t key_taken bqhi bqlo".split()]
        lg_mm, lg_taken, lg_used = [sem(n) for n in "lg_mm lg_taken lg_used".split()]
        sel_ok, qabs_mm, qabs_ok = [sem(n) for n in "sel_ok qabs_mm qabs_ok".split()]
        th_ok = [sem(f"th_ok{b}") for b in range(2)]
        ph = {}
        for n in ("w1", "la", "df", "w2"):
            ph[n] = {k: sem(f"{n}_{k}") for k in "s neg p pt ptx pv lat o es on".split()}
        oT_mm, o_hi, o_lo = [sem(n) for n in "oT_mm o_hi o_lo".split()]
        mix_ok, mix_hi, mix_lo, t_ok, hid_ok, hid_hi, hid_lo = [
            sem(n) for n in "mix_ok mix_hi mix_lo t_ok hid_ok hid_hi hid_lo".split()]
        h_sq, h_sq2, hg_hi, hg_lo = [sem(n) for n in "h_sq h_sq2 hg_hi hg_lo".split()]
        biasD_ok, biasW_ok, dist_ok, df_sum, y_sq, lam_e = [
            sem(n) for n in "biasD_ok biasW_ok dist_ok df_sum y_sq lam_e".split()]
        fin_gain, fin_rms, fin_out = sem("fin_gain"), sem("fin_rms"), sem("fin_out")
        fin_t, fin_ok = [sem("fin_t0"), sem("fin_t1")], [sem("fin_ok0"), sem("fin_ok1")]

        block = ctx.enter_context(nc.Block())

        def by_rows(w, k0=0, kc=None):
            v = w.rearrange("(k p) n -> p k n", p=P)
            return v if kc is None else v[:, k0:k0 + kc, :]

        win1, win2 = by_rows(t["w_in"][0]), by_rows(t["w_in_2"][0])

        @block.sync
        def _(sp):
            def load(name, i, b, src, col, piece=0, width=P):
                kc = KC[name]
                slot = stage[:, b, 0:kc * P].rearrange("p (k n) -> p k n", k=kc)
                if piece == 0 and not (name == "kv1" and isinstance(i, int) and i == 0):
                    sp.wait_ge(lo[b], PAIR0[name] + i)
                sp.dma_start(slot[:, :, piece:piece + width], src[:, :, bass.ds(col, width)]).then_inc(w_in[b], 16)

            kv_cols = (1024, 1408, 512, 640)
            XQ = D // 4
            for q in range(4):
                sp.dma_start(xin[:, :, q * XQ:(q + 1) * XQ], t["x"][0].rearrange("(n p) d -> p n d", p=P)[:, :, q * XQ:(q + 1) * XQ]).then_inc(x_in[q], 16)
                if q == 0:
                    load("kv1", 0, 0, win1, kv_cols[0])
            load("kv1", 0, 1, win1, kv_cols[1])
            for name, n in ROWS[1:]:
                src = t[name].rearrange("a (k p) -> (a k) p", p=P) if len(t[name].shape) == 2 else t[name].rearrange("(k p) -> k p", p=P)
                sp.dma_start(rows[ROW[name]:ROW[name] + n, :], src).then_inc(rows_in, 16)
            sp.dma_start(tab[0:BUCKETS, :], t["rel_bias"]).then_inc(tab_in, 16)
            sp.dma_start(hotA[:], t["hot_a"]).then_inc(tab_in, 16)
            sp.dma_start(hotB[:], t["hot_b"]).then_inc(tab_in, 16)
            for n in range(2, 4):
                load("kv1", 1, n % 2, win1, kv_cols[n])
            sp.dma_start(wuk[:], t["w_uk"][0].rearrange("c h d -> c (h d)")).then_inc(wuk_in, 16)
            sp.dma_start(wuv[:], t["w_uv"][0].rearrange("c h d -> c (h d)")).then_inc(wuk_in, 16)
            for n in range(2):
                load("bq1", 0, n, win1, 768 + n * P)
            for n in range(2):
                load("iq1", 0, n, win1, 1152 + n * P)
            for n in range(4):
                for half in range(2):
                    load("aq1", n // 2, n % 2, win1, (n + 4 * half) * HD, half * HD, HD)
            for n in range(4):
                load("uq1", n // 2, n % 2, by_rows(t["w_uq"][0]), n * P)

            def layer_rest(l, win, gates_at, wa, wb, wo, wg, wu, wd):
                with sp.Fori(0, PAIRS[f"gates{l}"]) as i:
                    for b in range(2):
                        load(f"gates{l}", i, b, win, i * (2 * P) + (gates_at + b * P))
                with sp.Fori(0, PAIRS[f"br{l}"]) as i:
                    load(f"br{l}", i, 0, by_rows(wa), i * P)
                    load(f"br{l}", i, 1, by_rows(wb), i * P)
                with sp.Fori(0, PAIRS[f"out{l}"]) as i:
                    for b in range(2):
                        load(f"out{l}", i, b, by_rows(wo), i * (2 * P) + b * P)
                for half, ab in enumerate("ab"):
                    with sp.Fori(0, PAIRS[f"gu{l}{ab}"]) as i:
                        load(f"gu{l}{ab}", i, 0, by_rows(wg), i * P + half * NFH * P)
                        load(f"gu{l}{ab}", i, 1, by_rows(wu), i * P + half * NFH * P)
                    with sp.Fori(0, PAIRS[f"dn{l}{ab}"]) as i:
                        for b in range(2):
                            load(f"dn{l}{ab}", i, b, by_rows(wd, half * NFH, NFH), i * (2 * P) + b * P)

            layer_rest(1, win1, 1476, t["w_branch_a"][0], t["w_branch_b"][0], t["w_out"][0],
                       t["w_ffn_gate"][0], t["w_ffn_up"][0], t["w_ffn_down"][0])
            with sp.Fori(0, PAIRS["kv2"] - 1) as i:
                for b in range(2):
                    load("kv2", i, b, win2, i * (2 * P) + (512 + b * P))
            for b in range(2):
                load("kv2", PAIRS["kv2"] - 1, b, win2, 2048 + b * P)
            with sp.Fori(0, PAIRS["qa2"]) as i:
                for b in range(2):
                    load("qa2", i, b, win2, i * (2 * P) + b * P)
            for n in range(4):
                for half in range(2):
                    load("qb2", n // 2, n % 2, win2, 1536 + (n + 4 * half) * HD, half * HD, HD)
            layer_rest(2, win2, 2304, t["w_branch_a_2"][0], t["w_branch_b_2"][0], t["w_out_2"][0],
                       t["w_ff_gate_2"][0], t["w_ff_up_2"][0], t["w_ff_down_2"][0])
            for n in range(NB):
                for half in range(2):
                    sp.wait_ge(fin_ok[half], n + 1)
                    cols = slice(half * SEQ, (half + 1) * SEQ)
                    sp.dma_start(out[0, n * P:(n + 1) * P, cols], yout[:, n, cols]).then_inc(fin_out, 16)
            sp.wait_ge(fin_out, 2 * NB * 16)

        @block.gpsimd
        def _(pool):
            own = Tally(pool, pool_own)
            own.link(pool.memset(ident[:], 0.0))
            own.link(pool.affine_select(out=ident[:], in_=ident[:], compare_op=ALU.not_equal, fill=1.0, base=0,
                                        pattern=[[-1, P]], channel_multiplier=1))
            own.link(pool.tensor_copy(identb[:], ident[:]))
            own.link(pool.memset(tab[BUCKETS:BUCKETS + 1, :], NEG))
            own.link(pool.memset(Rk[:, 0:META], 1.0))
            pool.memset(ones[:], 1.0).then_inc(consts, 1)
            for l, name in enumerate(("sinks", "sink_logits_2")):
                src = t[name]
                pool.dma_start(sinkb[:, l, :], bass.AP(tensor=src.tensor, offset=0, ap=[[0, P], [1, NH]])).then_inc(vec_in, 16)
            pool.dma_start(kvg[:], bass.AP(tensor=t["kv_norm_g"].tensor, offset=0, ap=[[0, P], [1, P]])).then_inc(vec_in, 16)
            for n, name in enumerate(("idx_k_ln_g", "idx_k_ln_b")):
                pool.dma_start(ikg[:, n, :], bass.AP(tensor=t[name].tensor, offset=0, ap=[[0, P], [1, HD]])).then_inc(vec_in, 16)
            for n, name in enumerate(("lambda_q1_2", "lambda_k1_2", "lambda_q2_2", "lambda_k2_2")):
                pool.dma_start(lam4[:, n, :], bass.AP(tensor=t[name].tensor, offset=0, ap=[[0, P], [1, HD]])).then_inc(lam_in, 16)
            for tile_ in (cn, ikn, avn):
                pool.memset(tile_[:, MC, :], 0.0)
            own.link(pool.memset(causal[:], 0.0))
            pool.affine_select(out=causal[:], in_=causal[:], compare_op=ALU.is_ge, fill=NEG, base=NKEY - P,
                               pattern=[[-1, NKEY]], channel_multiplier=1).then_inc(zeros, 1)
            def low(name, i, b):
                pool.wait_ge(hi[b], PAIR0[name] + i + 1)
                n = KC[name] * P
                pool.tensor_tensor(wl[:, b, 0:n], stage[:, b, 0:n], wh[:, b, 0:n].bitcast(F32), ALU.subtract).then_inc(lo[b], 1)

            def low_pair(name, i):
                low(name, i, 0)
                low(name, i, 1)

            def lows(name):
                with pool.Fori(0, PAIRS[name]) as i:
                    low_pair(name, i)

            tables = ((fA, fA_dram, LEN_A, biasA, NEAR), (fB, fB_dram, LEN_B, biasB, NKEY))

            def bias_out(h):
                for f, dram, length, _, _ in tables:
                    pool.dma_start(dram[h:h + 2, :, 0:length], f[h:h + 2, :].unsqueeze(1).broadcast_to([2, P, length])).then_inc(f_out, 16)

            def bias_back(h):
                for _, dram, length, tile_, width in tables:
                    src = bass.AP(tensor=dram.tensor, offset=h * P * (length + 1) + P - 1, ap=[[length, P], [P * (length + 1), 2], [1, width]])
                    pool.dma_start(tile_[:, h:h + 2, :], src).then_inc(bias_in, 16)

            pool.wait_ge(fA_ok, 2)
            bias_out(0)
            bias_out(2)
            low_pair("iq1", 0)
            bias_out(4)
            bias_out(6)
            low_pair("aq1", 0)
            pool.wait_ge(f_out, 8 * 16)
            bias_back(0)
            low_pair("aq1", 1)
            bias_back(2)
            low_pair("uq1", 0)
            bias_back(4)
            bias_back(6)
            low_pair("uq1", 1)
            lows("gates1")
            lows("br1")
            pool.wait_ge(ev[1], PAIR0["kv2"] + 1)
            pool.iota(dist[:], pattern=[[-1, DIST]], base=3 * P, channel_multiplier=1,
                      allow_small_or_imprecise_dtypes=True).then_inc(dist_ok, 1)

            def bias_block(i):
                if i:
                    pool.wait_ge(ph["df"]["neg"], 8 * i)
                for h in range(4):
                    pool.tensor_scalar(biasD[:, h, META:NKEY], dist[:, 3 * P - P * i:3 * P - P * i + SEQ],
                                       -(2.0 ** (-8.0 * (h + 1) / 4)), None, ALU.mult).then_inc(biasD_ok, 1)

            def bias_window(h0, h1):
                for h in range(h0, h1):
                    pool.tensor_scalar(biasW[:, h, META:META + WIN2], tmp[:, 0, 0:WIN2],
                                       -(2.0 ** -(h + 1.0)), None, ALU.mult).then_inc(biasW_ok, 1)

            low_pair("qa2", 0)
            low_pair("qa2", 1)
            pool.wait_ge(dist_ok, 2)
            pool.memset(biasD[:, :, 0:META], 0.0)
            low_pair("qb2", 0)
            low_pair("qb2", 1)
            bias_block(0)
            bias_block(1)
            pool.wait_ge(nat_t, 3)
            pool.wait_ge(dist_ok, 3)
            pool.memset(biasW[:, :, 0:META], 0.0)
            pool.memset(biasW[:, :, META + WIN2:], 0.0)
            bias_window(0, NH // 2)
            bias_block(2)
            bias_window(NH // 2, NH)
            bias_block(3)
            lows("gates2")
            lows("br2")

        @block.scalar
        def _(act):
            act.preload_act_table(ACT.Exp)
            act.dma_start(rows[0:KD, :], t["attn_norm_g"].rearrange("a (k p) -> (a k) p", p=P)).then_inc(g1_in, 16)
            act.dma_start(metain[:, 0, :], t["meta_tokens"]).then_inc(meta_in, 16)
            act.dma_start(metain[:, 1, :], t["meta_tokens_2"]).then_inc(meta_in, 16)

            def high(name, i, b):
                act.wait_ge(w_in[b], 16 * (LOAD0[name] + LOADS[name]) + i * (16 * LOADS[name]))
                if not (name == "kv1" and isinstance(i, int) and i == 0):
                    act.wait_ge(mm[b], PAIR0[name] + i)
                n = KC[name] * P
                act.activation(wh[:, b, 0:n], stage[:, b, 0:n], ACT.Copy).then_inc(hi[b], 1)

            def high_next(name, i, last):
                if not last:
                    high(name, i + 1, 0)
                elif AFTER[name]:
                    high(AFTER[name], 0, 0)

            def only_high(name):
                if PAIRS[name] == 2:
                    high(name, 0, 1)
                    high_next(name, 0, False)
                elif PAIRS[name] > 2:
                    with act.Fori(0, PAIRS[name] - 1) as i:
                        high(name, i, 1)
                        high_next(name, i, False)
                high(name, PAIRS[name] - 1, 1)
                high_next(name, PAIRS[name] - 1, True)

            for k in range(KD):
                act.wait_ge(x_t, k + 1)
                if k == 0:
                    act.wait_ge(gvec_ok, 1)
                g = ROW["attn_norm_g"] + k
                act.activation(hn[:, 0, k, META:], x_bank(k), ACT.Copy, scale=gvec[:, g:g + 1])
                act.activation(hT[:, k, :], x_bank(k), ACT.Copy).then_inc(x_taken, 1)
                if k == 1:
                    high("kv1", 0, 0)
                if k == 2:
                    act.wait_ge(meta_in, 32)
                    for n in range(2):
                        if n:
                            act.wait_ge(meta_sq, n)
                        act.activation(junk[0:META, :], metain[:, n, :], ACT.Square, accum_out=st[0:META, 1, n:n + 1]).then_inc(meta_sq, 1)
            act.wait_ge(metaT_ok, 1)
            act.activation(hn[:, 0, :, 0:META], metaT[:, 0, :, :], ACT.Copy).then_inc(mhi, 1)
            high("kv1", 0, 1)
            act.wait_ge(meta_sq, 2)
            for q in range(4):
                act.wait_ge(x_in[q], 16)
            for n in range(NB - 1):
                if n:
                    act.wait_ge(x_sq, n)
                act.activation(junk[:], xin[:, n, :], ACT.Square, accum_out=st[:, 0, n:n + 1]).then_inc(x_sq, 1)
            high("kv1", 1, 0)
            act.wait_ge(lam_sum, 1)
            act.activation(lam[:, 2:4], lam[:, 0:2], ACT.Exp).then_inc(lam_e, 1)
            high("kv1", 1, 1)
            high_next("kv1", 1, True)
            for name in ("bq1", "iq1", "aq1"):
                only_high(name)
            act.wait_ge(ssq_in, 1)
            for k in range(2):
                g = ROW["q_norm_g"] + k
                act.activation(bqg[:, 0, k, :], bqT[:, k, :], ACT.Copy, scale=gvec[:, g:g + 1]).then_inc(bqhi, 1)
            high("uq1", 0, 1)
            high("uq1", 1, 0)
            for u in range(4 * NB):
                K = META + P * (u // 4 + 1)
                act.wait_ge(lg_mm, u + 1)
                if u >= 2:
                    act.wait_ge(lg_used, u - 1)
                src = psS[:, 2 * (u % 2):2 * (u % 2) + 2, :]
                if K > 512:
                    act.activation(relu[:, u % 2, :].rearrange("p (a b) -> p a b", a=2), src[:, :, 0:K // 2], ACT.Relu).then_inc(lg_taken, 1)
                else:
                    act.activation(relu[:, u % 2, 0:K], src[:, 0, 0:K], ACT.Relu).then_inc(lg_taken, 1)
                if u == 5:
                    high("uq1", 1, 1)
                if u == 9:
                    high_next("uq1", 1, True)

            def gate_high(l, j):
                for step in range(2 * KD):
                    if GATE_START[l][step] == j:
                        if step % 2 == 0:
                            high(f"gates{l}", step // 2, 1)
                        else:
                            high_next(f"gates{l}", step // 2, step == 2 * KD - 1)

            def gate_tanh(l, j):
                for step in range(2 * KD):
                    if GATE_DONE[l][step] == j - 2:
                        i, b = divmod(step, 2)
                        act.wait_ge(ev[b], PAIR0[f"gates{l}"] + i + 1)
                        bias = bhalf[:, step:step + 1] if l == 1 else 0.0
                        act.activation(gate[:, step, :], tmp[:, b, :], ACT.Tanh, bias=bias, scale=0.5).then_inc(th_ok[b], 1)

            def softmax_unit(p, u, tile, col):
                act.wait_ge(p["neg"], u + 1)
                act.activation(tile, tile, ACT.Exp, bias=negm[:, col:col + 1],
                               accum_out=rsum[:, col:col + 1]).then_inc(p["p"], 1)

            def sink_part(p, l, i):
                act.wait_ge(p["es"], 2 * i + 1)
                act.activation(st[:, 3, :], st[:, 2, :], ACT.Exp).then_inc(p["es"], 1)

            def take_pt(p, u, chunks, dst):
                act.wait_ge(p["pt"], u + 1)
                if u >= 2:
                    act.wait_ge(p["pv"], u - 1)
                whole = [c for c in chunks if c[2] == P]
                if any(c[2] == META for c in chunks):
                    act.activation(dst[0:META, dst.shape[-1] - P:], psT[0:META, 1, 0:P], ACT.Copy)
                act.activation(dst[:, 0:len(whole) * P], psT[:, 0, 0:len(whole) * P], ACT.Copy).then_inc(p["ptx"], 1)

            def heads_high(m, dst, gain=1.0):
                for i in range(NB):
                    act.wait_ge(oT_mm, NB * m + i + 1)
                    act.activation(dst[:, 0, :, i * P:(i + 1) * P], psS[:, i, :].rearrange("p (c q) -> p c q", c=4),
                                   ACT.Copy, scale=gain).then_inc(o_hi, 1)

            units = list(window1_units())
            p = ph["w1"]
            for j in range(len(units) + 5):
                gate_high(1, j)
                if j < len(units):
                    softmax_unit(p, j, W3a[:, j % 3, 0:units[j][3]], j)
                gate_tanh(1, j)
                if 2 <= j < len(units) + 2:
                    take_pt(p, j - 2, units[j - 2][4], PTa[:, j % 2, :])
                if 3 <= j < len(units) + 3 and (j - 3) % NH == NH - 1:
                    sink_part(p, 0, (j - 3) // NH)
            heads_high(0, oA)
            units = list(latent_units())
            p = ph["la"]
            for j in range(len(units) + 2):
                if j < len(units):
                    softmax_unit(p, j, W3[:, j % 3, 0:units[j][2]], j)
                if j >= 2:
                    take_pt(p, j - 2, units[j - 2][3], PT[:, j % 2, :])
            heads_high(1, oB)

            def branches(l):
                name, m0 = f"br{l}", (l - 1) * KD

                def pair(i, last):
                    high_next(name, i, last)
                    if not last:
                        high(name, i + 1, 1)
                    act.wait_ge(mix_ok, m0 + i + 1)
                    act.activation(mix[:, 0, bass.ds(i, 1), :], mix32[:, 2, :], ACT.Copy).then_inc(mix_hi, 1)

                high(name, 0, 1)
                with act.Fori(0, PAIRS[name] - 1) as i:
                    pair(i, False)
                pair(PAIRS[name] - 1, True)

            def squares_and_gain(name, norm, grow):
                def chunk(i, b):
                    act.wait_ge(ev[b], PAIR0[name] + i + 1)
                    act.wait_ge(h_sq2, 2 * i + (squares_cleared(norm) + b))
                    act.activation(hn[:, 0, bass.ds(2 * i + b, 1), META:], hT[:, bass.ds(2 * i + b, 1), :], ACT.Copy,
                                   scale=gvec[:, bass.ds(2 * i + (grow + b), 1)]).then_inc(hg_hi, 1)
                    act.activation(sq[:], hT[:, bass.ds(2 * i + b, 1), :], ACT.Square).then_inc(h_sq, 1)

                def pair(i, last):
                    high(name, i, 1)
                    chunk(i, 0)
                    high_next(name, i, last)
                    chunk(i, 1)

                with act.Fori(0, PAIRS[name] - 1) as i:
                    pair(i, False)
                pair(PAIRS[name] - 1, True)

            def swiglu(name, f0, early=0):
                def pair(i, last, early=False):
                    high(name, i, 1)
                    if early:
                        high_next(name, i, last)
                    act.wait_ge(ev[0], PAIR0[name] + i + 1)
                    act.activation(ft[:, 1, :], ft[:, 0, :], ACT.Tanh, scale=0.5).then_inc(t_ok, 1)
                    if not early:
                        high_next(name, i, last)
                    act.wait_ge(hid_ok, f0 + i + 1)
                    act.activation(hid[:, 0, bass.ds(i, 1), :], ft[:, 4, :], ACT.Copy).then_inc(hid_hi, 1)

                for i in range(early):
                    pair(i, False, True)
                with act.Fori(early, PAIRS[name] - 1) as i:
                    pair(i, False)
                pair(PAIRS[name] - 1, True)

            branches(1)
            squares_and_gain("out1", 0, ROW["ffn_norm_g"])
            swiglu("gu1a", 0, 1)
            only_high("dn1a")
            swiglu("gu1b", NFH)
            name = "dn1b"

            def chunk1(i, b):
                act.wait_ge(ev[b], PAIR0[name] + i + 1)
                act.wait_ge(h_sq2, 2 * i + (squares_cleared(1) + b))
                n = bass.ds(2 * i + b, 1)
                act.activation(hn[:, 0, n, META:], hT[:, n, :], ACT.Copy, scale=g12[:, n]).then_inc(hg_hi, 1)
                act.activation(tmp[:, 0, :], hT[:, n, :], ACT.Square)
                act.activation(tmp[:, 1, :], hT[:, n, :], ACT.Square,
                               scale=gvec[:, bass.ds(2 * i + (ROW["final_norm_g"] + b), 1)]).then_inc(h_sq, 1)

            def pair1(i, last):
                high(name, i, 1)
                chunk1(i, 0)
                high_next(name, i, last)
                chunk1(i, 1)

            act.wait_ge(mm[1], PAIR0[name])
            act.activation(hn[:, 0, :, 0:META], metaT[:, 1, :, :], ACT.Copy).then_inc(mhi, 1)
            with act.Fori(0, PAIRS[name] - 1) as i:
                pair1(i, False)
            pair1(PAIRS[name] - 1, True)

            for name in ("kv2", "qa2", "qb2"):
                only_high(name)
            p = ph["df"]
            for j in range(16 + 2):
                if j < 16:
                    for m in range(2):
                        softmax_unit(p, 2 * j + m, W6[:, j % 3, m, :], 2 * j + m)
                if j >= 2:
                    take_pt(p, j - 2, [(MC, 0, META)] + [(c, 0, P) for c in range(NB)], PT2[:, j % 2, :])
            units = list(window2_units())
            p = ph["w2"]
            for j in range(len(units) + 6):
                gate_high(2, j)
                if j < len(units):
                    softmax_unit(p, j, W3b[:, j % 3, 0:units[j][3] + META], j)
                gate_tanh(2, j)
                if j in Y_NORM:
                    i = Y_NORM.index(j)
                    act.wait_ge(ph["df"]["on"], NB)
                    if i:
                        act.wait_ge(y_sq, 2 * i)
                    act.activation(sq[:], yn[:, i, :], ACT.Square).then_inc(y_sq, 1)
                if j >= 2 and j - 2 < len(units):
                    take_pt(p, j - 2, units[j - 2][7], PTb[:, j % 2, :])
                if 3 <= j < len(units) + 3 and (j - 3) % NH == NH - 1:
                    sink_part(p, 1, (j - 3) // NH)
            heads_high(2, oA, subg[:])
            heads_high(3, oB)
            branches(2)
            squares_and_gain("out2", 2, ROW["norm_ffn_2"])
            swiglu("gu2a", 2 * NFH, 1)
            only_high("dn2a")
            swiglu("gu2b", 3 * NFH)
            name = "dn2b"

            def chunk2(i, b):
                act.wait_ge(ev[b], PAIR0[name] + i + 1)
                act.wait_ge(h_sq2, 2 * i + (squares_cleared(3) + b))
                act.activation(sq[:], hT[:, bass.ds(2 * i + b, 1), :], ACT.Square).then_inc(h_sq, 1)
                act.activation(hgf[:, bass.ds(2 * i + b, 1), :], hT[:, bass.ds(2 * i + b, 1), :], ACT.Copy,
                               scale=gvec[:, bass.ds(2 * i + (ROW["norm_final_2"] + b), 1)]).then_inc(fin_gain, 1)

            def pair2(i, last):
                high(name, i, 1)
                chunk2(i, 0)
                high_next(name, i, last)
                chunk2(i, 1)

            with act.Fori(0, PAIRS[name] - 1) as i:
                pair2(i, False)
            pair2(PAIRS[name] - 1, True)
            act.wait_ge(fin_rms, 1)
            for n in range(NB):
                act.wait_ge(fin_t[1], n + 1)
                act.activation(yout[:, n, SEQ:D], fin_bank(n, 1), ACT.Copy, scale=st[:, 9, n:n + 1]).then_inc(fin_ok[1], 1)

        @block.vector
        def _(v):
            dv = Tally(v, dve_own)

            def spread(ap, width):
                return ap.unsqueeze(2).broadcast_to([ap.shape[0], ap.shape[1], width])

            def low(name, i, b):
                if name in POOL_LOW:
                    return
                v.wait_ge(hi[b], PAIR0[name] + i + 1)
                n = KC[name] * P
                v.tensor_tensor(wl[:, b, 0:n], stage[:, b, 0:n], wh[:, b, 0:n].bitcast(F32), ALU.subtract).then_inc(lo[b], 1)

            def low_next(name, i, last):
                if not last:
                    low(name, i + 1, 0)
                elif AFTER[name]:
                    low(AFTER[name], 0, 0)

            def done(name, i, b):
                v.wait_ge(mm[b], PAIR0[name] + i + 1)

            def pairs(name, pair, first=0):
                if PAIRS[name] - 1 > first:
                    with v.Fori(first, PAIRS[name] - 1) as i:
                        pair(i, False)
                pair(PAIRS[name] - 1, True)

            def rsqrt(x, y, n, parts=P):
                step = rst[0:parts, 0:n]
                c = 3 / 8
                dv.link(v.tensor_scalar(y.bitcast(I32), x.bitcast(I32), -0.5, RSQRT_SEED, ALU.mult, ALU.add))
                dv.link(v.tensor_tensor(step, y, y, ALU.mult))
                dv.link(v.tensor_tensor(step, step, x, ALU.mult))
                dv.link(v.scalar_tensor_tensor(out=step, in0=step, scalar=-10 / 3, in1=step, op0=ALU.add, op1=ALU.mult))
                dv.link(v.scalar_tensor_tensor(out=y, in0=step, scalar=5.0, in1=y, op0=ALU.add, op1=ALU.mult))
                dv.link(v.scalar_tensor_tensor(out=step, in0=y, scalar=-0.5 * c ** 3, in1=y, op0=ALU.mult, op1=ALU.mult))
                dv.link(v.tensor_tensor(step, step, x, ALU.mult))
                dv.link(v.scalar_tensor_tensor(out=y, in0=step, scalar=1.5 * c, in1=y, op0=ALU.add, op1=ALU.mult))

            def diagonals(dst, r):
                for n in range(NB):
                    ins = v.tensor_scalar(dst[:, n, :], ident[:], r[:, n:n + 1], None, ALU.mult)
                return ins

            def x_low(k):
                g = ROW["attn_norm_g"] + k
                v.wait_ge(x_taken, k + 1)
                v.scalar_tensor_tensor(out=hn[:, 1, k, META:], in0=hT[:, k, :], scalar=gvec[:, g:g + 1],
                                       in1=hn[:, 0, k, META:].bitcast(F32), op0=ALU.mult, op1=ALU.subtract).then_inc(xlo, 1)

            v.wait_ge(gvec_t, 1)
            v.tensor_copy(gvec[:, 0:KD], psT[:, 1, 0:KD]).then_inc(gvec_ok, 1)
            v.wait_ge(gvec_ok, 1)
            def meta_low(count):
                v.wait_ge(mhi, count)
                v.tensor_tensor(hn[:, 1, :, 0:META], metaT[:, count - 1, :, :], hn[:, 0, :, 0:META].bitcast(F32), ALU.subtract).then_inc(mlo, 1)

            x_low(0)
            x_low(1)
            low("kv1", 0, 0)
            x_low(2)
            v.wait_ge(meta_sq, 2)
            dv.link(v.tensor_scalar(st[0:META, 1, 2:4], st[0:META, 1, 0:2], 1.0 / D, EPS, ALU.mult, ALU.add))
            rsqrt(st[0:META, 1, 2:4], rs[0:META, 0:2], 2, META)
            for n in range(2):
                v.tensor_scalar(metain[:, n, :], metain[:, n, :], rs[0:META, n:n + 1], None, ALU.mult).then_inc(meta_ok, 1)
            for k in range(3, 6):
                x_low(k)
            v.wait_ge(gvec_t, 2)
            v.tensor_copy(gvec[:, KD:], psT[:, 1, KD:NROWS]).then_inc(gvec_ok, 1)
            v.wait_ge(gvec_ok, 2)
            v.wait_ge(meta_t, 1)
            for l, name in enumerate(("attn_norm_g", "norm_mix_2")):
                ins = v.tensor_tensor(metaT[:, l, :, :], psT[:, 0, l * P:(l + 1) * P].rearrange("p (k m) -> p k m", k=KD),
                                      spread(gvec[:, ROW[name]:ROW[name] + KD], META), ALU.mult)
            ins.then_inc(metaT_ok, 1)
            for k in range(6, KD):
                x_low(k)
            meta_low(1)
            low("kv1", 0, 1)
            v.wait_ge(lam_in, 64)
            dv.link(v.tensor_tensor_reduce(out=lamj[:], in0=lam4[:, 0, :], in1=lam4[:, 1, :], scale=1.0, scalar=0.0,
                                           op0=ALU.mult, op1=ALU.add, accum_out=lam[:, 0:1]))
            dv.link(v.tensor_tensor_reduce(out=lamj[:], in0=lam4[:, 2, :], in1=lam4[:, 3, :], scale=1.0, scalar=0.0,
                                           op0=ALU.mult, op1=ALU.add, accum_out=lam[:, 1:2]))
            v.memset(lamj[:, 0:1], 0.0).then_inc(lam_sum, 1)
            for q in range(4):
                v.wait_ge(x_in[q], 16)
            for n in range(NB - 1, NB):
                dv.link(v.tensor_tensor_reduce(out=squares[:], in0=xin[:, n, :], in1=xin[:, n, :], scale=1.0, scalar=0.0,
                                               op0=ALU.mult, op1=ALU.add, accum_out=st[:, 0, n:n + 1]))
            v.wait_ge(x_sq, NB - 1)
            dv.link(v.tensor_scalar(st[:, 0, 4:8], st[:, 0, 0:4], 1.0 / D, EPS, ALU.mult, ALU.add))
            rsqrt(st[:, 0, 4:8], rs[:, 0:4], 4)
            v.wait_ge(consts, 1)
            diagonals(diag, rs[:, 0:4]).then_inc(diag_ok, 1)
            low("kv1", 1, 0)
            v.wait_ge(bcast, 1)
            v.tensor_copy(R, psT[:, 1, :]).then_inc(R_ok, 1)
            v.wait_ge(R_ok, 1)

            def start_rest():
                b0 = ROW["b_gates"]
                g = ROW["subln_gain_2"]
                dv.link(v.tensor_scalar(subg[:], gvec[:, g:g + 1], 1.0 - LAMBDA0, None, ALU.mult))
                g1, g2 = ROW["final_norm_g"], ROW["norm_mix_2"]
                dv.link(v.tensor_tensor(g12[:], gvec[:, g1:g1 + KD], gvec[:, g2:g2 + KD], ALU.mult))
                dv.link(v.tensor_scalar(bhalf[:], gvec[:, b0:b0 + 2 * KD], 0.5, None, ALU.mult))
                v.wait_ge(f_mm, 1)
                v.tensor_copy(fA[:], psL[0:NH, 0, 0:LEN_A]).then_inc(fA_ok, 1)
                v.wait_ge(f_mm, 2)
                v.tensor_copy(fB[:, 0:512], psL[0:NH, 1, :])
                v.tensor_copy(fB[:, 512:LEN_B], psT[0:NH, 0, 0:LEN_B - 512]).then_inc(fA_ok, 1)
                v.wait_ge(lam_e, 1)
                dv.link(v.tensor_tensor(neglam[:], lam[:, 3:4], lam[:, 2:3], ALU.subtract))
                dv.link(v.tensor_scalar(neglam[:], neglam[:], -LAMBDA0, None, ALU.add))

            def take_keys(name, i, b, dst):
                done(name, i, b)
                v.tensor_tensor(as_halves(dst, NKEY), psS[:, 2 * b:2 * b + 2, 0:NKEY // 2], as_halves(Rk[:], NKEY), ALU.mult).then_inc(ev[b], 1)

            def take_scaled(name, i, b, dst, by, scale=1.0):
                done(name, i, b)
                v.scalar_tensor_tensor(out=dst, in0=psL[:, b, :], scalar=scale, in1=by, op0=ALU.mult, op1=ALU.mult).then_inc(ev[b], 1)

            keys = [bkvT[:], ikwT[:], akT[:], avT[:]]
            for i in range(2):
                if i:
                    low("kv1", i, 1)
                take_keys("kv1", i, 0, keys[2 * i])
                if i:
                    low_next("kv1", i, True)
                take_keys("kv1", i, 1, keys[2 * i + 1])
                if i == 0:
                    start_rest()
            low("bq1", 0, 1)
            take_scaled("bq1", 0, 0, bqT[:, 0, :], R)
            low_next("bq1", 0, True)
            take_scaled("bq1", 0, 1, bqT[:, 1, :], R)
            v.wait_ge(ev[0], PAIR0["bq1"] + 1)
            v.wait_ge(ev[1], PAIR0["bq1"] + 1)
            dv.link(v.tensor_tensor(sq[:], bqT[:, 0, :], bqT[:, 0, :], ALU.mult))
            dv.link(v.tensor_tensor(tmp[:, 0, :], bqT[:, 1, :], bqT[:, 1, :], ALU.mult))
            v.tensor_tensor(sq[:], sq[:], tmp[:, 0, :], ALU.add).then_inc(ssq_in, 1)
            v.wait_ge(zeros, 1)
            v.wait_ge(nat_t, 1)
            for n, dst in enumerate((cn, ikn, avn)):
                dv.link(v.tensor_copy(dst[:, 0:NB, :], psS[:, n, :].rearrange("p (c f) -> p c f", c=NB)))
                ins = v.tensor_copy(dst[0:META, MC, :], psT[0:META, 0, n * P:(n + 1) * P])
            ins.then_inc(nat_taken, 1)
            v.wait_ge(nat_taken, 1)
            low("iq1", 0, 1)
            take_scaled("iq1", 0, 0, iqT[:, 0, :], R)
            low_next("iq1", 0, True)
            take_scaled("iq1", 0, 1, iqT[:, 1, :], R)
            low("aq1", 0, 1)
            take_scaled("aq1", 0, 0, aqT[:, 0, :], R, QSCALE)
            NC = NB + 1
            flat = tmp[:, :, :].rearrange("p a n -> p (a n)")
            t5 = flat[:, 0:NC * P].rearrange("p (c f) -> p c f", c=NC)
            dv.link(v.tensor_tensor(t5, cn[:], cn[:], ALU.mult))
            dv.link(v.tensor_reduce(st[:, 6, 0:NC], t5, AX_X, ALU.add))
            dv.link(v.tensor_scalar(st[:, 7, 0:NC], st[:, 6, 0:NC], 1.0 / P, EPS, ALU.mult, ALU.add))
            rsqrt(st[:, 7, 0:NC], rs[:, 0:NC], NC)
            dv.link(v.tensor_tensor(cn[:], cn[:], spread(rs[:, 0:NC], P), ALU.mult))
            v.wait_ge(vec_in, 80)
            v.tensor_tensor(cn[:], cn[:], kvg[:].unsqueeze(1).broadcast_to([P, NC, P]), ALU.mult).then_inc(nat_ok, 1)
            low_next("aq1", 0, False)
            take_scaled("aq1", 0, 1, aqT[:, 1, :], R, QSCALE)
            low("aq1", 1, 1)
            t5 = flat[:, 0:NC * HD].rearrange("p (c f) -> p c f", c=NC)
            ik = ikn[:, :, 0:HD]
            dv.link(v.tensor_scalar(iwn[:], ikn[:, 0:NB, HD:HD + 4], (4 * HD) ** -0.5, None, ALU.mult))
            dv.link(v.tensor_reduce(st[:, 6, 0:NC], ik, AX_X, ALU.add))
            dv.link(v.tensor_scalar(st[:, 7, 0:NC], st[:, 6, 0:NC], 1.0 / HD, None, ALU.mult))
            dv.link(v.tensor_tensor(ikx[:], ik, spread(st[:, 7, 0:NC], HD), ALU.subtract))
            dv.link(v.tensor_tensor(t5, ikx[:], ikx[:], ALU.mult))
            dv.link(v.tensor_reduce(st[:, 6, 0:NC], t5, AX_X, ALU.add))
            dv.link(v.tensor_scalar(st[:, 7, 0:NC], st[:, 6, 0:NC], 1.0 / HD, EPS, ALU.mult, ALU.add))
            rsqrt(st[:, 7, 0:NC], rs[:, 0:NC], NC)
            dv.link(v.tensor_tensor(ikx[:], ikx[:], spread(rs[:, 0:NC], HD), ALU.mult))
            dv.link(v.tensor_tensor(ikx[:], ikx[:], ikg[:, 0, :].unsqueeze(1).broadcast_to([P, NC, HD]), ALU.mult))
            for c in range(2):
                ins = v.tensor_tensor(ikn[:, :, c * HD:(c + 1) * HD], ikx[:], ikg[:, 1, :].unsqueeze(1).broadcast_to([P, NC, HD]), ALU.add)
            ins.then_inc(nat_ok, 1)
            take_scaled("aq1", 1, 0, aqT[:, 2, :], R, QSCALE)
            low_next("aq1", 1, True)
            v.wait_ge(ssq_mm, 1)
            dv.link(v.tensor_scalar(st[:, 7, 0:4], psT[:, 1, 0:4], 1.0 / 256, EPS, ALU.mult, ALU.add))
            rsqrt(st[:, 7, 0:4], rs[:, 0:4], 4)
            diagonals(diag, rs[:, 0:4]).then_inc(diag_ok, 1)
            v.wait_ge(bqhi, 2)
            for k in range(2):
                g = ROW["q_norm_g"] + k
                v.scalar_tensor_tensor(out=bqg[:, 1, k, :], in0=bqT[:, k, :], scalar=gvec[:, g:g + 1], in1=bqg[:, 0, k, :].bitcast(F32),
                                       op0=ALU.mult, op1=ALU.subtract).then_inc(bqlo, 1)
            take_scaled("aq1", 1, 1, aqT[:, 3, :], R, QSCALE)
            low("uq1", 0, 1)
            v.wait_ge(key_t, 1)
            for n, dst in enumerate((cT, ikT)):
                v.tensor_copy(dst[:, META:NKEY], psS[:, n, :])
                v.tensor_copy(dst[:, 0:META], psT[:, 0, n * META:(n + 1) * META])
            v.tensor_copy(wukT[:], psS[:, 2, :].rearrange("p (c f) -> p c f", c=4)).then_inc(key_taken, 1)
            v.wait_ge(bcast, 2)
            v.tensor_copy(sq[:], psT[:, 1, :]).then_inc(R_ok, 1)
            v.wait_ge(R_ok, 2)
            take_scaled("uq1", 0, 0, qT[:, 0, :], sq[:])
            for u in range(4 * NB):
                i, h = divmod(u, 4)
                K = META + P * (i + 1)
                v.wait_ge(lg_taken, u + 1)
                if h:
                    v.wait_ge(lg_used, u)
                v.scalar_tensor_tensor(out=acc[:, i, 0:K], in0=relu[:, u % 2, 0:K], scalar=iwn[:, i, h:h + 1],
                                       in1=acc[:, i, 0:K] if h else causal[:, NKEY - K:NKEY], op0=ALU.mult, op1=ALU.add).then_inc(lg_used, 1)
                if u in UQ_AFTER:
                    n, b = UQ_AFTER[u]
                    take_scaled("uq1", n, b, qT[:, 2 * n + b, :], sq[:])
            v.wait_ge(lg_used, 4 * NB)

            def gate_part(l, j):
                for step in range(2 * KD):
                    if GATE_DONE[l][step] == j - 1:
                        name, (i, b) = f"gates{l}", divmod(step, 2)
                        done(name, i, b)
                        if l == 2 or i:
                            v.wait_ge(th_ok[b], KD * (l - 1) + i)
                        v.tensor_tensor(tmp[:, b, :], psL[:, b, :], R, ALU.mult).then_inc(ev[b], 1)

            best = st[:, 9, :]
            ROUNDS = TOPK // 8

            def top_rounds(j):
                blk, n = divmod(j, ROUNDS // 2)
                K = META + P * (blk + 1)
                for _ in range(2):
                    dv.link(v.max(best, acc[:, blk, 0:K]))
                    dv.link(v.match_replace(acc[:, blk, 0:K], best, acc[:, blk, 0:K], TAKEN))
                if n == ROUNDS // 2 - 1:
                    v.tensor_scalar(selm[:, blk, 0:K], acc[:, blk, 0:K], TAKEN / 2, NEG, ALU.is_gt, ALU.mult).then_inc(sel_ok, 1)

            def biased(p, u, tile, scores, bias, least, col):
                dv.link(v.tensor_tensor_reduce(out=tile, in0=scores, in1=bias, scale=1.0, scalar=least,
                                               op0=ALU.add, op1=ALU.max, accum_out=mx[:, col:col + 1]))
                v.tensor_scalar(negm[:, col:col + 1], mx[:, col:col + 1], -1.0, None, ALU.mult).then_inc(p["neg"], 1)

            def sink_sum(p, l, i):
                v.wait_ge(p["neg"], NH * (i + 1))
                v.tensor_tensor(st[:, 2, :], sinkb[:, l, :], negm[:, i * NH:(i + 1) * NH], ALU.add).then_inc(p["es"], 1)

            def sink_normed(p, i, dst):
                v.wait_ge(p["es"], 2 * i + 2)
                dv.link(v.tensor_tensor(st[:, 4, :], st[:, 3, :], rsum[:, i * NH:(i + 1) * NH], ALU.add))
                dv.link(v.reciprocal(st[:, 5, :], st[:, 4, :]))
                v.wait_ge(p["pv"], NH * (i + 1))
                v.tensor_tensor(dst[:, i, :].rearrange("p (h d) -> p h d", h=NH), psS[:, 2 * (i % 2) + 1, :].rearrange("p (h d) -> p h d", h=NH),
                                spread(st[:, 5, :], HD), ALU.mult).then_inc(p["on"], 1)

            def heads_low(m, dst, gain=1.0, before=None):
                for i in range(NB):
                    if before:
                        before(i)
                    v.wait_ge(o_hi, NB * m + i + 1)
                    c = slice(i * P, (i + 1) * P)
                    v.scalar_tensor_tensor(out=dst[:, 1, :, c], in0=psS[:, i, :].rearrange("p (c q) -> p c q", c=4), scalar=gain,
                                           in1=dst[:, 0, :, c].bitcast(F32), op0=ALU.mult, op1=ALU.subtract).then_inc(o_lo, 1)

            v.wait_ge(bias_in, 8 * 16)
            units = list(window1_units())
            p = ph["w1"]
            for j in range(len(units) + 4):
                if j < len(units):
                    i, h, _, W, _ = units[j]
                    v.wait_ge(p["s"], j + 1)
                    if j >= 3:
                        v.wait_ge(p["pt"], j - 2)
                    biased(p, j, W3a[:, j % 3, 0:W], psS[:, 2 * (j % 2), 0:W], biasA[:, h, NEAR - W:NEAR], sinkb[:, 0, h:h + 1], j)
                    if h == NH - 1:
                        sink_sum(p, 0, i)
                    top_rounds(j)
                gate_part(1, j)
                if j >= 4 and (j - 4) % NH == NH - 1:
                    sink_normed(p, (j - 4) // NH, on)
            def take_absorbed(h):
                v.wait_ge(qabs_mm, h + 1)
                v.tensor_scalar(qabs[:, h, :], psL[:, h % 2, :], QSCALE, None, ALU.mult).then_inc(qabs_ok, 1)

            take_absorbed(0)
            heads_low(0, oA, before=lambda i: take_absorbed(i + 1))
            for h in range(NB + 1, NH):
                take_absorbed(h)
            units = list(latent_units())
            p = ph["la"]
            for j in range(len(units) + 6):
                if j < len(units):
                    i, h, K, _ = units[j]
                    v.wait_ge(p["s"], j + 1)
                    if j >= 3:
                        v.wait_ge(p["pt"], j - 2)
                    biased(p, j, as_halves(W3[:, j % 3, 0:K], K), two_banks(psS[:, 2 * (j % 2):2 * (j % 2) + 2, :], K),
                           as_halves(biasB[:, h, NKEY - K:NKEY], K), TAKEN, j)
                if j >= 5 and (j - 5) % NH == NH - 1:
                    i = (j - 5) // NH
                    v.wait_ge(p["p"], NH * (i + 1))
                    dv.link(v.reciprocal(st[:, 5, :], rsum[:, i * NH:(i + 1) * NH]))
                    v.wait_ge(p["o"], NH * (i + 1))
                    v.tensor_tensor(on[:, i, :].rearrange("p (h d) -> p h d", h=NH), o_bank(i).rearrange("p (h d) -> p h d", h=NH),
                                    spread(st[:, 5, :], HD), ALU.mult).then_inc(p["on"], 1)
                if 3 <= j < len(units) + 3:
                    u = j - 3
                    v.wait_ge(p["pv"], u + 1)
                    if u >= 2:
                        v.wait_ge(p["o"], u - 1)
                    v.tensor_copy(lat[:, u % 2, :], psL[:, 0, 0:P]).then_inc(p["lat"], 1)
            heads_low(1, oB)

            def branches(l):
                name, m0 = f"br{l}", (l - 1) * KD

                def pair(i, last):
                    low(name, i, 1)
                    done(name, i, 0)
                    v.scalar_tensor_tensor(out=mix32[:, 0, :], in0=gate[:, bass.ds(i, 1), :], scalar=1.0, in1=psL[:, 0, :],
                                           op0=ALU.add, op1=ALU.mult).then_inc(ev[0], 1)
                    low_next(name, i, last)
                    done(name, i, 1)
                    v.scalar_tensor_tensor(out=mix32[:, 1, :], in0=gate[:, bass.ds(i + KD, 1), :], scalar=1.0, in1=psL[:, 1, :],
                                           op0=ALU.add, op1=ALU.mult).then_inc(ev[1], 1)
                    for b in range(2):
                        v.wait_ge(ev[b], PAIR0[name] + i + 1)
                    v.tensor_tensor(mix32[:, 2, :], mix32[:, 0, :], mix32[:, 1, :], ALU.add).then_inc(mix_ok, 1)
                    v.wait_ge(mix_hi, m0 + i + 1)
                    v.tensor_tensor(mix[:, 1, bass.ds(i, 1), :], mix32[:, 2, :], mix[:, 0, bass.ds(i, 1), :].bitcast(F32),
                                    ALU.subtract).then_inc(mix_lo, 1)

                pairs(name, pair)

            def clear_squares():
                v.memset(sqacc[:], 0.0).then_inc(h_sq2, 1)

            def add_squares(norm, n, total, squares):
                v.wait_ge(h_sq, n + (norm * KD + 1))
                v.wait_ge(h_sq2, n + squares_cleared(norm))
                v.tensor_tensor(total, total, squares, ALU.add).then_inc(h_sq2, 1)

            def gain_low(n, count, gains, grow):
                v.wait_ge(hg_hi, count + 1)
                v.scalar_tensor_tensor(out=hn[:, 1, bass.ds(n, 1), META:], in0=hT[:, bass.ds(n, 1), :], scalar=gains[:, bass.ds(n + grow, 1)],
                                       in1=hn[:, 0, bass.ds(n, 1), META:].bitcast(F32), op0=ALU.mult, op1=ALU.subtract).then_inc(hg_lo, 1)

            def out_project(l, norm, hg0, grow):
                name = f"out{l}"

                def chunk(i, b):
                    n = 2 * i + b
                    done(name, i, b)
                    v.scalar_tensor_tensor(out=hT[:, bass.ds(n, 1), :], in0=psL[:, b, :], scalar=0.5, in1=hT[:, bass.ds(n, 1), :],
                                           op0=ALU.mult, op1=ALU.add).then_inc(ev[b], 1)
                    gain_low(n, 2 * i + (hg0 + b), gvec, grow)
                    add_squares(norm, n, sqacc[:, 0, :], sq[:])

                def pair(i, last):
                    low(name, i, 1)
                    chunk(i, 0)
                    low_next(name, i, last)
                    chunk(i, 1)

                clear_squares()
                pairs(name, pair)

            def new_rms(ssq_count):
                v.wait_ge(ssq_mm, ssq_count)
                dv.link(v.tensor_scalar(st[:, 8, 0:4], psT[:, 1, 0:4], 1.0 / D, EPS, ALU.mult, ALU.add))
                rsqrt(st[:, 8, 0:4], rs[:, 0:4], 4)

            def swiglu(name, f0, head=None):
                def pair(i, last, head=None):
                    low(name, i, 1)
                    if head:
                        new_rms(head[0])
                        diagonals(diag, rs[:, 0:4]).then_inc(diag_ok, 1)
                        low_next(name, i, last)
                        v.wait_ge(bcast, head[1])
                        v.tensor_copy(R, psT[:, 1, :]).then_inc(R_ok, 1)
                        v.wait_ge(R_ok, head[1])
                    done(name, i, 0)
                    v.tensor_tensor(ft[:, 0, :], psL[:, 0, :], R, ALU.mult).then_inc(ev[0], 1)
                    if not head:
                        low_next(name, i, last)
                    v.wait_ge(t_ok, f0 + i + 1)
                    dv.link(v.scalar_tensor_tensor(out=ft[:, 2, :], in0=ft[:, 1, :], scalar=1.0, in1=ft[:, 0, :], op0=ALU.add, op1=ALU.mult))
                    done(name, i, 1)
                    v.tensor_tensor(ft[:, 3, :], psL[:, 1, :], R, ALU.mult).then_inc(ev[1], 1)
                    v.wait_ge(ev[1], PAIR0[name] + i + 1)
                    v.scalar_tensor_tensor(out=ft[:, 4, :], in0=ft[:, 2, :], scalar=0.5, in1=ft[:, 3, :], op0=ALU.mult, op1=ALU.mult).then_inc(hid_ok, 1)
                    v.wait_ge(hid_hi, f0 + i + 1)
                    v.tensor_tensor(hid[:, 1, bass.ds(i, 1), :], ft[:, 4, :], hid[:, 0, bass.ds(i, 1), :].bitcast(F32), ALU.subtract).then_inc(hid_lo, 1)

                first = 0
                if head:
                    pair(0, False, head)
                    first = 1
                with v.Fori(first, PAIRS[name] - 1) as i:
                    dv.enter(i - first, 1)
                    pair(i, False)
                dv.leave(PAIRS[name] - 1 - first)
                pair(PAIRS[name] - 1, True)

            def add_down(name, i, b):
                done(name, i, b)
                n = bass.ds(2 * i + b, 1)
                v.tensor_tensor(hT[:, n, :], hT[:, n, :], psL[:, b, :], ALU.add).then_inc(ev[b], 1)

            def down(name):
                def pair(i, last):
                    low(name, i, 1)
                    add_down(name, i, 0)
                    low_next(name, i, last)
                    add_down(name, i, 1)

                pairs(name, pair)

            branches(1)
            out_project(1, 0, 0, ROW["ffn_norm_g"])
            swiglu("gu1a", 0, (2, 3))
            down("dn1a")
            swiglu("gu1b", NFH)

            def end_chunk(i, b):
                n = 2 * i + b
                add_down("dn1b", i, b)
                gain_low(n, 2 * i + (KD + b), g12, 0)
                add_squares(1, n, sqacc[:], tmp[:])

            def end_pair(i, last):
                low("dn1b", i, 1)
                end_chunk(i, 0)
                low_next("dn1b", i, last)
                end_chunk(i, 1)

            clear_squares()
            meta_low(2)
            pairs("dn1b", end_pair)
            low("kv2", 0, 1)
            new_rms(3)
            dv.link(v.tensor_tensor(st[:, 9, 0:4], rs[:, 0:4], rs[:, 0:4], ALU.mult))
            dv.link(v.tensor_tensor(st[:, 9, 0:4], st[:, 9, 0:4], psT[:, 1, 4:8], ALU.mult))
            dv.link(v.tensor_scalar(st[:, 9, 0:4], st[:, 9, 0:4], 1.0 / D, EPS, ALU.mult, ALU.add))
            rsqrt(st[:, 9, 0:4], rs[:, 4:8], 4)
            dv.link(v.tensor_tensor(rs[:, 8:12], rs[:, 0:4], rs[:, 4:8], ALU.mult))
            diag2 = tmp[:, 0, :].rearrange("p (n c) -> p n c", n=NB)
            diagonals(diag, rs[:, 0:4])
            diagonals(diag2, rs[:, 8:12]).then_inc(diag_ok, 1)
            low_next("kv2", 0, False)
            v.wait_ge(bcast, 4)
            v.tensor_copy(R, psT[:, 1, :])
            v.tensor_copy(tmp[:, 1, :], psT[:, 0, :]).then_inc(R_ok, 1)
            v.wait_ge(R_ok, 4)
            keys = [kaT[:, c, :] for c in range(4)] + [vaT[:, c, :] for c in range(4)] + [kbT[:], vbT[:]]
            for i in range(PAIRS["kv2"]):
                if i:
                    low("kv2", i, 1)
                take_keys("kv2", i, 0, keys[2 * i])
                if i:
                    low_next("kv2", i, i == PAIRS["kv2"] - 1)
                take_keys("kv2", i, 1, keys[2 * i + 1])
                if i < 4:
                    for n in (2 * i, 2 * i + 1):
                        g = ROW["final_norm_g"] + n
                        dv.link(v.scalar_tensor_tensor(out=hT[:, n, :], in0=hT[:, n, :], scalar=gvec[:, g:g + 1], in1=tmp[:, 1, :],
                                                       op0=ALU.mult, op1=ALU.mult))
            v.wait_ge(dist_ok, 1)
            v.scalar_tensor_tensor(out=dist[:], in0=dist[:], scalar=-1.0, in1=dist[:], op0=ALU.mult, op1=ALU.max).then_inc(dist_ok, 1)
            v.wait_ge(dist_ok, 2)
            dv.link(v.tensor_scalar(tmp[:, 0, 0:WIN2], dist[:, NEAR:NEAR + WIN2], float(P), -NEG * 100, ALU.is_gt, ALU.mult))
            v.tensor_tensor(tmp[:, 0, 0:WIN2], tmp[:, 0, 0:WIN2], dist[:, NEAR:NEAR + WIN2], ALU.add).then_inc(dist_ok, 1)
            low("qa2", 0, 1)
            v.wait_ge(nat_t, 2)
            for h in range(4):
                v.tensor_copy(van[:, 0:NB, h * P:(h + 1) * P], psS[:, h, :].rearrange("p (c f) -> p c f", c=NB))
            v.tensor_copy(van[0:META, MC, :], psT[0:META, 0, :]).then_inc(nat_taken, 1)
            take_scaled("qa2", 0, 0, qaT[:, 0, :], R, QSCALE)
            v.wait_ge(nat_t, 3)
            v.tensor_copy(vbn[:, 0:NB, :], psS[:, 0, :].rearrange("p (c f) -> p c f", c=NB))
            v.tensor_copy(vbn[0:META, MC, :], psT[0:META, 1, 0:P]).then_inc(nat_taken, 1)
            for name, dst in (("qa2", qaT), ("qb2", qbT)):
                for i in range(2):
                    if i or name == "qb2":
                        low(name, i, 1)
                    if i or name == "qb2":
                        take_scaled(name, i, 0, dst[:, 2 * i, :], R, QSCALE)
                    low_next(name, i, i == 1)
                    take_scaled(name, i, 1, dst[:, 2 * i + 1, :], R, QSCALE)
            p = ph["df"]
            for j in range(16 + 4):
                if j < 16:
                    i, h = divmod(j, 4)
                    for m in range(2):
                        u = 2 * j + m
                        v.wait_ge(p["s"], u + 1)
                        v.wait_ge(biasD_ok, 4 * i + h + 1)
                        if j >= 3 and m == 0:
                            v.wait_ge(p["pt"], j - 2)
                        biased(p, u, as_halves(W6[:, j % 3, m, :], NKEY), two_banks(psS[:, 2 * m:2 * m + 2, :], NKEY),
                               as_halves(biasD[:, h, :], NKEY), TAKEN, u)
                if 1 <= j < 17:
                    u = j - 1
                    v.wait_ge(p["p"], 2 * u + 2)
                    dv.link(v.reciprocal(st[:, 6, 0:1], rsum[:, 2 * u + 1:2 * u + 2]))
                    dv.link(v.scalar_tensor_tensor(out=st[:, 6, 1:2], in0=rsum[:, 2 * u:2 * u + 1], scalar=st[:, 6, 0:1], in1=neglam[:],
                                                   op0=ALU.mult, op1=ALU.mult))
                    v.scalar_tensor_tensor(out=W6[:, u % 3, 0, :], in0=W6[:, u % 3, 1, :], scalar=st[:, 6, 1:2], in1=W6[:, u % 3, 0, :],
                                           op0=ALU.mult, op1=ALU.add).then_inc(df_sum, 1)
                if j >= 4 and (j - 4) % 4 == 3:
                    i = (j - 4) // 4
                    dv.link(v.reciprocal(st[:, 7, 0:4], rsum[:, 8 * i:8 * i + 8:2]))
                    v.wait_ge(p["pv"], 4 * (i + 1))
                    v.tensor_tensor(yn[:, i, :].rearrange("p (h d) -> p h d", h=4), psL[:, i % 2, :].rearrange("p (h d) -> p h d", h=4),
                                    spread(st[:, 7, 0:4], P), ALU.mult).then_inc(p["on"], 1)
            v.wait_ge(biasW_ok, NH)
            units = list(window2_units())
            p = ph["w2"]
            for j in range(len(units) + 5):
                if j < len(units):
                    i, h, _, n, _, _, b, _ = units[j]
                    W = n + META
                    v.wait_ge(p["s"], j + 1)
                    if j >= 3:
                        v.wait_ge(p["pt"], j - 2)
                    biased(p, j, W3b[:, j % 3, 0:W], psS[:, 2 * (j % 2), 0:W], biasW[:, h, b:b + W], sinkb[:, 1, h:h + 1], j)
                    if h == NH - 1:
                        sink_sum(p, 1, i)
                gate_part(2, j)
                if j - 1 in Y_NORM:
                    i = Y_NORM.index(j - 1)
                    v.wait_ge(y_sq, 2 * i + 1)
                    v.tensor_reduce(st[:, 8 + i // 2, 4 * (i % 2):4 * (i % 2) + 4], sq[:].rearrange("p (h d) -> p h d", h=4), AX_X, ALU.add).then_inc(y_sq, 1)
                if j == Y_NORM[-1] + 2:
                    v.wait_ge(y_sq, 2 * NB)
                    s16 = st[:, 8:10, :].rearrange("p a b -> p (a b)")
                    dv.link(v.tensor_scalar(s16, s16, 1.0 / P, EPS, ALU.mult, ALU.add))
                    rsqrt(s16, rs[:], 16)
                    y16 = yn[:].rearrange("p i (h d) -> p (i h) d", h=4)
                    v.tensor_tensor(y16, y16, spread(rs[:], P), ALU.mult).then_inc(ph["df"]["es"], 1)
                if j >= 5 and (j - 5) % NH == NH - 1:
                    sink_normed(p, (j - 5) // NH, yw)
            heads_low(2, oA, subg[:])
            heads_low(3, oB)
            branches(2)
            out_project(2, 2, 2 * KD, ROW["norm_ffn_2"])
            swiglu("gu2a", 2 * NFH, (4, 5))
            down("dn2a")
            swiglu("gu2b", 3 * NFH)

            def last_pair(i, last):
                low("dn2b", i, 1)
                add_down("dn2b", i, 0)
                add_squares(3, 2 * i, sqacc[:, 0, :], sq[:])
                low_next("dn2b", i, last)
                add_down("dn2b", i, 1)
                add_squares(3, 2 * i + 1, sqacc[:, 0, :], sq[:])

            clear_squares()
            pairs("dn2b", last_pair)
            new_rms(5)
            v.tensor_copy(st[:, 9, 0:4], rs[:, 0:4]).then_inc(fin_rms, 1)
            for n in range(NB):
                v.wait_ge(fin_t[0], n + 1)
                v.tensor_scalar(yout[:, n, 0:SEQ], fin_bank(n, 0), rs[:, n:n + 1], None, ALU.mult).then_inc(fin_ok[0], 1)

        @block.tensor
        def _(pe):
            def product(name, i, b, x, meta=0, made=None, between={}):
                pe.wait_ge(lo[b], PAIR0[name] + i + 1)
                if not (name == "kv1" and isinstance(i, int) and i == 0):
                    pe.wait_ge(ev[b], PAIR0[name] + i)
                kc = KC[name]
                parts = [(psL[:, b, :], META, NKEY)] if x is hn else [(psL[:, b, :], 0, SEQ)]
                if meta:
                    half = NKEY // 2
                    parts = [(psS[:, 2 * b + 1, 0:half], half, NKEY), (psS[:, 2 * b, 0:half], 0, half)]
                for m, (dst, c0, c1) in enumerate(parts):
                    if m and meta > 1:
                        pe.wait_ge(mlo, meta - 1)
                    for k in range(kc):
                        if (m, k) in between:
                            between[m, k]()
                        if made and m == 0:
                            pe.wait_ge(made[0], made[1] + k + 1)
                        for n, (w, part) in enumerate(((wh, 0), (wh, 1), (wl, 0))):
                            ins = pe.matmul(dst, w[:, b, k * P:(k + 1) * P], x[:, part, k, c0:c1], start=k + n == 0, stop=k == kc - 1 and n == 2)
                ins.then_inc(mm[b], 1)

            def products(name, x, first=0, meta=0, made=None):
                if made:
                    product(name, first, 0, x, made=made)
                    product(name, first, 1, x)
                    first += 1
                if PAIRS[name] - first > 2:
                    with pe.Fori(first, PAIRS[name]) as i:
                        for b in range(2):
                            product(name, i, b, x, meta=meta)
                else:
                    for i in range(first, PAIRS[name]):
                        for b in range(2):
                            product(name, i, b, x, meta=meta)

            def sums(which, col):
                for n in range(NB):
                    ins = pe.matmul(psT[:, 1, col + n:col + n + 1], which[:, n * P:(n + 1) * P], ones[:, 0:1], start=True, stop=True)
                return ins

            def spread_rms(bank, d):
                return pe.matmul(psT[:, bank, :], ones[:], d.rearrange("p n c -> p (n c)"), start=True, stop=True)

            pe.wait_ge(consts, 1)
            pe.wait_ge(g1_in, 16)
            pe.transpose(psT[:, 1, 0:KD], rows[0:KD, :], ident[0:KD, 0:KD]).then_inc(gvec_t, 1)
            def meta_columns():
                pe.wait_ge(meta_ok, 2)
                for l in range(2):
                    for k in range(KD):
                        c = l * P + k * META
                        ins = pe.transpose(psT[:, 0, c:c + META], metain[:, l, k * P:(k + 1) * P], ident[0:META, 0:META])
                ins.then_inc(meta_t, 1)
                pe.wait_ge(rows_in, 16 * (len(ROWS) - 1))
                pe.wait_ge(gvec_ok, 1)
                pe.transpose(psT[:, 1, 0:NROWS], rows[:], ident[0:NROWS, 0:NROWS]).then_inc(gvec_t, 1)

            for k in range(KD):
                if k % 2 == 0:
                    pe.wait_ge(x_in[k // 2], 16)
                if k >= 4:
                    pe.wait_ge(x_taken, k - 3)
                for n in range(NB):
                    ins = pe.transpose(x_bank(k)[:, n * P:(n + 1) * P], xin[:, n, k * P:(k + 1) * P], ident[:])
                ins.then_inc(x_t, 1)

            product("kv1", 0, 0, hn, meta=2, made=(xlo, 0), between={(0, 4): meta_columns})
            def spread_first():
                pe.wait_ge(diag_ok, 1)
                spread_rms(1, diag).then_inc(bcast, 1)

            product("kv1", 0, 1, hn, meta=1, between={(1, 2): spread_first})
            pe.wait_ge(tab_in, 48)
            pe.matmul(psL[0:NH, 0, 0:LEN_A], tab[:, 0:NH], hotA[:], start=True, stop=True).then_inc(f_mm, 1)
            pe.matmul(psL[0:NH, 1, :], tab[:, NH:2 * NH], hotB[:, 0:512], start=True, stop=True)
            pe.matmul(psT[0:NH, 0, 0:LEN_B - 512], tab[:, NH:2 * NH], hotB[:, 512:LEN_B], start=True, stop=True).then_inc(f_mm, 1)
            products("kv1", hn, first=1, meta=1)
            pe.wait_ge(fA_ok, 2)
            products("bq1", hn)
            pe.wait_ge(ev[1], PAIR0["kv1"] + 2)
            pe.wait_ge(ev[0], PAIR0["kv1"] + 2)
            for n, src in enumerate((bkvT, ikwT, avT)):
                for c in range(NB):
                    pe.transpose(psS[:, n, c * P:(c + 1) * P], src[:, META + c * P:META + (c + 1) * P], ident[:])
                ins = pe.transpose(psT[0:META, 0, n * P:(n + 1) * P], src[:, 0:META], ident[:])
            ins.then_inc(nat_t, 1)
            products("iq1", hn)
            pe.wait_ge(ssq_in, 1)
            pe.wait_ge(R_ok, 1)
            sums(sq, 0).then_inc(ssq_mm, 1)
            products("aq1", hn)
            pe.wait_ge(nat_ok, 2)
            pe.wait_ge(nat_taken, 1)
            for n, src in enumerate((cn, ikn)):
                for c in range(NB):
                    pe.transpose(psS[:, n, c * P:(c + 1) * P], src[:, c, :], ident[:])
                pe.transpose(psT[:, 0, n * META:(n + 1) * META], src[0:META, MC, :], ident[0:META, 0:META])
            pe.wait_ge(wuk_in, 32)
            for c in range(4):
                ins = pe.transpose(psS[:, 2, c * P:(c + 1) * P], wuk[:, c * P:(c + 1) * P], ident[:])
            ins.then_inc(key_t, 1)
            pe.wait_ge(diag_ok, 2)
            spread_rms(1, diag).then_inc(bcast, 1)
            pe.wait_ge(bqlo, 2)
            product("uq1", 0, 0, bqg)
            pe.wait_ge(key_taken, 1)
            for u in range(4 * NB):
                i, h = divmod(u, 4)
                K = META + P * (i + 1)
                r = slice(h % 2 * HD, h % 2 * HD + HD)
                if u >= 2:
                    pe.wait_ge(lg_taken, u - 1)
                q = iqT[r, h // 2, i * P:(i + 1) * P]
                if K > 512:
                    pe.matmul(psS[:, 2 * (u % 2), 0:K // 2], q, ikT[r, 0:K // 2], start=True, stop=True)
                    ins = pe.matmul(psS[:, 2 * (u % 2) + 1, 0:K // 2], q, ikT[r, K // 2:K], start=True, stop=True)
                else:
                    ins = pe.matmul(psS[:, 2 * (u % 2), 0:K], q, ikT[r, 0:K], start=True, stop=True)
                ins.then_inc(lg_mm, 1)
                if u in UQ_AFTER:
                    product("uq1", *UQ_AFTER[u], bqg)

            def gate_quarters(l, j, part):
                name, before, count = f"gates{l}", sum(GATE_QUARTERS[l][:j]), (GATE_QUARTERS[l] + [0, 0])[j]
                mine = range(before, before + count - count // 2) if part == 0 else range(before + count - count // 2, before + count)
                for quarter in mine:
                    i, b = divmod(quarter // 4, 2)
                    k0 = quarter % 4 * (KD // 4)
                    if k0 == 0:
                        pe.wait_ge(lo[b], PAIR0[name] + i + 1)
                        pe.wait_ge(ev[b], PAIR0[name] + i)
                    for k in range(k0, k0 + KD // 4):
                        for n, (w, part_) in enumerate(((wh, 0), (wh, 1), (wl, 0))):
                            ins = pe.matmul(psL[:, b, :], w[:, b, k * P:(k + 1) * P], hn[:, part_, k, META:], start=k + n == 0, stop=k == KD - 1 and n == 2)
                    if k0 + KD // 4 == KD:
                        ins.then_inc(mm[b], 1)

            def transposed(p, u, chunks, tile):
                if u:
                    pe.wait_ge(p["ptx"], u)
                n = 0
                for c, col, width in chunks:
                    if width == P:
                        ins = pe.transpose(psT[:, 0, n * P:(n + 1) * P], tile[:, col:col + P], ident[:])
                        n += 1
                    else:
                        pe.transpose(psT[0:META, 1, 0:P], tile[:, col:col + META], ident[:])
                ins.then_inc(p["pt"], 1)

            def pieces(chunks, pt):
                n, found = 0, []
                for c, _, width in chunks:
                    if width == P:
                        found.append((pt[:, n * P:(n + 1) * P], c, P))
                        n += 1
                    else:
                        found.append((pt[0:META, pt.shape[-1] - P:], c, META))
                return found

            def heads_out(m, src, normed=None, counts=(), before=None):
                for i in range(NB):
                    if before:
                        before(i)
                    if normed and counts[i]:
                        pe.wait_ge(normed, counts[i])
                    if m == 3:
                        pe.wait_ge(o_lo, 2 * NB + i + 1)
                    for c in range(4):
                        ins = pe.transpose(psS[:, i, c * P:(c + 1) * P], src[:, i, c * P:(c + 1) * P], ident[:])
                    ins.then_inc(oT_mm, 1)

            pe.wait_ge(lg_taken, 4 * NB)
            units = list(window1_units())
            p = ph["w1"]
            for j in range(len(units) + 3):
                if j < len(units):
                    i, h, k0, W, _ = units[j]
                    r = slice(h // 4 * HD, h // 4 * HD + HD)
                    if j >= 2:
                        pe.wait_ge(p["neg"], j - 1)
                    pe.matmul(psS[:, 2 * (j % 2), 0:W], aqT[r, h % 4, i * P:(i + 1) * P], akT[r, k0:k0 + W], start=True, stop=True).then_inc(p["s"], 1)
                gate_quarters(1, j, 0)
                if 2 <= j < len(units) + 2:
                    pe.wait_ge(p["p"], j - 1)
                    transposed(p, j - 2, units[j - 2][4], W3a[:, (j - 2) % 3, :])
                gate_quarters(1, j, 1)
                if j >= 3:
                    u = j - 3
                    i, h = units[u][:2]
                    pe.wait_ge(p["ptx"], u + 1)
                    if h == 0 and i >= 2:
                        pe.wait_ge(p["on"], i - 1)
                    parts = pieces(units[u][4], PTa[:, u % 2, :])
                    for n, (pt, c, w) in enumerate(parts):
                        ins = pe.matmul(psS[:, 2 * (i % 2) + 1, h * HD:(h + 1) * HD], pt, avn[0:w, c, h // 4 * HD:h // 4 * HD + HD],
                                        start=n == 0, stop=n == len(parts) - 1)
                    ins.then_inc(p["pv"], 1)
            def absorbed(h):
                r = slice(h % 2 * HD, h % 2 * HD + HD)
                if h < 2:
                    pe.wait_ge(ev[h], PAIR0["br1"])
                else:
                    pe.wait_ge(qabs_ok, h - 1)
                pe.matmul(psL[:, h % 2, :], wukT[r, h // 2, :], qT[r, h // 2, :], start=True, stop=True).then_inc(qabs_mm, 1)

            absorbed(0)
            heads_out(0, on, p["on"], (1, 3, 3, 4), lambda i: absorbed(i + 1))
            for h in range(NB + 1, NH):
                absorbed(h)
            pe.wait_ge(sel_ok, NB)
            units = list(latent_units())
            p = ph["la"]
            for j in range(len(units) + 5):
                if j < len(units):
                    i, h, K, _ = units[j]
                    if j >= 2:
                        pe.wait_ge(p["neg"], j - 1)
                    if i == NB - 1 and h == 0:
                        pe.wait_ge(p["on"], 2)
                    if i == 0:
                        pe.wait_ge(qabs_ok, h + 1)
                        pe.wait_ge(o_lo, (1, 3, NB)[min(j, 2)])
                    q = qabs[:, h, i * P:(i + 1) * P]
                    cuts = [(0, 0, K)] if K <= 512 else [(0, 0, K // 2), (1, K // 2, K)]
                    for bank, k0, k1 in cuts:
                        dst = psS[:, 2 * (j % 2) + bank, 0:k1 - k0]
                        pe.matmul(dst, q, cT[:, k0:k1], start=True, stop=False)
                        ins = pe.matmul(dst, identb[:], selm[:, i, k0:k1], start=False, stop=True)
                    ins.then_inc(p["s"], 1)
                if 2 <= j < len(units) + 2:
                    pe.wait_ge(p["p"], j - 1)
                    transposed(p, j - 2, units[j - 2][3], W3[:, (j - 2) % 3, :])
                if j >= 4 and j - 4 < len(units):
                    u = j - 4
                    i, h = units[u][:2]
                    pe.wait_ge(p["lat"], u + 1)
                    if h == 0 and i >= 2:
                        pe.wait_ge(p["on"], i - 1 if i == 2 else i)
                    pe.matmul(o_bank(i)[:, h * HD:(h + 1) * HD], lat[:, u % 2, :], wuv[:, h * HD:(h + 1) * HD], start=True, stop=True).then_inc(p["o"], 1)
                if 3 <= j < len(units) + 3:
                    u = j - 3
                    pe.wait_ge(p["ptx"], u + 1)
                    if u:
                        pe.wait_ge(p["lat"], u)
                    else:
                        pe.wait_ge(qabs_ok, NH)
                    parts = pieces(units[u][3], PT[:, u % 2, :])
                    for n, (pt, c, w) in enumerate(parts):
                        ins = pe.matmul(psL[:, 0, 0:P], cn[0:w, c, :], pt, start=n == 0, stop=n == len(parts) - 1)
                    ins.then_inc(p["pv"], 1)
            heads_out(1, on, p["on"], (1, 2, 3, 4))
            pe.wait_ge(p["lat"], len(units))

            def layer_rest(l, ssq0, norm):
                name = f"br{l}"
                pe.wait_ge(o_lo, (2 * l - 1) * NB)
                product(name, 0, 0, oA)
                pe.wait_ge(o_lo, 2 * l * NB)
                product(name, 0, 1, oB)
                with pe.Fori(1, PAIRS[name]) as i:
                    product(name, i, 0, oA)
                    product(name, i, 1, oB)
                products(f"out{l}", mix, made=(mix_lo, KD * (l - 1)))
                name = f"gu{l}a"

                def norm_sums():
                    pe.wait_ge(h_sq2, squares_cleared(norm) + KD)
                    pe.wait_ge(R_ok, ssq0)
                    sums(sqacc[:, 0, :], 0).then_inc(ssq_mm, 1)

                def norm_spread():
                    pe.wait_ge(diag_ok, ssq0 + 1)
                    spread_rms(1, diag).then_inc(bcast, 1)

                product(name, 0, 0, hn, made=(hg_lo, KD * (2 * l - 2)))
                product(name, 0, 1, hn, between={(0, 1): norm_sums, (0, 6): norm_spread})
                products(name, hn, first=1)
                products(f"dn{l}a", hid, made=(hid_lo, NFH * (2 * l - 2)))
                products(f"gu{l}b", hn)
                products(f"dn{l}b", hid, made=(hid_lo, NFH * (2 * l - 1)))

            layer_rest(1, 2, 0)
            def sums_of_both():
                pe.wait_ge(h_sq2, squares_cleared(1) + KD)
                pe.wait_ge(R_ok, 3)
                sums(sqacc[:, 0, :], 0)
                sums(sqacc[:, 1, :], NB).then_inc(ssq_mm, 1)

            def spread_both():
                pe.wait_ge(diag_ok, 4)
                spread_rms(0, diag)
                spread_rms(1, tmp[:, 0, :].rearrange("p (n c) -> p n c", n=NB)).then_inc(bcast, 1)

            product("kv2", 0, 0, hn, meta=3, made=(hg_lo, KD), between={(1, 2): sums_of_both})
            product("kv2", 0, 1, hn, meta=1, between={(1, 1): spread_both})
            products("kv2", hn, first=1, meta=1)
            product("qa2", 0, 0, hn)
            for b in range(2):
                pe.wait_ge(ev[b], PAIR0["qa2"])
            for h in range(4):
                for c in range(NB):
                    pe.transpose(psS[:, h, c * P:(c + 1) * P], vaT[:, h, META + c * P:META + (c + 1) * P], ident[:])
                ins = pe.transpose(psT[0:META, 0, h * P:(h + 1) * P], vaT[:, h, 0:META], ident[:])
            ins.then_inc(nat_t, 1)
            product("qa2", 0, 1, hn)
            pe.wait_ge(nat_taken, 2)
            pe.wait_ge(R_ok, 4)
            for c in range(NB):
                pe.transpose(psS[:, 0, c * P:(c + 1) * P], vbT[:, META + c * P:META + (c + 1) * P], ident[:])
            pe.transpose(psT[0:META, 1, 0:P], vbT[:, 0:META], ident[:]).then_inc(nat_t, 1)
            products("qa2", hn, first=1)
            products("qb2", hn)
            for b in range(2):
                pe.wait_ge(ev[b], PAIR0["gates2"])
            pe.wait_ge(nat_taken, 3)
            p = ph["df"]
            all_keys = [(MC, 0, META)] + [(c, META + P * c, P) for c in range(NB)]
            for j in range(16 + 3):
                if j < 16:
                    i, h = divmod(j, 4)
                    for m in range(2):
                        u = 2 * j + m
                        r = slice(m * HD, (m + 1) * HD)
                        if u >= 2:
                            pe.wait_ge(p["neg"], u - 1)
                        q = qaT[r, h, i * P:(i + 1) * P]
                        pe.matmul(psS[:, 2 * m, 0:NKEY // 2], q, kaT[r, h, 0:NKEY // 2], start=True, stop=True)
                        pe.matmul(psS[:, 2 * m + 1, 0:NKEY // 2], q, kaT[r, h, NKEY // 2:NKEY], start=True, stop=True).then_inc(p["s"], 1)
                if 2 <= j < 18:
                    pe.wait_ge(df_sum, j - 1)
                    transposed(p, j - 2, all_keys, W6[:, (j - 2) % 3, 0, :])
                if j >= 3:
                    u = j - 3
                    i, h = divmod(u, 4)
                    pe.wait_ge(p["ptx"], u + 1)
                    if h == 0 and i >= 2:
                        pe.wait_ge(p["on"], i - 1)
                    parts = pieces(all_keys, PT2[:, u % 2, :])
                    for n, (pt, c, w) in enumerate(parts):
                        ins = pe.matmul(psL[:, i % 2, h * P:(h + 1) * P], pt, van[0:w, c, h * P:(h + 1) * P], start=n == 0, stop=n == len(parts) - 1)
                    ins.then_inc(p["pv"], 1)
            units = list(window2_units())
            p = ph["w2"]
            for j in range(len(units) + 4):
                if j < len(units):
                    i, h, lo_c, W, wcol, mcol, _, _ = units[j]
                    r = slice(h // 4 * HD, h // 4 * HD + HD)
                    if j >= 2:
                        pe.wait_ge(p["neg"], j - 1)
                    q = qbT[r, h % 4, i * P:(i + 1) * P]
                    k0 = META + P * lo_c
                    if lo_c == 0 and wcol == META:
                        ins = pe.matmul(psS[:, 2 * (j % 2), 0:META + W], q, kbT[r, 0:META + W], start=True, stop=True)
                    else:
                        pe.matmul(psS[:, 2 * (j % 2), mcol:mcol + META], q, kbT[r, 0:META], start=True, stop=True)
                        ins = pe.matmul(psS[:, 2 * (j % 2), wcol:wcol + W], q, kbT[r, k0:k0 + W], start=True, stop=True)
                    ins.then_inc(p["s"], 1)
                if j == 0:
                    pe.wait_ge(ph["df"]["on"], NB)
                gate_quarters(2, j, 0)
                if 2 <= j < len(units) + 2:
                    pe.wait_ge(p["p"], j - 1)
                    transposed(p, j - 2, units[j - 2][7], W3b[:, (j - 2) % 3, :])
                gate_quarters(2, j, 1)
                if 3 <= j < len(units) + 3:
                    u = j - 3
                    i, h = units[u][:2]
                    pe.wait_ge(p["ptx"], u + 1)
                    if h == 0 and i >= 2:
                        pe.wait_ge(p["on"], i - 1)
                    parts = pieces(units[u][7], PTb[:, u % 2, :])
                    for n, (pt, c, w) in enumerate(parts):
                        ins = pe.matmul(psS[:, 2 * (i % 2) + 1, h * HD:(h + 1) * HD], pt, vbn[0:w, c, h // 4 * HD:h // 4 * HD + HD],
                                        start=n == 0, stop=n == len(parts) - 1)
                    ins.then_inc(p["pv"], 1)
            pe.wait_ge(ph["df"]["es"], 1)
            heads_out(2, yn, p["on"], (0, 3, 3, 4))
            heads_out(3, yw)
            layer_rest(2, 4, 2)
            def rows_back(half):
                pe.wait_ge(fin_gain, (half + 1) * 4)
                for n in range(NB):
                    if half and n == NB - 1:
                        pe.wait_ge(fin_ok[0], 1)
                    for c in range(4):
                        ins = pe.transpose(fin_bank(n, half)[:, c * P:(c + 1) * P], hgf[:, 4 * half + c, n * P:(n + 1) * P], ident[:])
                    ins.then_inc(fin_t[half], 1)

            rows_back(0)
            pe.wait_ge(h_sq2, squares_cleared(3) + KD)
            pe.wait_ge(R_ok, 5)
            sums(sqacc[:, 0, :], 0).then_inc(ssq_mm, 1)
            rows_back(1)


_INS = ["x", "meta_tokens", "attn_norm_g", "w_in", "b_gates", "q_norm_g", "kv_norm_g", "w_uq", "w_uk", "w_uv",
        "idx_k_ln_g", "idx_k_ln_b", "sinks", "rel_bias", "w_branch_a", "w_branch_b", "w_out", "ffn_norm_g",
        "w_ffn_gate", "w_ffn_up", "w_ffn_down", "final_norm_g", "meta_tokens_2", "norm_mix_2", "w_in_2",
        "lambda_q1_2", "lambda_k1_2", "lambda_q2_2", "lambda_k2_2", "subln_gain_2", "sink_logits_2",
        "w_branch_a_2", "w_branch_b_2", "w_out_2", "norm_ffn_2", "w_ff_gate_2", "w_ff_up_2", "w_ff_down_2",
        "norm_final_2"]


def kernel(**inputs):
    import concourse.bacc as _bacc
    from concourse.bass_utils import run_bass_kernel_spmd as _run

    nc = _bacc.Bacc("TRN2", target_bir_lowering=False, num_devices=1)
    arrays, t = {}, {}
    for name in _INS:
        a = np.ascontiguousarray(inputs[name])
        arrays[f"in_{name}"] = a
        t[name] = nc.dram_tensor(f"in_{name}", a.shape, mybir.dt.from_np(a.dtype), kind="ExternalInput").ap()
    for name, a in zip(("hot_a", "hot_b"), bucket_rows()):
        arrays[f"const_{name}"] = a
        t[name] = nc.dram_tensor(f"const_{name}", a.shape, F32, kind="ExternalInput").ap()
    out = nc.dram_tensor("out_0", (1, SEQ, D), F32, kind="ExternalOutput").ap()
    build(nc, t, out)
    r = _run(nc, [arrays], core_ids=[0])
    return r.results[0]["out_0"]
```
